# Optimizing a Trainium2 kernel written in Bass

```python
import math
import jax, jax.numpy as jnp
from jax import lax
import numpy as np

D_MODEL = 1024
BATCH = 1
SEQ = 256
DEPTH = 2

N_MIXERS = 2
RET_QK_DIM = 256
RET_HEADS = D_MODEL // RET_QK_DIM
RET_V_DIM = 2 * RET_QK_DIM
RET_QK = RET_HEADS * RET_QK_DIM
RET_V = RET_HEADS * RET_V_DIM
RET_CHUNK = 128
ROPE_BASE = 10000.0
DILATED_PAIRS = ((128, 1), (512, 4), (2048, 16))
ATT_GROUPS = 3
ATT_HEAD_DIM = 64
ATT_HEADS = D_MODEL // ATT_HEAD_DIM
ATT_GROUP_W = ATT_HEADS * ATT_HEAD_DIM
BAND_BLOCK = 128
NUM_BUCKETS = 32
MAX_DISTANCE = 2048
D_FF = ((8 * D_MODEL + 3 * 256 - 1) // (3 * 256)) * 256
DEEPNORM_ALPHA = (2 * DEPTH) ** 0.25
DEEPNORM_BETA = (8 * DEPTH) ** -0.25
LN_EPS = 1e-5
GN_EPS = 1e-5


def _layer_norm(x, g, b):
    xf = x.astype(jnp.float32)
    mu = jnp.mean(xf, axis=-1, keepdims=True)
    var = jnp.mean(jnp.square(xf - mu), axis=-1, keepdims=True)
    y = (xf - mu) * lax.rsqrt(var + LN_EPS) * g.astype(jnp.float32) + b.astype(jnp.float32)
    return y.astype(x.dtype)

def _rope(x):
    B, T, H, d = x.shape
    inv = 1.0 / (ROPE_BASE ** jnp.linspace(0.0, 1.0, d // 2, dtype=jnp.float32))
    ang = jnp.arange(T, dtype=jnp.float32)[:, None] * inv[None, :]
    c = jnp.cos(ang)[None, :, None, :]
    s = jnp.sin(ang)[None, :, None, :]
    xp = x.reshape(B, T, H, d // 2, 2)
    a, b = xp[..., 0], xp[..., 1]
    return jnp.stack([a * c - b * s, a * s + b * c], axis=-1).reshape(B, T, H, d)

def retention(x, w_in, w_out):
    B, T, _ = x.shape
    H, dk, dv, C = RET_HEADS, RET_QK_DIM, RET_V_DIM, RET_CHUNK
    N = T // C
    proj = x @ w_in
    q, k, v, gate = jnp.split(proj, [RET_QK, 2 * RET_QK, 2 * RET_QK + RET_V], axis=-1)
    q = _rope(q.reshape(B, T, H, dk).astype(jnp.float32))
    k = _rope(k.reshape(B, T, H, dk).astype(jnp.float32)) * (dk ** -0.5)
    v = v.reshape(B, T, H, dv).astype(jnp.float32)

    def to_chunks(t):
        return t.reshape(B, N, C, H, t.shape[-1]).transpose(1, 0, 3, 2, 4)

    qc, kc, vc = to_chunks(q), to_chunks(k), to_chunks(v)
    log_gamma = jnp.log(1.0 - 2.0 ** (-5.0 - jnp.arange(H, dtype=jnp.float32)))
    idx = jnp.arange(C, dtype=jnp.float32)
    diff = idx[:, None] - idx[None, :]
    intra = jnp.where(diff[None] >= 0,
                      jnp.exp(jnp.maximum(diff, 0.0)[None] * log_gamma[:, None, None]), 0.0)
    xi = jnp.exp((idx[None, :] + 1.0) * log_gamma[:, None])[..., None]
    zeta = jnp.exp((C - 1.0 - idx[None, :]) * log_gamma[:, None])[..., None]
    gamma_c = jnp.exp(C * log_gamma)[:, None, None]

    def body(state, inp):
        qi, ki, vi = inp
        s = jnp.einsum('bhid,bhjd->bhij', qi, ki) * intra
        inner = jnp.einsum('bhij,bhje->bhie', s, vi)
        cross = jnp.einsum('bhid,bhde->bhie', qi * xi, state)
        state = gamma_c * state + jnp.einsum('bhjd,bhje->bhde', ki * zeta, vi)
        return state, inner + cross

    state0 = jnp.zeros((B, H, dk, dv), jnp.float32)
    _, y = lax.scan(body, state0, (qc, kc, vc))
    y = y.transpose(1, 0, 3, 2, 4).reshape(B, T, H, dv)
    mu = jnp.mean(y, axis=-1, keepdims=True)
    var = jnp.mean(jnp.square(y - mu), axis=-1, keepdims=True)
    y = ((y - mu) * lax.rsqrt(var + GN_EPS)).reshape(B, T, RET_V).astype(x.dtype)
    return (jax.nn.silu(gate) * y) @ w_out

def _t5_bucket(dist):
    max_exact = NUM_BUCKETS // 2
    d_f = jnp.maximum(dist, 1).astype(jnp.float32)
    large = max_exact + (jnp.log(d_f / max_exact) / math.log(MAX_DISTANCE / max_exact)
                         * (NUM_BUCKETS - max_exact)).astype(jnp.int32)
    large = jnp.minimum(large, NUM_BUCKETS - 1)
    return jnp.where(dist < max_exact, dist, large)

def _dilated_group(q, k, v, bias_table, window, dil):
    B, H, T, hd = q.shape
    blk = BAND_BLOCK
    steps = window // dil
    L = T // dil
    nb = -(-L // blk)
    Lp = nb * blk

    def to_blocks(t):
        t = t.reshape(B, H, L, dil, hd).transpose(0, 1, 3, 2, 4)
        t = jnp.pad(t, ((0, 0), (0, 0), (0, 0), (0, Lp - L), (0, 0)))
        return t.reshape(B, H, dil, nb, blk, hd)

    def band(t):
        prev = jnp.pad(t, ((0, 0), (0, 0), (0, 0), (1, 0), (0, 0), (0, 0)))[:, :, :, :-1]
        return jnp.concatenate([prev, t], axis=4)

    qb = to_blocks(q)
    kw = band(to_blocks(k))
    vw = band(to_blocks(v))
    qi = jnp.arange(blk)[:, None]
    kj = jnp.arange(2 * blk)[None, :]
    delta = qi + blk - kj
    band_ok = (delta >= 0) & (delta <= steps)
    key_ok = (jnp.arange(nb)[:, None, None] * blk - blk + kj[None]) >= 0
    mask = band_ok[None] & key_ok
    bucket = _t5_bucket(jnp.maximum(delta, 0) * dil)
    bias = bias_table[:, bucket].astype(jnp.float32)

    s = jnp.einsum('bhrnqd,bhrnkd->bhrnqk', qb, kw).astype(jnp.float32) * (hd ** -0.5)
    s = s + bias[None, :, None, None]
    s = jnp.where(mask[None, None, None], s, -jnp.inf)
    m = jnp.max(s, axis=-1, keepdims=True)
    e = jnp.exp(s - m)
    den = jnp.sum(e, axis=-1, keepdims=True)
    p = e / den
    lse = (m + jnp.log(den))[..., 0]
    o = jnp.einsum('bhrnqk,bhrnkd->bhrnqd', p.astype(v.dtype), vw)
    o = o.reshape(B, H, dil, Lp, hd)[:, :, :, :L].transpose(0, 1, 3, 2, 4).reshape(B, H, T, hd)
    lse = lse.reshape(B, H, dil, Lp)[..., :L].transpose(0, 1, 3, 2).reshape(B, H, T)
    return o, lse

def dilated_attention(x, w_in, w_out, rel_bias):
    B, T, _ = x.shape
    proj = (x @ w_in).reshape(B, T, 3, ATT_GROUPS, ATT_HEADS, ATT_HEAD_DIM)
    proj = proj.transpose(2, 3, 0, 4, 1, 5)
    outs, lses = [], []
    for g, (window, dil) in enumerate(DILATED_PAIRS):
        o, lse = _dilated_group(proj[0, g], proj[1, g], proj[2, g],
                                rel_bias[g * ATT_HEADS:(g + 1) * ATT_HEADS], window, dil)
        outs.append(o)
        lses.append(lse)
    w = jax.nn.softmax(jnp.stack(lses, axis=0), axis=0)
    o = jnp.sum(w[..., None] * jnp.stack(outs, axis=0).astype(jnp.float32), axis=0)
    o = o.transpose(0, 2, 1, 3).reshape(B, T, ATT_GROUP_W).astype(x.dtype)
    return o @ w_out

def swiglu_ffn(x, w_up, w_down):
    gate, up = jnp.split(x @ w_up, 2, axis=-1)
    return (jax.nn.silu(gate) * up) @ w_down

def first_inputs(seed: int = 0) -> dict:
    key = jax.random.key(seed)
    ks = jax.random.split(key, 10)
    n_ret = (DEPTH + 1) // 2
    n_att = DEPTH // 2
    f32 = jnp.float32
    x = jax.random.normal(ks[0], (BATCH, SEQ, D_MODEL), f32)
    ret_w_in = jax.random.normal(ks[1], (n_ret, D_MODEL, 2 * RET_QK + 2 * RET_V), f32) * D_MODEL ** -0.5
    ret_w_out = jax.random.normal(ks[2], (n_ret, RET_V, D_MODEL), f32) * (RET_V ** -0.5 * DEEPNORM_BETA)
    attn_w_in = jax.random.normal(ks[3], (n_att, D_MODEL, 3 * ATT_GROUPS * ATT_GROUP_W), f32) * D_MODEL ** -0.5
    attn_w_out = jax.random.normal(ks[4], (n_att, ATT_GROUP_W, D_MODEL), f32) * (ATT_GROUP_W ** -0.5 * DEEPNORM_BETA)
    rel_bias = jax.random.normal(ks[5], (ATT_GROUPS * ATT_HEADS, NUM_BUCKETS), f32) * 0.2
    ffn_w_up = jax.random.normal(ks[6], (DEPTH, D_MODEL, 2 * D_FF), f32) * D_MODEL ** -0.5
    ffn_w_down = jax.random.normal(ks[7], (DEPTH, D_FF, D_MODEL), f32) * (D_FF ** -0.5 * DEEPNORM_BETA)
    ln_gain = 1.0 + 0.02 * jax.random.normal(ks[8], (DEPTH, 2, D_MODEL), f32)
    ln_bias = 0.02 * jax.random.normal(ks[9], (DEPTH, 2, D_MODEL), f32)
    return {"x": x, "ret_w_in": ret_w_in, "ret_w_out": ret_w_out,
            "attn_w_in": attn_w_in, "attn_w_out": attn_w_out, "rel_bias": rel_bias,
            "ffn_w_up": ffn_w_up, "ffn_w_down": ffn_w_down,
            "ln_gain": ln_gain, "ln_bias": ln_bias}

def first_block(x, ret_w_in, ret_w_out, attn_w_in, attn_w_out, rel_bias,
              ffn_w_up, ffn_w_down, ln_gain, ln_bias):
    for i in range(DEPTH):
        j = i // N_MIXERS
        if i % N_MIXERS == 0:
            mix = retention(x, ret_w_in[j], ret_w_out[j])
        else:
            mix = dilated_attention(x, attn_w_in[j], attn_w_out[j], rel_bias)
        x = _layer_norm(DEEPNORM_ALPHA * x + mix, ln_gain[i, 0], ln_bias[i, 0])
        x = _layer_norm(DEEPNORM_ALPHA * x + swiglu_ffn(x, ffn_w_up[i], ffn_w_down[i]),
                        ln_gain[i, 1], ln_bias[i, 1])
    return x


D_MIX = D_MODEL
ATT_HEADS_2 = 8
ATT_HD = 64
D_ATT = ATT_HEADS_2 * ATT_HD
D_CONV = 256
CONV_GROUPS = 4
CONV_K = 31
D_RNN = 256
RNN_BLOCKS = 4
RNN_BD = D_RNN // RNN_BLOCKS
RNN_CONV_K = 4
RG_C = 8.0
Q_BLOCK = 128
EPS = 1e-6

Q0, Q1 = 0, D_ATT
K0, K1 = Q1, Q1 + D_ATT
V0, V1 = K1, K1 + D_ATT
F0, F1 = V1, V1 + ATT_HEADS_2
C0, C1 = F1, F1 + 2 * D_CONV
R0, R1 = C1, C1 + D_RNN
G0, G1 = R1, R1 + D_RNN
N_IN = G1

PEER_HEADS = 8
N_KEYS = 128
N_EXPERTS = N_KEYS * N_KEYS
D_KEY = 256
D_HALF = D_KEY // 2
TOPK = 16
TOK_CHUNK = 128


def rms_norm(x, g):
    xf = x.astype(jnp.float32)
    y = xf * lax.rsqrt(jnp.mean(xf * xf, axis=-1, keepdims=True) + EPS)
    return (y * g.astype(jnp.float32)).astype(x.dtype)

def layer_norm(x, g, b):
    xf = x.astype(jnp.float32)
    mu = jnp.mean(xf, axis=-1, keepdims=True)
    var = jnp.mean(jnp.square(xf - mu), axis=-1, keepdims=True)
    y = (xf - mu) * lax.rsqrt(var + EPS)
    return (y * g.astype(jnp.float32) + b.astype(jnp.float32)).astype(x.dtype)

def causal_dwconv(x, w, b):
    k = w.shape[0]
    y = lax.conv_general_dilated(
        x, w[:, None, :], window_strides=(1,), padding=[(k - 1, 0)],
        dimension_numbers=("NWC", "WIO", "NWC"), feature_group_count=x.shape[-1])
    return y + b

def forgetting_attention(q, k, v, log_f):
    b, s, h, hd = q.shape
    nb = s // Q_BLOCK
    scale = 1.0 / math.sqrt(hd)
    cum = jnp.cumsum(log_f.astype(jnp.float32), axis=1).transpose(0, 2, 1)
    q = q.transpose(0, 2, 1, 3)
    k = k.transpose(0, 2, 1, 3)
    v = v.transpose(0, 2, 1, 3)
    qb = q.reshape(b, h, nb, Q_BLOCK, hd).transpose(2, 0, 1, 3, 4)
    cb = cum.reshape(b, h, nb, Q_BLOCK).transpose(2, 0, 1, 3)
    kpos = jnp.arange(s)

    def one_block(args):
        qi, ci, blk = args
        qpos = blk * Q_BLOCK + jnp.arange(Q_BLOCK)
        logits = jnp.einsum("bhqd,bhkd->bhqk", qi, k).astype(jnp.float32) * scale
        logits = logits + ci[..., :, None] - cum[:, :, None, :]
        logits = jnp.where(kpos[None, :] <= qpos[:, None], logits, -jnp.inf)
        p = jax.nn.softmax(logits, axis=-1)
        return jnp.einsum("bhqk,bhkd->bhqd", p.astype(v.dtype), v)

    o = lax.map(one_block, (qb, cb, jnp.arange(nb)))
    return o.transpose(1, 0, 3, 2, 4).reshape(b, s, h * hd)

def conformer_conv(u, w_dw, b_dw, ln_g, ln_b):
    a, gate = u[..., :D_CONV], u[..., D_CONV:]
    y = a * jax.nn.sigmoid(gate)
    y = causal_dwconv(y, w_dw, b_dw)
    y = layer_norm(y, ln_g, ln_b)
    return jax.nn.silu(y)

def _lin_combine(c1, c2):
    a1, b1 = c1
    a2, b2 = c2
    return a1 * a2, a2 * b1 + b2

def rglru_block(xr, gate_in, conv_w, conv_b, w_r, b_r, w_i, b_i, lam):
    xr = causal_dwconv(xr, conv_w, conv_b)
    b, s, c = xr.shape
    xh = xr.reshape(b, s, RNN_BLOCKS, RNN_BD)
    r = jax.nn.sigmoid(jnp.einsum("bshi,hij->bshj", xh, w_r).reshape(b, s, c) + b_r)
    i = jax.nn.sigmoid(jnp.einsum("bshi,hij->bshj", xh, w_i).reshape(b, s, c) + b_i)
    log_a = -RG_C * r.astype(jnp.float32) * jax.nn.softplus(-lam.astype(jnp.float32))
    a = jnp.exp(log_a)
    mult = jnp.sqrt(-jnp.expm1(2.0 * log_a))
    bterm = mult * (i * xr).astype(jnp.float32)
    _, hs = lax.associative_scan(_lin_combine, (a, bterm), axis=1)
    return hs.astype(xr.dtype) * jax.nn.gelu(gate_in)

def peer(xn, wq, k1, k2, u_tab, v_tab):
    b, s, d = xn.shape
    t = b * s
    xt = xn.reshape(t, d)
    q = (xt @ wq).reshape(t, PEER_HEADS, D_KEY)
    q1, q2 = q[..., :D_HALF], q[..., D_HALF:]
    s1 = jnp.einsum("thd,hnd->thn", q1, k1).astype(jnp.float32)
    s2 = jnp.einsum("thd,hnd->thn", q2, k2).astype(jnp.float32)
    v1, i1 = lax.top_k(s1, TOPK)
    v2, i2 = lax.top_k(s2, TOPK)
    cand = (v1[..., :, None] + v2[..., None, :]).reshape(t, PEER_HEADS, TOPK * TOPK)
    sv, ci = lax.top_k(cand, TOPK)
    e1 = jnp.take_along_axis(i1, ci // TOPK, axis=-1)
    e2 = jnp.take_along_axis(i2, ci % TOPK, axis=-1)
    nc = t // TOK_CHUNK
    experts = (e1 * N_KEYS + e2).reshape(nc, TOK_CHUNK, PEER_HEADS * TOPK)
    gates = jax.nn.softmax(sv, axis=-1).astype(xn.dtype).reshape(nc, TOK_CHUNK, PEER_HEADS * TOPK)
    xc = xt.reshape(nc, TOK_CHUNK, d)

    def chunk(args):
        xi, ei, gi = args
        hid = jax.nn.gelu(jnp.einsum("td,tkd->tk", xi, u_tab[ei]))
        return jnp.einsum("tk,tkd->td", gi * hid, v_tab[ei])

    out = lax.map(chunk, (xc, experts, gates))
    return out.reshape(b, s, d)

def second_inputs(seed: int = 0) -> dict:
    key = jax.random.key(seed)
    ks = jax.random.split(key, 26)
    L, D = DEPTH, D_MODEL
    nrm = jax.random.normal
    u_lr = jax.random.uniform(ks[14], (L, D_RNN), minval=0.9, maxval=0.999)
    p_lr = u_lr ** (1.0 / RG_C)
    lam = jnp.log(p_lr) - jnp.log1p(-p_lr)
    return {
        "x": nrm(ks[0], (BATCH, SEQ, D), jnp.float32),
        "norm1_g": 1.0 + 0.01 * nrm(ks[1], (L, D)),
        "w_in": nrm(ks[2], (L, D, N_IN)) * D ** -0.5,
        "b_forget": jax.random.uniform(ks[3], (L, ATT_HEADS_2), minval=1.0, maxval=5.0),
        "conv_dw_w": nrm(ks[4], (L, CONV_K, D_CONV)) * CONV_K ** -0.5,
        "conv_dw_b": 0.01 * nrm(ks[5], (L, D_CONV)),
        "conv_ln_g": 1.0 + 0.01 * nrm(ks[6], (L, D_CONV)),
        "conv_ln_b": 0.01 * nrm(ks[7], (L, D_CONV)),
        "rg_conv_w": nrm(ks[8], (L, RNN_CONV_K, D_RNN)) * RNN_CONV_K ** -0.5,
        "rg_conv_b": 0.01 * nrm(ks[9], (L, D_RNN)),
        "rg_w_r": nrm(ks[10], (L, RNN_BLOCKS, RNN_BD, RNN_BD)) * RNN_BD ** -0.5,
        "rg_b_r": 0.01 * nrm(ks[11], (L, D_RNN)),
        "rg_w_i": nrm(ks[12], (L, RNN_BLOCKS, RNN_BD, RNN_BD)) * RNN_BD ** -0.5,
        "rg_b_i": 0.01 * nrm(ks[13], (L, D_RNN)),
        "rg_lambda": lam,
        "w_out": nrm(ks[15], (L, D_MIX, D)) * D_MIX ** -0.5,
        "norm2_g": 1.0 + 0.01 * nrm(ks[16], (L, D)),
        "peer_wq": nrm(ks[17], (L, D, PEER_HEADS * D_KEY)) * D ** -0.5,
        "peer_k1": nrm(ks[18], (L, PEER_HEADS, N_KEYS, D_HALF)) * D_HALF ** -0.5,
        "peer_k2": nrm(ks[19], (L, PEER_HEADS, N_KEYS, D_HALF)) * D_HALF ** -0.5,
        "peer_u": nrm(ks[20], (L, N_EXPERTS, D)) * D ** -0.5,
        "peer_v": nrm(ks[21], (L, N_EXPERTS, D)) * 0.5 * PEER_HEADS ** -0.5,
        "final_g": 1.0 + 0.01 * nrm(ks[22], (D,)),
    }

def second_block(x, norm1_g, w_in, b_forget, conv_dw_w, conv_dw_b, conv_ln_g, conv_ln_b,
              rg_conv_w, rg_conv_b, rg_w_r, rg_b_r, rg_w_i, rg_b_i, rg_lambda, w_out,
              norm2_g, peer_wq, peer_k1, peer_k2, peer_u, peer_v, final_g):
    b, s, _ = x.shape
    for l in range(DEPTH):
        h = rms_norm(x, norm1_g[l])
        proj = h @ w_in[l]
        q = proj[..., Q0:Q1].reshape(b, s, ATT_HEADS_2, ATT_HD)
        k = proj[..., K0:K1].reshape(b, s, ATT_HEADS_2, ATT_HD)
        v = proj[..., V0:V1].reshape(b, s, ATT_HEADS_2, ATT_HD)
        log_f = jax.nn.log_sigmoid((proj[..., F0:F1] + b_forget[l]).astype(jnp.float32))
        y_att = forgetting_attention(q, k, v, log_f)
        y_conv = conformer_conv(proj[..., C0:C1], conv_dw_w[l], conv_dw_b[l],
                                conv_ln_g[l], conv_ln_b[l])
        y_rnn = rglru_block(proj[..., R0:R1], proj[..., G0:G1], rg_conv_w[l], rg_conv_b[l],
                            rg_w_r[l], rg_b_r[l], rg_w_i[l], rg_b_i[l], rg_lambda[l])
        mixed = jnp.concatenate([y_att, y_conv.astype(x.dtype), y_rnn.astype(x.dtype)], axis=-1)
        x = x + mixed @ w_out[l]
        h2 = rms_norm(x, norm2_g[l])
        x = x + peer(h2, peer_wq[l], peer_k1[l], peer_k2[l], peer_u[l], peer_v[l])
    return rms_norm(x, final_g)


def setup_inputs(seed=0):
    out = dict(first_inputs(seed))
    for name, value in second_inputs(seed + 1).items():
        if name != "x":
            out[name + "_2"] = value
    return out


def reference(
    x, ret_w_in, ret_w_out, attn_w_in, attn_w_out, rel_bias, ffn_w_up, ffn_w_down, ln_gain,
    ln_bias, norm1_g_2, w_in_2, b_forget_2, conv_dw_w_2, conv_dw_b_2, conv_ln_g_2, conv_ln_b_2,
    rg_conv_w_2, rg_conv_b_2, rg_w_r_2, rg_b_r_2, rg_w_i_2, rg_b_i_2, rg_lambda_2, w_out_2,
    norm2_g_2, peer_wq_2, peer_k1_2, peer_k2_2, peer_u_2, peer_v_2, final_g_2,
):
    x = first_block(
        x, ret_w_in, ret_w_out, attn_w_in, attn_w_out, rel_bias, ffn_w_up, ffn_w_down, ln_gain,
        ln_bias,
    )
    return second_block(
        x, norm1_g_2, w_in_2, b_forget_2, conv_dw_w_2, conv_dw_b_2, conv_ln_g_2, conv_ln_b_2,
        rg_conv_w_2, rg_conv_b_2, rg_w_r_2, rg_b_r_2, rg_w_i_2, rg_b_i_2, rg_lambda_2, w_out_2,
        norm2_g_2, peer_wq_2, peer_k1_2, peer_k2_2, peer_u_2, peer_v_2, final_g_2,
    )


_drawn_inputs = setup_inputs


def setup_inputs(seed=0):
    import zlib

    import numpy as np

    out = dict(_drawn_inputs(seed))
    spreads = {}
    factors = {'rel_bias': 2.99,
     'norm1_g_2': 4.299,
     'conv_dw_b_2': 11.632,
     'conv_ln_g_2': 42.876,
     'conv_ln_b_2': 44.051,
     'rg_conv_b_2': 2.8,
     'rg_b_r_2': 24.07,
     'rg_b_i_2': 8.0,
     'norm2_g_2': 29.693,
     'final_g_2': 35.296}
    for name, (base, spread) in spreads.items():
        noise = np.random.default_rng([zlib.crc32(name.encode()), seed]).standard_normal(out[name].shape)
        drawn = base * np.exp(spread * noise) if base else spread * noise
        out[name] = __import__('jax').numpy.asarray(drawn.astype(out[name].dtype))
    for name, factor in factors.items():
        out[name] = (out[name] * factor).astype(out[name].dtype)
    return out
```

```python
from contextlib import ExitStack

import numpy as np

import concourse.bass as bass
from concourse import mybir

F32 = mybir.dt.float32
F32R = mybir.dt.float32r
U32 = mybir.dt.uint32
ACT = mybir.ActivationFunctionType
ALU = mybir.AluOpType
AX = mybir.AxisListType.X

P = 128
T = 256
D = 1024
DB = D // P
TILE = 1024
NC_T = T // P

RH, RQ, RV = 4, 256, 512
RVB = RH * RV // P
FF = 2816
FU = FF // P // 2
G3, AH, HD = 3, 16, 64
PAIRS = ((128, 1), (512, 4), (2048, 16))
BUCKETS, MAXD = 32, 2048
ALPHA = 4 ** 0.25
LN_EPS = 1e-5
H2 = 8
CK, RK = 31, 4
NK, TOPK = 128, 16
EPS2 = 1e-6
RG_C = 8.0
MASKED = -1e30
LOWEST = -3.0e38

RET0 = 0
RET_V, RET_G, RET_O = 16, 32, 48
FFN_TILES = 6 * FU
ATT_TILES = 80
B2_TILES = 21 + 8 + 16 + 128 + 128
START = {"ret": 0, "ffn0": 64, "att": 64 + FFN_TILES, "ffn1": 64 + FFN_TILES + ATT_TILES}
START["b0"] = START["ffn1"] + FFN_TILES
START["b1"] = START["b0"] + B2_TILES
TILES = START["b1"] + B2_TILES
EV = {"ret": 0, "ffn0": 48, "att": 48 + 4 * FU, "ffn1": 48 + 4 * FU + 80}
EV["b0"] = EV["ffn1"] + 4 * FU
EV["b1"] = EV["b0"] + 173
PAIR = {"ret": 0, "ffn0": 8, "ffn1": 8 + FU, "b0": 8 + 2 * FU, "b1": 8 + 2 * FU + 64}

C_ID, C_ONE, C_J, C_MASK, C_IOTA, C_I16 = 0, 128, 256, 384, 512, 640
NCONST = 656
R_ROT, R_COS, R_SIN, R_D = 0, 128, 640, 1152
NRET = 1152 + RH * 384
NATT = G3 * 384 + G3 * AH

V_LNG, V_LNB, V_N1, V_N2, V_FIN = 0, 32, 64, 80, 96
V_CW, V_CB, V_CG, V_CN, V_RW, V_RB, V_BR, V_BI, V_LAM, V_BF, V_EPS1, V_EPS2 = \
    104, 228, 232, 236, 240, 256, 260, 264, 268, 272, 274, 275
NVEC = 276


def build(nc, stream, x_in, consts, ret_c, att_c, vecs, rg_w, keys, scratch, out):
    with ExitStack() as ctx:
        def sb(name, cols, dt=F32):
            return ctx.enter_context(nc.sbuf_tensor(name, [P, *cols], dt))

        def sem(name):
            return ctx.enter_context(nc.semaphore(name))

        arena = sb("arena", [32768])
        xT = sb("xT", [DB, T])
        xh, xl = sb("xh", [DB, T], F32R), sb("xl", [DB, T], F32R)
        raw = sb("raw", [4, TILE])
        wh = [sb(f"wh{i}", [DB, P], F32R) for i in range(2)]
        wl = [sb(f"wl{i}", [DB, P], F32R) for i in range(2)]
        mh, ml = sb("mh", [4, T], F32R), sb("ml", [4, T], F32R)
        cst = sb("cst", [NCONST])
        vec = sb("vec", [NVEC])
        e1T, e2T, gT = sb("e1T", [T]), sb("e2T", [T]), sb("gT", [T])
        oh1 = [sb(f"oh1_{i}", [4, P]) for i in range(2)]
        oh2 = [sb(f"oh2_{i}", [4, P]) for i in range(2)]
        ps = ctx.enter_context(nc.psum_tensor("ps", [P, 8, 512], F32))
        ps_a, ps_t, ps_x = ps[:, 0:4, :], ps[:, 4:6, :], ps[:, 6:8, :]
        acc = ps_a.rearrange("p a (b t) -> p (a b) t", b=2)

        def ar(off, *shape):
            n = int(np.prod(shape))
            v = arena[:, off:off + n]
            if len(shape) == 2:
                v = v.rearrange("p (a b) -> p a b", a=shape[0])
            elif len(shape) == 3:
                v = v.rearrange("p (a b c) -> p a b c", a=shape[0], b=shape[1])
            elif len(shape) == 4:
                v = v.rearrange("p (a b c d) -> p a b c d", a=shape[0], b=shape[1], c=shape[2])
            return v

        ident, ones = cst[:, C_ID:C_ID + P], cst[:, C_ONE:C_ONE + P]
        flip, tri = cst[:, C_J:C_J + P], cst[:, C_MASK:C_MASK + P]
        iota, iota16 = cst[:, C_IOTA:C_IOTA + P], cst[:, C_I16:C_I16 + 16]

        mix, sq, yn = ar(0, DB, T), ar(2048, DB, T), ar(4096, DB, T)
        std, rstd = ar(6144, T), ar(6400, T)
        unused = ar(6656, 1)
        vT = ar(7168, 2, T)
        x_rows = ar(8192, NC_T, D)
        rc = ar(8192, NRET)
        qk, vt, sg = ar(12288, 16, T), ar(16384, NC_T, RH * RV), ar(20480, RVB, T)
        ry, rt = ar(24576, RVB, T), ar(28672, 2, 512)
        sd, rsq = ar(29696, 2, 384), ar(30720, 4, T)
        rstat = ar(10880, 2, 2, T)
        fg, fu, fm = ar(8192, 2, 512), ar(9216, 2, 512), ar(10240, 2, 512)
        aq, ak, av = ar(8192, 24, T), ar(14336, 24, T), ar(20480, NC_T, G3 * D)
        ac = ar(26624, NATT)
        bv = ar(27904, G3, 384)
        bs = ar(2112, 2, G3, T)
        pr = ar(29056, 2, 1152)
        pt_s = ar(31360, 1152)
        ao = ar(0, DB, T)
        ast = ar(2048, 2, 8)
        q2, k2, v2 = ar(8192, 4, T), ar(9216, 4, T), ar(10240, NC_T, 512)
        fz = ar(11264, 6, T)
        ca, cg = ar(12800, 2, T), ar(13312, 2, T)
        cpad, cy = ar(13824, 2, T + 32), ar(14400, 2, T)
        xrp, xc = ar(14912, 2, T + 4), ar(15440, 2, T)
        gg, rr, ri = ar(15952, 2, T), ar(16464, 2, T), ar(16976, 2, T)
        la, aa, th, mu, bt, hs = (ar(17488 + 512 * i, 2, T) for i in range(6))
        csq, cstd = ar(20560, 2, T), ar(21072, 2, T)
        spw = ar(21584, 8, 2)
        bd = ar(21632, 2, 2, P)
        p2, p2T, o2 = ar(22144, 2, 384), ar(22912, 384), ar(23296, DB, T)
        st2 = ar(25344, 2, 8)
        pq, pk = ar(8192, 16, T), ar(12288, 2, H2, P)
        sc = ar(14336, H2, 2, P)
        sc2 = ar(16384, H2, 2, P)
        cand, cand2 = ar(18432, H2, 16, 16), ar(20480, H2, 16, 16)
        hot = ar(22528, H2, 16, 16)
        tv, tf = ar(24576, H2, 2, 16), ar(24832, H2, 2, 16)
        ti = ar(25088, H2, 2, 16).bitcast(U32)
        sv, ge = ar(25344, H2, 16), ar(25472, H2, 16)
        ci, cr = ar(25600, H2, 16).bitcast(U32), ar(25728, 2, H2, 16).bitcast(U32)
        crf, ee = ar(25984, 2, H2, 16), ar(26240, 2, H2, 16)
        gd = ar(26496, 3, H2)
        hid = ar(0, NK, T)
        o_rows = ar(8192, NC_T, D)

        raw_ready = [sem(f"raw_ready{i}") for i in range(4)]
        w_hi, w_lo, mm_done, evac = sem("w_hi"), sem("w_lo"), sem("mm_done"), sem("evac")
        m_hi, m_lo = sem("m_hi"), sem("m_lo")
        const_in, x_in_s, retc_in, attc_in = sem("const_in"), sem("x_in"), sem("retc_in"), sem("attc_in")
        x_turned, x_copied, x_hi, x_lo = sem("x_turned"), sem("x_copied"), sem("x_hi"), sem("x_lo")
        v_turned, v_copied = sem("values_turned"), sem("values_copied")
        dve_step, act_step = sem("dve_step"), sem("act_step")
        n_res, n_mean, n_cen, n_sq, n_var, n_std, n_y, n_hi, n_lo = (
            sem(f"norm_{s}") for s in "residual mean centred squares variance std scaled hi lo".split())
        rope_mm, rope_done = sem("rope_mm"), sem("rope_done")
        r_s, r_sd, r_y, r_yc, r_mean, r_cen, r_sq, r_var, r_std, r_out = (
            sem(f"ret_{s}") for s in "scores decayed y y_copied mean centred squares var std out".split())
        f_mid = sem("ffn_mid")
        b_vec, b_vecc, b_store = sem("bias_vec"), sem("bias_vec_copied"), sem("bias_stored")
        b_in = [sem("bias_in0"), sem("bias_in1")]
        a_s, a_m, a_e, a_p, a_t, a_tc, a_o, a_oc, a_hi, a_lo = (
            sem(f"att_{s}") for s in "scores max exp probs turned turned_copied out out_copied hi lo".split())
        z_done, cum_done = sem("forget_z"), sem("forget_cum")
        z_abs, z_ln = sem("forget_abs"), sem("forget_ln")
        cv_y, cv_mean, cv_cen, cv_sq, cv_var, cv_std, cv_n, cv_o = (
            sem(f"conv_{s}") for s in "y mean centred squares var std normed out".split())
        bd_in, xc_done, rg_mm, rg_sig, rg_la, rg_exp, rg_m2, rg_mult, rg_o = (
            sem(s) for s in "bd_in rnn_x rnn_mm rnn_sigmoid rnn_log_a rnn_exp rnn_m2 rnn_mult rnn_out".split())
        sp_abs, sp_exp, sp_done = sem("rate_abs"), sem("rate_exp"), sem("rate_done")
        k_in, p_s, p_sc, p_used, p_sub, p_exp, p_e, p_t, p_tc = (
            sem(s) for s in "keys_in peer_scores peer_scores_copied peer_scores_used peer_sub peer_exp "
            "peer_picked peer_turned peer_turned_copied".split())
        g_hot, g_mm, g_mul = sem("peer_onehots"), sem("peer_gates"), sem("peer_weighted")
        o_turned, o_copied, o_stored = sem("out_turned"), sem("out_copied"), sem("out_stored")

        block = ctx.enter_context(nc.Block())

        NORMS = [("ln", "acc", V_LNG, V_LNB), ("ln", "acc", V_LNG + 8, V_LNB + 8),
                 ("ln", "mix", V_LNG + 16, V_LNB + 16), ("ln", "acc", V_LNG + 24, V_LNB + 24),
                 ("rms", None, V_N1, None), ("rms", "mix", V_N2, None),
                 ("rms", "acc", V_N1 + 8, None), ("rms", "mix", V_N2 + 8, None),
                 ("rms", "acc", V_FIN, None)]
        res_before = [4 * sum(s is not None for _, s, _, _ in NORMS[:k]) for k in range(10)]
        ln_before = [sum(m == "ln" for m, *_ in NORMS[:k]) for k in range(10)]

        def acc_tiles(k):
            return [START["ffn0"], START["att"], START["ffn1"], START["b0"], 0,
                    START["b0"] + 29, START["b1"], START["b1"] + 29, TILES][k]

        @block.sync
        def _(sp):
            def load(slot, g):
                sp.dma_start(raw[:, slot, :], stream[bass.ds(g, 1), :, :].rearrange("a p n -> p (a n)")) \
                    .then_inc(raw_ready[slot], 16)

            for g in range(4):
                load(g, g)
            with sp.Fori(1, TILES // 4) as i:
                for s in range(4):
                    sp.wait_ge(w_lo, i * 4 + (s - 3))
                    load(s, i * 4 + s)
            for g in range(TILES // 4 * 4, TILES):
                sp.wait_ge(w_lo, g - 3)
                load(g % 4, g)

        @block.gpsimd
        def _(pool):
            pool.dma_start(cst[:, :], consts).then_inc(const_in, 16)
            pool.dma_start(vec[:, :], vecs).then_inc(const_in, 16)
            pool.dma_start(x_rows, x_in.rearrange("(c p) d -> p c d", p=P)).then_inc(x_in_s, 16)
            pool.wait_ge(x_turned, 1)
            pool.dma_start(rc, ret_c).then_inc(retc_in, 16)
            pool.wait_ge(n_lo, 8)
            pool.dma_start(ac[0:33, :], att_c).then_inc(attc_in, 16)
            pool.wait_ge(b_vecc, G3)
            pool.dma_start(scratch.rearrange("g h x -> h g x"), bv[0:AH, :, :]).then_inc(b_store, 16)
            pool.wait_ge(b_store, 16)
            for h in range(AH):
                if h >= 2:
                    pool.wait_ge(a_s, h - 1)
                pool.dma_start(bs[:, h % 2, :, :], bass.AP(
                    scratch.tensor, h * 384, [[1, P], [AH * 384, G3], [1, T]])).then_inc(b_in[h % 2], 16)
            for k in range(2):
                pool.wait_ge(n_lo, 4 * (5 + 2 * k))
                pool.dma_start(bd, rg_w[k]).then_inc(bd_in, 16)
                pool.wait_ge(n_lo, 4 * (6 + 2 * k))
                pool.dma_start(pk, keys[k]).then_inc(k_in, 16)
            pool.wait_ge(o_copied, 4)
            pool.dma_start(out.rearrange("(c p) d -> p c d", p=P), o_rows).then_inc(o_stored, 16)
            pool.wait_ge(o_stored, 16)

        @block.scalar
        def _(act):
            A = nc.scalar.activation
            steps = [0]

            def link(ins):
                steps[0] = steps[0] + 1
                ins.then_inc(act_step, 1)
                act.wait_ge(act_step, steps[0])

            def hi(b, i=None, body=0):
                if i is None and b >= TILES:
                    return
                n = 0 if i is None else i
                act.wait_ge(raw_ready[b % 4], 16 * (b // 4 + 1) + n * (4 * body))
                if b >= 2:
                    act.wait_ge(mm_done, (b - 1) + n * body)
                A(wh[b % 2][:, :, :], raw[:, b % 4, :].rearrange("p (a b) -> p a b", a=DB), ACT.Copy) \
                    .then_inc(w_hi, 1)

            def evacuate(g, e, dst, func=ACT.Copy, i=None, body=0, ebody=0, scale=1.0, bias=None,
                         src=None, rows=P):
                n = 0 if i is None else i
                act.wait_ge(mm_done, g + 1 + n * body)
                src = ps_t[0:rows, e % 2, 0:T] if src is None else src
                kw = {} if bias is None else {"bias": bias}
                A(dst, src, func, scale=scale, **kw).then_inc(evac, 1)

            def run(g0, e0, count, dst, **kw):
                with act.Fori(0, count // 4) as i:
                    for j in range(4):
                        hi(g0 + j + 2, i, 4)
                        evacuate(g0 + j, e0 + j, dst(i * 4 + j), i=i, body=4, **kw)

            def values(g0, e0, count):
                with act.Fori(0, count // 4) as i:
                    for j in range(4):
                        hi(g0 + j + 2, i, 4)
                        evacuate(g0 + j, e0 + j, vT[:, j % 2, :], i=i, body=4)

            def one(ap, n):
                return ap[:, bass.ds(n, 1), :].rearrange("p a b -> p (a b)")

            def pair_hi(src, u, i=None, step=0, tile=0, body=0):
                n = 0 if i is None else i
                if tile:
                    act.wait_ge(mm_done, tile + n * body)
                s = 2 * (u % 2)
                A(mh[:, s:s + 2, :], src, ACT.Copy).then_inc(m_hi, 1)

            def norm(k):
                kind, _, gain, bias = NORMS[k]
                N = D
                for g in range(4):
                    if kind == "ln":
                        act.wait_ge(n_cen, 4 * ln_before[k] + g + 1)
                    elif NORMS[k][1] is not None:
                        act.wait_ge(n_res, res_before[k] + g + 1)
                    else:
                        act.wait_ge(n_lo, 4 * (k - 1) + g + 1)
                    A(sq[:, 2 * g:2 * g + 2, :], xT[:, 2 * g:2 * g + 2, :], ACT.Square).then_inc(n_sq, 1)
                A(unused, ones[:, 0:1], ACT.Sqrt)
                act.wait_ge(n_var, k + 1)
                eps = V_EPS1 if kind == "ln" else V_EPS2
                A(std, ps_x[:, 1, 0:T], ACT.Sqrt, bias=vec[:, eps:eps + 1], scale=1.0 / N).then_inc(n_std, 1)
                for g in range(4 if k < 8 else 0):
                    act.wait_ge(n_y, 4 * k + g + 1)
                    if kind == "ln":
                        for b in (2 * g, 2 * g + 1):
                            ins = A(xh[:, b, :], yn[:, b, :], ACT.Identity, bias=vec[:, bias + b:bias + b + 1])
                    else:
                        ins = A(xh[:, 2 * g:2 * g + 2, :], yn[:, 2 * g:2 * g + 2, :], ACT.Copy)
                    ins.then_inc(n_hi, 1)

            act.wait_ge(const_in, 32)
            hi(0)
            hi(1)
            act.wait_ge(x_turned, 1)
            for g in range(4):
                A(xT[:, 2 * g:2 * g + 2, :], acc[:, 2 * g:2 * g + 2, :], ACT.Copy).then_inc(x_copied, 1)
            act.wait_ge(x_copied, 4)
            A(xh[:, :, :], xT[:, :, :], ACT.Copy).then_inc(x_hi, 1)

            run(0, 0, 16, lambda n: one(qk, n))
            values(RET_V, RET_V, 16)
            run(RET_G, RET_G, 16, lambda n: one(sg, n), func=ACT.Silu)
            for h in range(RH):
                act.wait_ge(r_y, h + 1)
                yh = ry[:, 4 * h:4 * h + 4, :]
                b0 = 4 * (h % 2)
                A(yh, acc[:, b0:b0 + 4, :], ACT.Copy).then_inc(r_yc, 1)
                act.wait_ge(r_cen, h + 1)
                A(rsq, yh, ACT.Square).then_inc(r_sq, 1)
                act.wait_ge(r_var, h + 1)
                A(rstat[:, h % 2, 0, :], ps_t[:, 1, 0:T], ACT.Sqrt, bias=vec[:, V_EPS1:V_EPS1 + 1],
                  scale=1.0 / RV).then_inc(r_std, 1)
            act.wait_ge(r_out, RH)
            pair_hi(ry[:, 0:2, :], 0)
            pair_hi(ry[:, 2:4, :], 1)
            with act.Fori(0, 3) as i:
                for j in range(4):
                    hi(RET_O + j + 2, i, 4)
                    if j % 2:
                        u = j // 2 + 2
                        pair_hi(ry[:, bass.ds(i * 4 + 2 * u, 2), :], u, i, 2, RET_O + j + 1, 4)
            for j in range(12, 16):
                hi(RET_O + j + 2)
            norm(0)

            def ffn(k):
                name = f"ffn{k}"
                g0, e0, u0 = START[name], EV[name], PAIR[name]

                def a_tiles(g, e, u, i=None):
                    for j in range(4):
                        hi(g + j + 2, i, 12)
                        dst = (fg if j < 2 else fu)[:, u % 2, (j % 2) * T:(j % 2 + 1) * T]
                        evacuate(g + j, e + j, dst, ACT.Silu if j < 2 else ACT.Copy, i=i, body=12)

                def pair(u, tile, i=None):
                    n = 0 if i is None else i
                    act.wait_ge(f_mid, FU * k + u + 1 + n * 2)
                    pair_hi(fm[:, u % 2, :].rearrange("p (a t) -> p a t", a=2), u0 + u, i, 2, tile, 12)

                a_tiles(g0, e0, 0)
                pair(0, g0)
                with act.Fori(0, (FU - 1) // 2) as i:
                    for v in range(2):
                        b = g0 + 4 + 6 * v
                        a_tiles(b, e0 + 4 + 4 * v, v + 1, i)
                        hi(b + 4 + 2, i, 12)
                        pair(v + 1, b, i)
                        hi(b + 5 + 2, i, 12)
                b = g0 + FFN_TILES - 2
                hi(b + 2)
                hi(b + 3)

            ffn(0)
            norm(1)

            g0, e0 = START["att"], EV["att"]
            act.wait_ge(b_vec, 1)
            for g in range(G3):
                A(bv[0:AH, g, :], ps_a[0:AH, g, 0:384], ACT.Copy).then_inc(b_vecc, 1)
            run(g0, e0, 24, lambda n: one(aq, n), scale=HD ** -0.5)
            run(g0 + 24, e0 + 24, 24, lambda n: one(ak, n))
            values(g0 + 48, e0 + 48, 24)

            def exps(h):
                act.wait_ge(a_m, h + 1)
                s = h % 2
                if h >= 2:
                    act.wait_ge(a_t, h - 1)
                flat = ps[:, 3 * s:3 * s + 3, :].rearrange("p a b -> p (a b)")
                A(pr[:, s, 0:768], flat[:, 0:768], ACT.Exp, bias=ast[:, s, 2:3],
                  accum_out=ast[:, s, 4:5]).then_inc(act_step, 1)
                A(pr[:, s, 768:1152], flat[:, 1024:1408], ACT.Exp, bias=ast[:, s, 3:4],
                  accum_out=ast[:, s, 5:6]).then_inc(a_e, 1)
                steps[0] += 1

            def turned(h):
                s = h % 2
                act.wait_ge(a_t, h + 1)
                A(pt_s[:, 0:512], ps[:, 6, :], ACT.Copy).then_inc(a_tc, 1)
                A(pt_s[:, 512:1024], ps[:, 7, :], ACT.Copy).then_inc(a_tc, 1)
                A(pt_s[:, 1024:1152], ps[:, 3 * s, 0:P], ACT.Copy).then_inc(a_tc, 1)

            def outs(h):
                s, r = h % 2, 64 * (h % 2)
                act.wait_ge(a_o, h + 1)
                A(ao[r:r + HD, h // 2, :], ps[r:r + HD, 3 * s + 1, 0:T], ACT.Copy).then_inc(a_oc, 1)

            exps(0)
            for h in range(AH):
                turned(h)
                if h + 1 < AH:
                    exps(h + 1)
                outs(h)
            act.wait_ge(a_oc, AH)
            A(xh[:, :, :], ao, ACT.Copy).then_inc(a_hi, 1)
            run(g0 + 72, e0 + 72, 8, lambda n: one(mix, n))
            norm(2)
            ffn(1)
            norm(3)

            norm(4)
            for k in range(2):
                g0, e0 = START[f"b{k}"], EV[f"b{k}"]
                dsts = [(q2[:, j, :], ACT.Copy, {"scale": HD ** -0.5}) for j in range(4)]
                dsts += [(k2[:, j, :], ACT.Copy, {}) for j in range(4)]
                dsts += [(vT[:, j % 2, :], ACT.Copy, {}) for j in range(4)]
                dsts += [(fz[0:H2, 0, :], ACT.Identity, {"bias": vec[0:H2, V_BF + k:V_BF + k + 1], "rows": H2})]
                dsts += [(ca[:, j, :], ACT.Copy, {}) for j in range(2)]
                dsts += [(cg[:, j, :], ACT.Sigmoid, {}) for j in range(2)]
                dsts += [(xrp[:, j, 4:4 + T], ACT.Copy, {}) for j in range(2)]
                dsts += [(gg[:, j, :], ACT.Gelu_apprx_tanh, {}) for j in range(2)]
                for j, (dst, func, kw) in enumerate(dsts):
                    hi(g0 + j + 2)
                    evacuate(g0 + j, e0 + j, dst, func, **kw)
                act.wait_ge(z_abs, k + 1)
                link(A(fz[0:H2, 2, :], fz[0:H2, 1, :], ACT.Exp, scale=-1.0))
                A(fz[0:H2, 3, :], fz[0:H2, 2, :], ACT.Ln, bias=ones[0:H2, 0:1]).then_inc(z_ln, 1)
                act.wait_ge(sp_abs, k + 1)
                A(spw[:, 2, :], spw[:, 1, :], ACT.Exp, scale=-1.0).then_inc(sp_exp, 1)
                def exps2(h):
                    s = h % 2
                    act.wait_ge(a_m, AH + H2 * k + h + 1)
                    if h >= 2:
                        act.wait_ge(a_t, AH + H2 * k + h - 1)
                    A(p2[:, s, 0:256], ps[:, s, 0:256], ACT.Exp, bias=st2[:, s, 2:3],
                      accum_out=st2[:, s, 4:5]).then_inc(act_step, 1)
                    A(p2[:, s, 256:384], ps[:, s, 256:384], ACT.Exp, bias=st2[:, s, 3:4],
                      accum_out=st2[:, s, 5:6]).then_inc(a_e, 1)
                    steps[0] += 1

                exps2(0)
                exps2(1)
                for h in range(H2):
                    s, r = h % 2, 64 * (h % 2)
                    act.wait_ge(a_t, AH + H2 * k + h + 1)
                    A(p2T, ps_x[:, 0, 0:384], ACT.Copy).then_inc(a_tc, 1)
                    if h + 2 < H2:
                        exps2(h + 2)
                    act.wait_ge(a_o, AH + H2 * k + h + 1)
                    A(o2[r:r + HD, h // 2, :], ps_x[r:r + HD, 1, 0:T], ACT.Copy).then_inc(a_oc, 1)
                act.wait_ge(cv_cen, k + 1)
                A(csq, cy, ACT.Square).then_inc(cv_sq, 1)
                act.wait_ge(cv_var, k + 1)
                A(cstd[:, 0, :], ps_x[:, 1, 0:T], ACT.Sqrt, bias=vec[:, V_EPS2:V_EPS2 + 1],
                  scale=1.0 / 256).then_inc(cv_std, 1)
                act.wait_ge(cv_n, k + 1)
                for b in range(2):
                    c = 2 * k + b
                    A(o2[:, 4 + b, :], cy[:, b, :], ACT.Silu, scale=vec[:, V_CG + c:V_CG + c + 1],
                      bias=vec[:, V_CN + c:V_CN + c + 1]).then_inc(cv_o, 1)
                act.wait_ge(rg_mm, k + 1)
                for b in range(2):
                    c = 2 * k + b
                    A(rr[:, b, :], ps_a[:, 2, b * T:(b + 1) * T], ACT.Sigmoid,
                      bias=vec[:, V_BR + c:V_BR + c + 1]).then_inc(rg_sig, 1)
                    A(ri[:, b, :], ps_a[:, 3, b * T:(b + 1) * T], ACT.Sigmoid,
                      bias=vec[:, V_BI + c:V_BI + c + 1]).then_inc(rg_sig, 1)
                act.wait_ge(rg_la, k + 1)
                A(aa, la, ACT.Exp).then_inc(rg_exp, 1)
                A(th, la, ACT.Tanh, scale=-1.0).then_inc(rg_exp, 1)
                act.wait_ge(rg_m2, k + 1)
                A(mu, mu, ACT.Sqrt).then_inc(rg_mult, 1)
                act.wait_ge(rg_o, k + 1)
                act.wait_ge(cv_o, 2 * k + 2)
                act.wait_ge(a_oc, AH + H2 * (k + 1))
                A(xh[:, :, :], o2, ACT.Copy).then_inc(a_hi, 1)
                run(g0 + 21, e0 + 21, 8, lambda n: one(mix, n))
                norm(5 + 2 * k)

                run(g0 + 29, e0 + 29, 16, lambda n: one(pq, n))
                for c in range(NC_T):
                    if c:
                        act.wait_ge(p_used, 2 * k + c)
                    for j in range(4):
                        act.wait_ge(p_s, 4 * (2 * k + c) + j + 1)
                        A(sc[:, 2 * j:2 * j + 2, :, :], ps_a[:, j, :].rearrange("p (a b c) -> p a b c", a=2, b=2),
                          ACT.Copy).then_inc(p_sc, 1)
                    act.wait_ge(p_sub, 2 * k + c + 1)
                    A(ge, ge, ACT.Exp).then_inc(p_exp, 1)
                    act.wait_ge(p_t, 2 * k + c + 1)
                    for m, dst in enumerate((e1T, e2T, gT)):
                        A(dst[:, c * P:(c + 1) * P], ps_x[:, 0, m * P:(m + 1) * P], ACT.Copy).then_inc(p_tc, 1)
                run(g0 + 45, e0 + 45, 128, lambda n: one(hid, n), func=ACT.Gelu_apprx_tanh)
                act.wait_ge(g_mul, 64 * (k + 1))
                gv, u0 = g0 + 173, PAIR[f"b{k}"]
                pair_hi(hid[:, 0:2, :], u0)
                pair_hi(hid[:, 2:4, :], u0 + 1)
                with act.Fori(0, 31) as i:
                    for j in range(4):
                        hi(gv + j + 2, i, 4)
                        if j % 2:
                            u = j // 2 + 2
                            pair_hi(hid[:, bass.ds(i * 4 + 2 * u, 2), :], u0 + u, i, 2, gv + j + 1, 4)
                for j in range(124, 128):
                    hi(gv + j + 2)
                norm(6 + 2 * k)
            for j in range(4):
                act.wait_ge(o_turned, j + 1)
                A(o_rows[:, j // 2, (j % 2) * 512:(j % 2 + 1) * 512], ps_a[:, j, :], ACT.Copy).then_inc(o_copied, 1)

        @block.vector
        def _(dve):
            V = nc.vector
            steps = [0]

            def link(ins, wait=True):
                steps[0] = steps[0] + 1
                ins.then_inc(dve_step, 1)
                if wait:
                    dve.wait_ge(dve_step, steps[0])

            def lo(b, i=None, body=0):
                if i is None and b >= TILES:
                    return
                n = 0 if i is None else i
                dve.wait_ge(w_hi, b + 1 + n * body)
                V.tensor_tensor(wl[b % 2][:, :, :], raw[:, b % 4, :].rearrange("p (a b) -> p a b", a=DB),
                                wh[b % 2][:, :, :].bitcast(F32), ALU.subtract).then_inc(w_lo, 1)

            def run(g0, count):
                with dve.Fori(0, count // 4) as i:
                    for j in range(4):
                        lo(g0 + j + 2, i, 4)

            def pair_lo(src, u, i=None, step=0):
                n = 0 if i is None else i
                dve.wait_ge(m_hi, u + 1 + n * step)
                s = 2 * (u % 2)
                V.tensor_tensor(ml[:, s:s + 2, :], src, mh[:, s:s + 2, :].bitcast(F32), ALU.subtract) \
                    .then_inc(m_lo, 1)

            def norm(k):
                kind, source, gain, bias = NORMS[k]
                if source == "acc":
                    dve.wait_ge(mm_done, acc_tiles(k))
                elif source == "mix":
                    dve.wait_ge(evac, {2: EV["att"] + 80, 5: EV["b0"] + 29, 7: EV["b1"] + 29}[k])
                if source is not None:
                    src = acc if source == "acc" else mix
                    for g in range(4):
                        b = slice(2 * g, 2 * g + 2)
                        V.scalar_tensor_tensor(out=xT[:, b, :], in0=xT[:, b, :],
                                               scalar=ALPHA if kind == "ln" else 1.0, in1=src[:, b, :],
                                               op0=ALU.mult, op1=ALU.add).then_inc(n_res, 1)
                if kind == "ln":
                    dve.wait_ge(n_mean, ln_before[k] + 1)
                    for g in range(4):
                        b = slice(2 * g, 2 * g + 2)
                        V.scalar_tensor_tensor(out=xT[:, b, :],
                                               in0=ps_x[:, 0, 0:T].unsqueeze(1).to_broadcast([P, 2, T]),
                                               scalar=-1.0 / D, in1=xT[:, b, :], op0=ALU.mult, op1=ALU.add) \
                            .then_inc(n_cen, 1)
                dve.wait_ge(n_std, k + 1)
                link(V.reciprocal(rstd, std))
                for g in range(4):
                    for b in (2 * g, 2 * g + 1):
                        ins = V.scalar_tensor_tensor(out=yn[:, b, :], in0=xT[:, b, :],
                                                     scalar=vec[:, gain + b:gain + b + 1], in1=rstd,
                                                     op0=ALU.mult, op1=ALU.mult)
                    ins.then_inc(n_y, 1)
                dve.wait_ge(n_y, 4 * (k + 1))
                y = xT if kind == "ln" else yn
                for g in range(4 if k < 8 else 0):
                    b = slice(2 * g, 2 * g + 2)
                    if kind == "ln":
                        for c in (2 * g, 2 * g + 1):
                            link(V.tensor_scalar(xT[:, c, :], yn[:, c, :], vec[:, bias + c:bias + c + 1], None,
                                                 ALU.add), wait=(c % 2 == 1))
                    dve.wait_ge(n_hi, 4 * k + g + 1)
                    V.tensor_tensor(xl[:, b, :], y[:, b, :], xh[:, b, :].bitcast(F32), ALU.subtract) \
                        .then_inc(n_lo, 1)

            lo(0)
            lo(1)
            dve.wait_ge(x_hi, 1)
            V.tensor_tensor(xl[:, :, :], xT[:, :, :], xh[:, :, :].bitcast(F32), ALU.subtract).then_inc(x_lo, 1)

            def values(g0, v0, count, dst):
                def copy(n, j, i=None):
                    dve.wait_ge(v_turned, n + 1 + (0 if i is None else i * 4))
                    m = j if i is None else i * 4 + j
                    V.tensor_copy(dst[:, :, bass.ds(m * P, P)],
                                  ps_x[:, n % 2, 0:T].rearrange("p (c n) -> p c n", c=2)).then_inc(v_copied, 1)

                for j in range(4):
                    lo(g0 + j + 2)
                    if j:
                        copy(v0 + j - 1, j - 1)
                if count > 4:
                    with dve.Fori(0, count // 4 - 1) as i:
                        for j in range(4):
                            lo(g0 + 4 + j + 2, i, 4)
                            copy(v0 + 3 + j, 3 + j, i)
                copy(v0 + count - 1, count - 1)

            run(0, 16)
            values(RET_V, 0, 16, vt)
            run(RET_G, 16)
            for b in range(8):
                dve.wait_ge(retc_in, 16)
                dve.wait_ge(evac, 16)
                dve.wait_ge(rope_mm, b + 1)
                pair = qk[:, 2 * b:2 * b + 2, :]
                cos, sin = (rc[:, c:c + 512].rearrange("p (a t) -> p a t", a=2) for c in (R_COS, R_SIN))
                t1 = rt[:, 0, :].rearrange("p (a t) -> p a t", a=2)
                t2 = rt[:, 1, :].rearrange("p (a t) -> p a t", a=2)
                link(V.tensor_tensor(t1, pair, cos, ALU.mult), wait=False)
                link(V.tensor_tensor(t2, ps_x[:, b % 2, :].rearrange("p (a t) -> p a t", a=2), sin, ALU.mult))
                V.tensor_tensor(pair, t1, t2, ALU.add).then_inc(rope_done, 1)
                dve.wait_ge(rope_done, b + 1)
            for h in range(RH):
                yh = ry[:, 4 * h:4 * h + 4, :]
                dve.wait_ge(r_s, h + 1)
                V.tensor_tensor(sd[:, h % 2, :], ps_x[:, h % 2, 0:384], rc[:, R_D + 384 * h:R_D + 384 * (h + 1)],
                                ALU.mult).then_inc(r_sd, 1)
                dve.wait_ge(r_mean, h + 1)
                V.scalar_tensor_tensor(out=yh, in0=ps_t[:, 0, 0:T].unsqueeze(1).to_broadcast([P, 4, T]),
                                       scalar=-1.0 / RV, in1=yh, op0=ALU.mult, op1=ALU.add).then_inc(r_cen, 1)
                dve.wait_ge(r_std, h + 1)
                link(V.reciprocal(rstat[:, h % 2, 1, :], rstat[:, h % 2, 0, :]))
                link(V.tensor_tensor(yh, yh, rstat[:, h % 2, 1, :].unsqueeze(1).to_broadcast([P, 4, T]), ALU.mult))
                V.tensor_tensor(yh, yh, sg[:, 4 * h:4 * h + 4, :], ALU.mult).then_inc(r_out, 1)
            pair_lo(ry[:, 0:2, :], 0)
            pair_lo(ry[:, 2:4, :], 1)
            with dve.Fori(0, 3) as i:
                for j in range(4):
                    lo(RET_O + j + 2, i, 4)
                    if j % 2:
                        u = j // 2 + 2
                        pair_lo(ry[:, bass.ds(i * 4 + 2 * u, 2), :], u, i, 2)
            for j in range(12, 16):
                lo(RET_O + j + 2)
            norm(0)

            def ffn(k):
                name = f"ffn{k}"
                g0, e0, u0 = START[name], EV[name], PAIR[name]

                def mid(u, e, i=None):
                    n = 0 if i is None else i
                    dve.wait_ge(evac, e + n * 8)
                    V.tensor_tensor(fm[:, u % 2, :], fg[:, u % 2, :], fu[:, u % 2, :], ALU.mult).then_inc(f_mid, 1)

                def rest(u, i=None):
                    pair_lo(fm[:, u % 2, :].rearrange("p (a t) -> p a t", a=2), u0 + u, i, 2)

                for j in range(4):
                    lo(g0 + j + 2)
                mid(0, e0 + 4)
                rest(0)
                with dve.Fori(0, (FU - 1) // 2) as i:
                    for v in range(2):
                        b = g0 + 4 + 6 * v
                        for j in range(5):
                            lo(b + j + 2, i, 12)
                        mid(v + 1, e0 + 8 + 4 * v, i)
                        rest(v + 1, i)
                        lo(b + 5 + 2, i, 12)
                lo(g0 + FFN_TILES)
                lo(g0 + FFN_TILES + 1)

            ffn(0)
            norm(1)

            g0, e0 = START["att"], EV["att"]
            run(g0, 48)
            values(g0 + 48, 16, 24, av)

            def softmax_max(n, s, st, views):
                dve.wait_ge(a_s, n + 1)
                for c, v in enumerate(views):
                    link(V.tensor_reduce(st[:, s, c:c + 1], v, AX, ALU.max), wait=(c == 1))
                V.tensor_scalar(st[:, s, 2:4], st[:, s, 0:2], -1.0, None, ALU.mult).then_inc(a_m, 1)

            def softmax_scale(n, s, st, probs):
                dve.wait_ge(a_e, n + 1)
                link(V.reciprocal(st[:, s, 6:8], st[:, s, 4:6]))
                link(V.tensor_scalar(probs[0], probs[0], st[:, s, 6:7], None, ALU.mult), wait=False)
                V.tensor_scalar(probs[1], probs[1], st[:, s, 7:8], None, ALU.mult).then_inc(a_p, 1)

            def att_max(h):
                s = h % 2
                flat = ps[:, 3 * s:3 * s + 3, :].rearrange("p a b -> p (a b)")
                softmax_max(h, s, ast, (flat[:, 0:768], flat[:, 1024:1408]))

            att_max(0)
            for h in range(AH):
                softmax_scale(h, h % 2, ast, (pr[:, h % 2, 0:768], pr[:, h % 2, 768:1152]))
                if h + 1 < AH:
                    att_max(h + 1)
            dve.wait_ge(a_hi, 1)
            V.tensor_tensor(xl[:, :, :], ao, xh[:, :, :].bitcast(F32), ALU.subtract).then_inc(a_lo, 1)
            run(g0 + 72, 8)
            norm(2)
            ffn(1)
            norm(3)

            norm(4)
            for k in range(2):
                g0, e0 = START[f"b{k}"], EV[f"b{k}"]
                link(V.memset(cpad[:, :, 0:32], 0.0), wait=False)
                link(V.memset(xrp[:, :, 0:4], 0.0), wait=False)
                for j in range(8):
                    lo(g0 + j + 2)
                values(g0 + 8, 40 + 4 * k, 4, v2)
                for j in range(12, 21):
                    lo(g0 + j + 2)
                dve.wait_ge(evac, e0 + 13)
                z = [fz[0:H2, j, :] for j in range(6)]
                link(V.tensor_scalar(z[4], z[0], -1.0, None, ALU.mult))
                V.tensor_tensor(z[1], z[0], z[4], ALU.max).then_inc(z_abs, 1)
                link(V.tensor_scalar(z[0], z[0], 0.0, None, ALU.min))
                dve.wait_ge(z_ln, k + 1)
                link(V.tensor_tensor(z[0], z[0], z[3], ALU.subtract))
                link(V.memset(z[2], 1.0))
                link(V.tensor_tensor_scan(z[4], z[2], z[0], 0.0, ALU.mult, ALU.add))
                V.tensor_scalar(z[5], z[4], -1.0, None, ALU.mult).then_inc(cum_done, 1)
                lam = vec[:, V_LAM + 2 * k:V_LAM + 2 * k + 2]
                link(V.tensor_scalar(spw[:, 0, :], lam, -1.0, None, ALU.mult))
                V.tensor_tensor(spw[:, 1, :], spw[:, 0, :], lam, ALU.max).then_inc(sp_abs, 1)
                dve.wait_ge(sp_exp, k + 1)
                link(V.tensor_scalar(spw[:, 3, :], spw[:, 2, :], 2.0, None, ALU.add))
                link(V.reciprocal(spw[:, 3, :], spw[:, 3, :]))
                link(V.tensor_tensor(spw[:, 3, :], spw[:, 3, :], spw[:, 2, :], ALU.mult))
                link(V.tensor_tensor(spw[:, 4, :], spw[:, 3, :], spw[:, 3, :], ALU.mult))
                link(V.memset(spw[:, 5, :], 1.0 / 19))
                for n in range(17, 0, -2):
                    link(V.tensor_tensor(spw[:, 5, :], spw[:, 5, :], spw[:, 4, :], ALU.mult))
                    link(V.tensor_scalar(spw[:, 5, :], spw[:, 5, :], 1.0 / n, None, ALU.add))
                link(V.tensor_tensor(spw[:, 5, :], spw[:, 5, :], spw[:, 3, :], ALU.mult))
                link(V.tensor_scalar(spw[:, 0, :], spw[:, 0, :], 0.0, -RG_C, ALU.max, ALU.mult))
                link(V.scalar_tensor_tensor(out=spw[:, 6, :], in0=spw[:, 5, :], scalar=-2.0 * RG_C,
                                            in1=spw[:, 0, :], op0=ALU.mult, op1=ALU.add))
                dve.wait_ge(evac, e0 + 21)
                for t in range(RK):
                    for b in range(2):
                        w = V_RW + (2 * k + b) * RK + t
                        src = xrp[:, b, t + 1:t + 1 + T]
                        if t == 0:
                            c = V_RB + 2 * k + b
                            ins = V.tensor_scalar(xc[:, b, :], src, vec[:, w:w + 1], vec[:, c:c + 1],
                                                  ALU.mult, ALU.add)
                        else:
                            ins = V.scalar_tensor_tensor(out=xc[:, b, :], in0=src, scalar=vec[:, w:w + 1],
                                                         in1=xc[:, b, :], op0=ALU.mult, op1=ALU.add)
                        if t == RK - 1 and b == 1:
                            ins.then_inc(xc_done, 1)
                        else:
                            link(ins, wait=(b == 1))
                def att2_max(h):
                    s = h % 2
                    softmax_max(AH + H2 * k + h, s, st2, (ps[:, s, 0:256], ps[:, s, 256:384]))

                att2_max(0)
                att2_max(1)
                for h in range(H2):
                    softmax_scale(AH + H2 * k + h, h % 2, st2, (p2[:, h % 2, 0:256], p2[:, h % 2, 256:384]))
                    if h + 2 < H2:
                        att2_max(h + 2)
                link(V.tensor_tensor(cpad[:, :, 32:32 + T], ca, cg, ALU.mult))
                for t in range(CK):
                    for b in range(2):
                        w = V_CW + (2 * k + b) * CK + t
                        src = cpad[:, b, t + 2:t + 2 + T]
                        if t == 0:
                            c = V_CB + 2 * k + b
                            ins = V.tensor_scalar(cy[:, b, :], src, vec[:, w:w + 1], vec[:, c:c + 1],
                                                  ALU.mult, ALU.add)
                        else:
                            ins = V.scalar_tensor_tensor(out=cy[:, b, :], in0=src, scalar=vec[:, w:w + 1],
                                                         in1=cy[:, b, :], op0=ALU.mult, op1=ALU.add)
                        if t == CK - 1 and b == 1:
                            ins.then_inc(cv_y, 1)
                        else:
                            link(ins, wait=(b == 1))
                dve.wait_ge(cv_mean, k + 1)
                V.scalar_tensor_tensor(out=cy, in0=ps_x[:, 0, 0:T].unsqueeze(1).to_broadcast([P, 2, T]),
                                       scalar=-1.0 / 256, in1=cy, op0=ALU.mult, op1=ALU.add).then_inc(cv_cen, 1)
                dve.wait_ge(cv_std, k + 1)
                link(V.reciprocal(cstd[:, 1, :], cstd[:, 0, :]))
                V.tensor_tensor(cy, cy, cstd[:, 1, :].unsqueeze(1).to_broadcast([P, 2, T]), ALU.mult) \
                    .then_inc(cv_n, 1)
                dve.wait_ge(rg_sig, 4 * (k + 1))
                link(V.tensor_tensor(la, rr, spw[:, 6, :].unsqueeze(2).to_broadcast([P, 2, T]), ALU.mult),
                     wait=False)
                V.tensor_tensor(bt, ri, xc, ALU.mult).then_inc(rg_la, 1)
                dve.wait_ge(rg_exp, 2 * (k + 1))
                link(V.tensor_scalar(mu, th, 1.0, None, ALU.add))
                link(V.reciprocal(mu, mu))
                V.scalar_tensor_tensor(out=mu, in0=th, scalar=2.0, in1=mu, op0=ALU.mult, op1=ALU.mult) \
                    .then_inc(rg_m2, 1)
                dve.wait_ge(rg_mult, k + 1)
                link(V.tensor_tensor(bt, bt, mu, ALU.mult))
                for b in range(2):
                    link(V.tensor_tensor_scan(hs[:, b, :], aa[:, b, :], bt[:, b, :], 0.0, ALU.mult, ALU.add),
                         wait=(b == 1))
                V.tensor_tensor(o2[:, 6:8, :], hs, gg, ALU.mult).then_inc(rg_o, 1)
                dve.wait_ge(a_hi, k + 2)
                V.tensor_tensor(xl[:, :, :], o2, xh[:, :, :].bitcast(F32), ALU.subtract).then_inc(a_lo, 1)
                run(g0 + 21, 8)
                norm(5 + 2 * k)

                run(g0 + 29, 16)
                for c in range(NC_T):
                    n = 2 * k + c
                    dve.wait_ge(p_sc, 4 * (n + 1))
                    hs_ = [(h, s) for h in range(H2) for s in range(2)]
                    for h, s in hs_:
                        link(V.max(tv[:, h, s, 0:8], sc[:, h, s, :]), wait=False)
                    dve.wait_ge(dve_step, steps[0])
                    for h, s in hs_:
                        link(V.max_index(ti[:, h, s, 0:8], tv[:, h, s, 0:8], sc[:, h, s, :]), wait=False)
                        link(V.match_replace(sc2[:, h, s, :], tv[:, h, s, 0:8], sc[:, h, s, :], LOWEST), wait=False)
                    dve.wait_ge(dve_step, steps[0])
                    for h, s in hs_:
                        link(V.max(tv[:, h, s, 8:16], sc2[:, h, s, :]), wait=False)
                    dve.wait_ge(dve_step, steps[0])
                    for h, s in hs_:
                        link(V.max_index(ti[:, h, s, 8:16], tv[:, h, s, 8:16], sc2[:, h, s, :]), wait=False)
                    link(V.tensor_tensor(cand, tv[:, :, 0, :].unsqueeze(3).to_broadcast([P, H2, 16, 16]),
                                         tv[:, :, 1, :].unsqueeze(2).to_broadcast([P, H2, 16, 16]), ALU.add))
                    V.tensor_copy(tf, ti).then_inc(p_used, 1)
                    flat = [v.rearrange("p h a b -> p h (a b)") for v in (cand, cand2)]
                    for h in range(H2):
                        link(V.max(sv[:, h, 0:8], flat[0][:, h, :]), wait=False)
                    dve.wait_ge(dve_step, steps[0])
                    for h in range(H2):
                        link(V.max_index(ci[:, h, 0:8], sv[:, h, 0:8], flat[0][:, h, :]), wait=False)
                        link(V.match_replace(flat[1][:, h, :], sv[:, h, 0:8], flat[0][:, h, :], LOWEST), wait=False)
                    dve.wait_ge(dve_step, steps[0])
                    for h in range(H2):
                        link(V.max(sv[:, h, 8:16], flat[1][:, h, :]), wait=False)
                    dve.wait_ge(dve_step, steps[0])
                    for h in range(H2):
                        link(V.max_index(ci[:, h, 8:16], sv[:, h, 8:16], flat[1][:, h, :]), wait=False)
                    V.tensor_tensor(ge, sv, sv[:, :, 0:1].to_broadcast([P, H2, 16]), ALU.subtract) \
                        .then_inc(p_sub, 1)
                    dve.wait_ge(dve_step, steps[0])
                    link(V.tensor_single_scalar(cr[:, 0, :, :], ci, 4, ALU.logical_shift_right), wait=False)
                    link(V.tensor_single_scalar(cr[:, 1, :, :], ci, 15, ALU.bitwise_and))
                    link(V.tensor_copy(crf, cr))
                    dve.wait_ge(p_used, n + 1)
                    for s in range(2):
                        link(V.tensor_tensor(hot, crf[:, s, :, :].unsqueeze(3).to_broadcast([P, H2, 16, 16]),
                                             iota16.unsqueeze(1).unsqueeze(1).to_broadcast([P, H2, 16, 16]),
                                             ALU.is_equal))
                        link(V.tensor_tensor(hot, hot, tf[:, :, s, :].unsqueeze(2).to_broadcast([P, H2, 16, 16]),
                                             ALU.mult))
                        link(V.tensor_reduce(ee[:, s, :, :], hot, AX, ALU.add))
                    dve.wait_ge(p_exp, n + 1)
                    link(V.tensor_reduce(gd[:, 0, :], ge, AX, ALU.add))
                    link(V.reciprocal(gd[:, 1, :], gd[:, 0, :]))
                    V.tensor_tensor(ge, ge, gd[:, 1, :].unsqueeze(2).to_broadcast([P, H2, 16]), ALU.mult) \
                        .then_inc(p_e, 1)
                    dve.wait_ge(p_t, n + 1)
                run(g0 + 45, 128)
                dve.wait_ge(p_tc, 6 * (k + 1))
                dve.wait_ge(evac, e0 + 173)

                def onehots(t, s):
                    for j in range(4):
                        V.tensor_scalar(oh1[s][:, j, :], iota, e1T[:, bass.ds(t + j, 1)], None, ALU.is_equal)
                        ins = V.tensor_scalar(oh2[s][:, j, :], iota, e2T[:, bass.ds(t + j, 1)],
                                              gT[:, bass.ds(t + j, 1)], ALU.is_equal, ALU.mult)
                    ins.then_inc(g_hot, 1)

                def weigh(t, s):
                    h = hid[:, :, bass.ds(t, 4)].rearrange("p m t -> p t m")
                    V.tensor_tensor(h, h, ps_x[:, s, :].rearrange("p (t m) -> p t m", t=4), ALU.mult) \
                        .then_inc(g_mul, 1)

                onehots(0, 0)
                onehots(4, 1)
                dve.wait_ge(g_mm, 64 * k + 1)
                weigh(0, 0)
                with dve.Fori(0, 31) as i:
                    onehots(i * 8 + 8, 0)
                    dve.wait_ge(g_mm, i * 2 + 64 * k + 2)
                    weigh(i * 8 + 4, 1)
                    onehots(i * 8 + 12, 1)
                    dve.wait_ge(g_mm, i * 2 + 64 * k + 3)
                    weigh(i * 8 + 8, 0)
                dve.wait_ge(g_mm, 64 * (k + 1))
                weigh(252, 1)
                gv, u0 = g0 + 173, PAIR[f"b{k}"]
                pair_lo(hid[:, 0:2, :], u0)
                pair_lo(hid[:, 2:4, :], u0 + 1)
                with dve.Fori(0, 31) as i:
                    for j in range(4):
                        lo(gv + j + 2, i, 4)
                        if j % 2:
                            u = j // 2 + 2
                            pair_lo(hid[:, bass.ds(i * 4 + 2 * u, 2), :], u0 + u, i, 2)
                for j in range(124, 128):
                    lo(gv + j + 2)
                norm(6 + 2 * k)

        @block.tensor
        def _(pe):
            M = nc.tensor.matmul

            def passes(out_ap, parts_l, parts_r, first=True, last=True, skip=False):
                (lh, ll), (rh, rl) = parts_l, parts_r
                M(out_ap, lh, rh, start=first, stop=False, skip_group_check=skip)
                M(out_ap, lh, rl, start=False, stop=False, skip_group_check=skip)
                return M(out_ap, ll, rh, start=False, stop=last, skip_group_check=skip)

            def wait_tile(b, i, body):
                pe.wait_ge(w_lo, b + 1 + (0 if i is None else i * body))

            def wait_free(e, i, ebody):
                if e >= 2:
                    pe.wait_ge(evac, e - 1 + (0 if i is None else i * ebody))

            def tile_a(b, e, i=None, body=0, ebody=0):
                wait_tile(b, i, body)
                wait_free(e, i, ebody)
                for c in range(DB):
                    ins = passes(ps_t[:, e % 2, 0:T], (wh[b % 2][:, c, :], wl[b % 2][:, c, :]),
                                 (xh[:, c, :], xl[:, c, :]), c == 0, c == DB - 1)
                ins.then_inc(mm_done, 1)

            def tile_b(b, u, j, first=False, last=False, i=None, body=0, ustep=0):
                wait_tile(b, i, body)
                pe.wait_ge(m_lo, u + 1 + (0 if i is None else i * ustep))
                s = 2 * (u % 2) + j
                for c in range(DB):
                    ins = passes(acc[:, c, :], (wh[b % 2][:, c, :], wl[b % 2][:, c, :]),
                                 (mh[:, s, :], ml[:, s, :]), first and c % 2 == 0, last, skip=True)
                ins.then_inc(mm_done, 1)

            def run(tile, g0, e0, count):
                with pe.Fori(0, count // 4) as i:
                    for j in range(4):
                        tile(g0 + j, e0 + j, i, 4, 4)

            def values(g0, e0, v0, count):
                def turn(n, i=None):
                    e = e0 + n - v0
                    pe.wait_ge(evac, e + 1 + (0 if i is None else i * 4))
                    if n >= 2:
                        pe.wait_ge(v_copied, n - 1 + (0 if i is None else i * 4))
                    for c in range(NC_T):
                        ins = nc.tensor.transpose(ps_x[:, n % 2, c * P:(c + 1) * P],
                                                  vT[:, (n - v0) % 2, c * P:(c + 1) * P], ident)
                    ins.then_inc(v_turned, 1)

                for j in range(4):
                    tile_a(g0 + j, e0 + j)
                    if j:
                        turn(v0 + j - 1)
                if count > 4:
                    with pe.Fori(0, count // 4 - 1) as i:
                        for j in range(4):
                            tile_a(g0 + 4 + j, e0 + 4 + j, i, 4, 4)
                            turn(v0 + 3 + j, i)
                turn(v0 + count - 1)
                pe.wait_ge(v_copied, v0 + count)

            def norm(k):
                kind, source, gain, bias = NORMS[k]
                if kind == "ln":
                    for b in range(DB):
                        pe.wait_ge(n_res, res_before[k] + b // 2 + 1)
                        ins = M(ps_x[:, 0, 0:T], ones, xT[:, b, :], start=(b == 0), stop=(b == DB - 1))
                    ins.then_inc(n_mean, 1)
                for b in range(DB):
                    pe.wait_ge(n_sq, 4 * k + b // 2 + 1)
                    ins = M(ps_x[:, 1, 0:T], ones, sq[:, b, :], start=(b == 0), stop=(b == DB - 1))
                ins.then_inc(n_var, 1)
                if k < 8:
                    pe.wait_ge(n_lo, 4 * (k + 1))

            pe.wait_ge(const_in, 32)
            pe.wait_ge(x_in_s, 16)
            for c in range(NC_T):
                for b in range(DB):
                    ins = nc.tensor.transpose(acc[:, b, c * P:(c + 1) * P], x_rows[:, c, b * P:(b + 1) * P], ident)
            ins.then_inc(x_turned, 1)
            pe.wait_ge(x_lo, 1)

            for j in range(4):
                tile_a(j, j)
            run(tile_a, 4, 4, 12)
            values(RET_V, RET_V, 0, 16)
            run(tile_a, RET_G, RET_G, 16)
            pe.wait_ge(retc_in, 16)
            for b in range(8):
                if b >= 2:
                    pe.wait_ge(rope_done, b - 1)
                for j in range(2):
                    ins = M(ps_x[:, b % 2, j * T:(j + 1) * T], rc[:, R_ROT:R_ROT + P], qk[:, 2 * b + j, :],
                            start=True, stop=True)
                ins.then_inc(rope_mm, 1)
            pe.wait_ge(rope_done, 8)

            def ret_scores(h):
                if h >= 2:
                    pe.wait_ge(r_sd, h - 1)
                for j in range(2):
                    dst = ps_x[:, h % 2, 0:T] if j == 0 else ps_x[:, h % 2, T:T + P]
                    for b in range(2):
                        ins = M(dst, qk[:, 8 + 2 * h + b, j * P:(j + 1) * P], qk[:, 2 * h + b, j * P:T],
                                start=(b == 0), stop=(b == 1))
                ins.then_inc(r_s, 1)

            ret_scores(0)
            for h in range(RH):
                if h + 1 < RH:
                    ret_scores(h + 1)
                pe.wait_ge(r_sd, h + 1)
                if h >= 2:
                    pe.wait_ge(r_yc, h - 1)
                for b in range(4):
                    c0 = h * RV + b * P
                    dst = acc[:, 4 * (h % 2) + b, :]
                    M(dst, vt[:, 0, c0:c0 + P], sd[:, h % 2, 0:T], start=True, stop=False)
                    ins = M(dst[:, P:T], vt[:, 1, c0:c0 + P], sd[:, h % 2, T:T + P], start=False, stop=True)
                ins.then_inc(r_y, 1)
                pe.wait_ge(r_yc, h + 1)
                if h == 0:
                    pe.wait_ge(evac, EV["ffn0"])
                for b in range(4):
                    ins = M(ps_t[:, 0, 0:T], ones, ry[:, 4 * h + b, :], start=(b == 0), stop=(b == 3))
                ins.then_inc(r_mean, 1)
                pe.wait_ge(r_sq, h + 1)
                for b in range(4):
                    ins = M(ps_t[:, 1, 0:T], ones, rsq[:, b, :], start=(b == 0), stop=(b == 3))
                ins.then_inc(r_var, 1)
            tile_b(RET_O, 0, 0, first=True)
            tile_b(RET_O + 1, 0, 1)
            tile_b(RET_O + 2, 1, 0)
            tile_b(RET_O + 3, 1, 1)
            with pe.Fori(0, 3) as i:
                for j in range(4):
                    tile_b(RET_O + 4 + j, 2 + j // 2, j % 2, i=i, body=4, ustep=2)
            norm(0)

            def ffn(k):
                name = f"ffn{k}"
                g0, e0, u0 = START[name], EV[name], PAIR[name]
                for j in range(4):
                    tile_a(g0 + j, e0 + j)
                for v in range(2):
                    b = g0 + 4 + 6 * v
                    for j in range(4):
                        tile_a(b + j, e0 + 4 + 4 * v + j)
                    for j in range(2):
                        tile_b(b + 4 + j, u0 + v, j, first=(v == 0 and j == 0))
                with pe.Fori(0, (FU - 1) // 2 - 1) as i:
                    for v in range(2):
                        b = g0 + 16 + 6 * v
                        for j in range(4):
                            tile_a(b + j, e0 + 12 + 4 * v + j, i, 12, 8)
                        for j in range(2):
                            tile_b(b + 4 + j, u0 + 2 + v, j, i=i, body=12, ustep=2)
                for j in range(2):
                    tile_b(g0 + FFN_TILES - 2 + j, u0 + FU - 1, j)

            ffn(0)
            norm(1)

            g0, e0 = START["att"], EV["att"]
            pe.wait_ge(attc_in, 16)
            for g in range(G3):
                ins = M(ps_a[0:AH, g, 0:384], ac[0:33, G3 * 384 + g * AH:G3 * 384 + (g + 1) * AH],
                        ac[0:33, g * 384:(g + 1) * 384], start=True, stop=True)
            ins.then_inc(b_vec, 1)
            run(tile_a, g0, e0, 48)
            values(g0 + 48, e0 + 48, 16, 24)
            pe.wait_ge(evac, e0 + 72)
            pe.wait_ge(b_vecc, G3)

            def att_scores(h):
                s, r, hp = h % 2, 64 * (h % 2), h // 2
                pe.wait_ge(b_in[s], 16 * (h // 2 + 1))
                if h >= 2:
                    pe.wait_ge(a_oc, h - 1)
                flat = ps[:, 3 * s:3 * s + 3, :].rearrange("p a b -> p (a b)")
                for g in range(G3):
                    m = 8 * g + hp
                    for c in (1, 0):
                        w = T if c else P
                        o = g * T if c else 1024 + g * P
                        M(flat[:, o:o + w], aq[r:r + HD, m, c * P:(c + 1) * P], ak[r:r + HD, m, 0:w],
                          start=True, stop=False)
                        ins = M(flat[:, o:o + w], flip, bs[:, s, g, T - w:T], start=False, stop=True)
                ins.then_inc(a_s, 1)

            att_scores(0)
            for h in range(AH):
                s, r = h % 2, 64 * (h % 2)
                if h + 1 < AH:
                    att_scores(h + 1)
                pe.wait_ge(a_p, h + 1)
                if h:
                    pe.wait_ge(a_tc, 3 * h)
                for g in range(G3):
                    dst = ps[:, 6 + g // 2, (g % 2) * T:(g % 2) * T + T]
                    nc.tensor.transpose(dst[:, 0:P], pr[:, s, 768 + g * P:768 + (g + 1) * P], ident)
                    nc.tensor.transpose(dst[:, P:T], pr[:, s, g * T:g * T + P], ident)
                for g in range(G3):
                    dst = ps[:, 7, T + g * P:T + (g + 1) * P] if g < 2 else ps[:, 3 * s, 0:P]
                    ins = nc.tensor.transpose(dst, pr[:, s, g * T + P:(g + 1) * T], ident)
                ins.then_inc(a_t, 1)
                dst = ps[r:r + HD, 3 * s + 1, 0:T]
                for g in range(G3):
                    pe.wait_ge(a_tc, 3 * h + 1 + g // 2)
                    c0 = g * D + h * HD
                    M(dst, av[:, 0, c0:c0 + HD], pt_s[:, g * T:(g + 1) * T], start=(g == 0), stop=False)
                for g in range(G3):
                    pe.wait_ge(a_tc, 3 * h + 2 + g // 2)
                    c0, o = g * D + h * HD, 768 + g * P
                    ins = M(dst[:, P:T], av[:, 1, c0:c0 + HD], pt_s[:, o:o + P], start=False, stop=(g == 2))
                ins.then_inc(a_o, 1)
            pe.wait_ge(a_lo, 1)
            run(tile_a, g0 + 72, e0 + 72, 8)
            norm(2)
            ffn(1)
            norm(3)

            norm(4)
            for k in range(2):
                g0, e0 = START[f"b{k}"], EV[f"b{k}"]
                for j in range(8):
                    tile_a(g0 + j, e0 + j)
                values(g0 + 8, e0 + 8, 40 + 4 * k, 4)
                for j in range(12, 21):
                    tile_a(g0 + j, e0 + j)
                pe.wait_ge(xc_done, k + 1)
                pe.wait_ge(bd_in, 16 * (k + 1))
                pe.wait_ge(evac, e0 + 21)
                for m in range(2):
                    for b in range(2):
                        ins = M(ps_a[:, 2 + m, b * T:(b + 1) * T], bd[:, m, b, :], xc[:, b, :], start=True, stop=True)
                ins.then_inc(rg_mm, 1)
                pe.wait_ge(cum_done, k + 1)

                def att2_scores(h):
                    s, r, hp = h % 2, 64 * (h % 2), h // 2
                    if h >= 2:
                        pe.wait_ge(a_e, AH + H2 * k + h - 1)
                    one_h = ident[0:H2, h:h + 1]
                    for c in (1, 0):
                        w = T if c else P
                        o = 0 if c else T
                        dst = ps[:, s, o:o + w]
                        M(dst, q2[r:r + HD, hp, c * P:(c + 1) * P], k2[r:r + HD, hp, 0:w], start=True, stop=False)
                        M(dst, fz[0:H2, 4, c * P:(c + 1) * P], one_h.to_broadcast([H2, w]), start=False, stop=False)
                        M(dst, one_h.to_broadcast([H2, P]), fz[0:H2, 5, 0:w], start=False, stop=False)
                        ins = M(dst[:, w - P:w], ident, tri, start=False, stop=True)
                    ins.then_inc(a_s, 1)

                att2_scores(0)
                att2_scores(1)
                for h in range(H2):
                    s, r = h % 2, 64 * (h % 2)
                    n = AH + H2 * k + h
                    pe.wait_ge(a_p, n + 1)
                    if h:
                        pe.wait_ge(a_tc, 3 * AH + H2 * k + h)
                    nc.tensor.transpose(ps_x[:, 0, 0:P], p2[:, s, T:T + P], ident)
                    nc.tensor.transpose(ps_x[:, 0, P:T], p2[:, s, 0:P], ident)
                    nc.tensor.transpose(ps_x[:, 0, T:T + P], p2[:, s, P:T], ident).then_inc(a_t, 1)
                    if h + 2 < H2:
                        att2_scores(h + 2)
                    pe.wait_ge(a_tc, 3 * AH + H2 * k + h + 1)
                    if h:
                        pe.wait_ge(a_oc, n)
                    dst = ps_x[r:r + HD, 1, 0:T]
                    M(dst, v2[:, 0, h * HD:(h + 1) * HD], p2T[:, 0:T], start=True, stop=False)
                    M(dst[:, P:T], v2[:, 1, h * HD:(h + 1) * HD], p2T[:, T:T + P], start=False, stop=True) \
                        .then_inc(a_o, 1)
                pe.wait_ge(cv_y, k + 1)
                pe.wait_ge(a_oc, AH + H2 * (k + 1))
                for b in range(2):
                    ins = M(ps_x[:, 0, 0:T], ones, cy[:, b, :], start=(b == 0), stop=(b == 1))
                ins.then_inc(cv_mean, 1)
                pe.wait_ge(cv_sq, k + 1)
                for b in range(2):
                    ins = M(ps_x[:, 1, 0:T], ones, csq[:, b, :], start=(b == 0), stop=(b == 1))
                ins.then_inc(cv_var, 1)
                pe.wait_ge(a_lo, k + 2)
                run(tile_a, g0 + 21, e0 + 21, 8)
                norm(5 + 2 * k)

                run(tile_a, g0 + 29, e0 + 29, 16)
                pe.wait_ge(evac, e0 + 45)
                pe.wait_ge(k_in, 16 * (k + 1))
                for c in range(NC_T):
                    n = 2 * k + c
                    for j in range(4):
                        if c:
                            pe.wait_ge(p_sc, 4 * n + j - 3)
                        for h in (2 * j, 2 * j + 1):
                            for s in range(2):
                                o = (h % 2) * 256 + s * P
                                ins = M(ps_a[:, j, o:o + P], pq[:, 2 * h + s, c * P:(c + 1) * P],
                                        pk[:, s, h, :], start=True, stop=True)
                        ins.then_inc(p_s, 1)
                for c in range(NC_T):
                    n = 2 * k + c
                    pe.wait_ge(p_e, n + 1)
                    if c:
                        pe.wait_ge(p_tc, 3 * n)
                    for m, src in enumerate((ee[:, 0, :, :], ee[:, 1, :, :], ge)):
                        ins = nc.tensor.transpose(ps_x[:, 0, m * P:(m + 1) * P],
                                                  src.rearrange("p h j -> p (h j)"), ident)
                    ins.then_inc(p_t, 1)
                run(tile_a, g0 + 45, e0 + 45, 128)

                def gates(s):
                    for j in range(4):
                        ins = M(ps_x[:, s, j * P:(j + 1) * P], oh1[s][:, j, :], oh2[s][:, j, :],
                                start=True, stop=True)
                    ins.then_inc(g_mm, 1)

                pe.wait_ge(p_tc, 6 * (k + 1))
                for s in range(2):
                    pe.wait_ge(g_hot, 64 * k + s + 1)
                    gates(s)
                with pe.Fori(0, 31) as i:
                    for s in range(2):
                        pe.wait_ge(g_hot, i * 2 + 64 * k + 3 + s)
                        pe.wait_ge(g_mul, i * 2 + 64 * k + 1 + s)
                        gates(s)
                gv, u0 = g0 + 173, PAIR[f"b{k}"]
                for j in range(4):
                    tile_b(gv + j, u0 + j // 2, j % 2, first=(j == 0))
                with pe.Fori(0, 31) as i:
                    for j in range(4):
                        tile_b(gv + 4 + j, u0 + 2 + j // 2, j % 2, i=i, body=4, ustep=2)
                norm(6 + 2 * k)
            for c in range(NC_T):
                for b in range(DB):
                    pe.wait_ge(n_y, 32 + b // 2 + 1)
                    ins = nc.tensor.transpose(ps_a[:, 2 * c + b // 4, (b % 4) * P:(b % 4 + 1) * P],
                                              yn[:, b, c * P:(c + 1) * P], ident)
                    if b % 4 == 3:
                        ins.then_inc(o_turned, 1)


def constants():
    c = np.zeros((P, NCONST), np.float32)
    p = np.arange(P)
    c[:, C_ID:C_ID + P] = np.eye(P)
    c[:, C_ONE:C_ONE + P] = 1.0
    c[:, C_J:C_J + P] = np.eye(P)[::-1]
    c[:, C_MASK:C_MASK + P] = np.where(p[None, :] > p[:, None], MASKED, 0.0)
    c[:, C_IOTA:C_IOTA + P] = p
    c[:, C_I16:C_I16 + 16] = np.arange(16)
    return c


def retention_constants():
    c = np.zeros((P, NRET), np.float32)
    e, p, t = np.arange(0, P, 2), np.arange(P), np.arange(T)
    c[e + 1, R_ROT + e] = -1.0
    c[e, R_ROT + e + 1] = 1.0
    inv = np.float32(1.0) / (np.float32(10000.0) ** np.linspace(0.0, 1.0, RQ // 2, dtype=np.float32))
    ang = (t.astype(np.float32)[None, :] * inv[:, None]).astype(np.float32).astype(np.float64)
    pair = ((np.arange(2)[None, :] * P + p[:, None]) // 2)
    c[:, R_COS:R_COS + 512] = np.cos(ang)[pair].reshape(P, 512)
    c[:, R_SIN:R_SIN + 512] = np.sin(ang)[pair].reshape(P, 512)
    diff = np.concatenate([t, np.arange(P)])[None, :] - p[:, None]
    for h in range(RH):
        g = np.log1p(-(2.0 ** (-5.0 - h)))
        d = np.where(diff >= 0, np.exp(np.maximum(diff, 0) * g), 0.0) * RQ ** -0.5
        c[:, R_D + 384 * h:R_D + 384 * (h + 1)] = d
    return c


def bias_one_hots():
    c = np.zeros((33, G3, 384), np.float32)
    x = np.arange(384)
    delta = 255 - x
    half = BUCKETS // 2
    d = np.maximum(delta, 1).astype(np.float32)
    large = half + (np.log(d / half) / np.float32(np.log(MAXD / half)) * half).astype(np.int32)
    bucket = np.where(delta < half, delta, np.minimum(large, BUCKETS - 1))
    for g, (window, dil) in enumerate(PAIRS):
        ok = (delta >= 0) & (delta % dil == 0) & (delta // dil <= window // dil)
        c[bucket[ok], g, x[ok]] = 1.0
        c[32, g, ~ok] = MASKED
    return c.reshape(33, G3 * 384)


def kernel(**inputs):
    import concourse.bacc as bacc
    from concourse.bass_utils import run_bass_kernel_spmd

    a = {k: np.asarray(v) for k, v in inputs.items()}

    def cols(w):
        return w.reshape(DB, P, -1, P).transpose(2, 1, 0, 3).reshape(-1, P, TILE)

    stream = np.empty((TILES, P, TILE), np.float32)
    at = [0]

    def put(tiles):
        stream[at[0]:at[0] + len(tiles)] = tiles
        at[0] += len(tiles)

    def put_ffn(k):
        up = cols(a["ffn_w_up"][k])
        down = a["ffn_w_down"][k].reshape(-1, P, TILE)
        for u in range(FU + 1):
            if u < FU:
                put(up[2 * u:2 * u + 2])
                put(up[FF // P + 2 * u:FF // P + 2 * u + 2])
            if u:
                put(down[2 * u - 2:2 * u])

    w = a["ret_w_in"][0]
    put(cols(w))
    put(a["ret_w_out"][0].reshape(-1, P, TILE))
    put_ffn(0)
    put(cols(a["attn_w_in"][0]))
    put(cols(a["attn_w_out"][0]))
    put_ffn(1)
    for k in range(2):
        w = a["w_in_2"][k]
        put(cols(w[:, 0:1536]))
        forget = np.zeros((D, P), np.float32)
        forget[:, 0:H2] = w[:, 1536:1536 + H2]
        put(cols(forget))
        put(cols(w[:, 1536 + H2:]))
        put(cols(a["w_out_2"][k]))
        put(cols(a["peer_wq_2"][k]))
        put(a["peer_u_2"][k].reshape(NK, NK, DB, P).transpose(1, 3, 2, 0).reshape(NK, P, TILE))
        put(a["peer_v_2"][k].reshape(NK, NK, TILE).transpose(1, 0, 2))
    assert at[0] == TILES

    def blocks(v):
        return v.reshape(-1, P).T

    vecs = np.zeros((P, NVEC), np.float32)
    for c, v in ((V_LNG, a["ln_gain"]), (V_LNB, a["ln_bias"]), (V_N1, a["norm1_g_2"]), (V_N2, a["norm2_g_2"]),
                 (V_FIN, a["final_g_2"]), (V_CB, a["conv_dw_b_2"]), (V_CG, a["conv_ln_g_2"]),
                 (V_CN, a["conv_ln_b_2"]), (V_RB, a["rg_conv_b_2"]), (V_BR, a["rg_b_r_2"]),
                 (V_BI, a["rg_b_i_2"]), (V_LAM, a["rg_lambda_2"])):
        m = blocks(v)
        vecs[:, c:c + m.shape[1]] = m
    for c, v in ((V_CW, a["conv_dw_w_2"]), (V_RW, a["rg_conv_w_2"])):
        taps = v.shape[1]
        vecs[:, c:c + 4 * taps] = v.reshape(2, taps, 2, P).transpose(3, 0, 2, 1).reshape(P, 4 * taps)
    vecs[0:H2, V_BF:V_BF + 2] = a["b_forget_2"].T
    vecs[:, V_EPS1], vecs[:, V_EPS2] = LN_EPS, EPS2

    rg_w = np.zeros((2, P, 2, 2, P), np.float32)
    for m, name in enumerate(("rg_w_r_2", "rg_w_i_2")):
        for h in range(4):
            r = slice(64 * (h % 2), 64 * (h % 2) + 64)
            rg_w[:, r, m, h // 2, r] = a[name][:, h]
    keys = np.stack([a["peer_k1_2"], a["peer_k2_2"]], 1).transpose(0, 4, 1, 2, 3)
    att_c = np.zeros((33, NATT), np.float32)
    att_c[:, 0:G3 * 384] = bias_one_hots()
    att_c[0:32, G3 * 384:] = a["rel_bias"].T
    att_c[32, G3 * 384:] = 1.0

    arrays = {"stream": stream, "x": a["x"].reshape(T, D), "consts": constants(), "ret_c": retention_constants(),
              "att_c": att_c, "vecs": vecs, "rg_w": rg_w, "keys": keys}
    arrays = {k: np.ascontiguousarray(v, np.float32) for k, v in arrays.items()}
    nc = bacc.Bacc("TRN2", target_bir_lowering=False, num_devices=1)
    args = {k: nc.dram_tensor(k + "_dram", v.shape, F32, kind="ExternalInput").ap() for k, v in arrays.items()}
    scratch = nc.dram_tensor("bias_scratch", (G3, AH, 384), F32, kind="Internal").ap()
    out = nc.dram_tensor("out_dram", (T, D), F32, kind="ExternalOutput").ap()
    build(nc, args["stream"], args["x"], args["consts"], args["ret_c"], args["att_c"], args["vecs"],
          args["rg_w"], args["keys"], scratch, out)
    r = run_bass_kernel_spmd(nc, [{k + "_dram": v for k, v in arrays.items()}], core_ids=[0])
    return r.results[0]["out_dram"].reshape(1, T, D)
```

```python
from contextlib import ExitStack

import numpy as np

import concourse.bass as bass
from concourse import mybir

F32 = mybir.dt.float32
F32R = mybir.dt.float32r
U32 = mybir.dt.uint32
ACT = mybir.ActivationFunctionType
ALU = mybir.AluOpType
AX = mybir.AxisListType.X

P = 128
T = 256
D = 1024
DB = D // P
TILE = 1024
NC_T = T // P

RH, RQ, RV = 4, 256, 512
RVB = RH * RV // P
FF = 2816
FU = FF // P // 2
G3, AH, HD = 3, 16, 64
PAIRS = ((128, 1), (512, 4), (2048, 16))
BUCKETS, MAXD = 32, 2048
ALPHA = 4 ** 0.25
LN_EPS = 1e-5
H2 = 8
CK, RK = 31, 4
NK, TOPK = 128, 16
EPS2 = 1e-6
RG_C = 8.0
PICK_STEPS = 43                     
MASKED = -1e30
LOWEST = -3.0e38

RET0 = 0
RET_V, RET_G, RET_O = 16, 32, 48
FFN_TILES = 6 * FU
ATT_TILES = 80
B2_TILES = 21 + 8 + 16 + 128 + 128
START = {"ret": 0, "ffn0": 64, "att": 64 + FFN_TILES, "ffn1": 64 + FFN_TILES + ATT_TILES}
START["b0"] = START["ffn1"] + FFN_TILES
START["b1"] = START["b0"] + B2_TILES
TILES = START["b1"] + B2_TILES
EV = {"ret": 0, "ffn0": 48, "att": 48 + 4 * FU, "ffn1": 48 + 4 * FU + 80}
EV["b0"] = EV["ffn1"] + 4 * FU
EV["b1"] = EV["b0"] + 173
PAIR = {"ret": 0, "ffn0": 8, "ffn1": 8 + FU, "b0": 8 + 2 * FU, "b1": 8 + 2 * FU + 64}

C_ID, C_ONE, C_J, C_MASK, C_IOTA, C_I16 = 0, 128, 256, 384, 512, 640
NCONST = 656
R_ROT, R_COS, R_SIN, R_D = 0, 128, 640, 1152
NRET = 1152 + RH * 384
NATT = G3 * 384 + G3 * AH

V_LNG, V_LNB, V_N1, V_N2, V_FIN = 0, 32, 64, 80, 96
V_CW, V_CB, V_CG, V_CN, V_RW, V_RB, V_BR, V_BI, V_LAM, V_BF, V_EPS1, V_EPS2 = \
    104, 228, 232, 236, 240, 256, 260, 264, 268, 272, 274, 275
NVEC = 276


def build(nc, stream, x_in, consts, ret_c, att_c, vecs, rg_w, keys, scratch, out):
    with ExitStack() as ctx:
        def sb(name, cols, dt=F32):
            return ctx.enter_context(nc.sbuf_tensor(name, [P, *cols], dt))

        def sem(name):
            return ctx.enter_context(nc.semaphore(name))

        arena = sb("arena", [32768])
        xT = sb("xT", [DB, T])
        xh, xl = sb("xh", [DB, T], F32R), sb("xl", [DB, T], F32R)
        raw = sb("raw", [4, TILE])
        wh = [sb(f"wh{i}", [DB, P], F32R) for i in range(2)]
        wl = [sb(f"wl{i}", [DB, P], F32R) for i in range(2)]
        mh, ml = sb("mh", [4, T], F32R), sb("ml", [4, T], F32R)
        cst = sb("cst", [NCONST])
        vec = sb("vec", [NVEC])
        pickT = sb("pickT", [3, T])
        picks = sb("picks", [2240])
        ps = ctx.enter_context(nc.psum_tensor("ps", [P, 8, 512], F32))
        ps_a, ps_t, ps_x = ps[:, 0:4, :], ps[:, 4:6, :], ps[:, 6:8, :]
        acc = ps_a.rearrange("p a (b t) -> p (a b) t", b=2)

        def ar(off, *shape):
            n = int(np.prod(shape))
            v = arena[:, off:off + n]
            if len(shape) == 2:
                v = v.rearrange("p (a b) -> p a b", a=shape[0])
            elif len(shape) == 3:
                v = v.rearrange("p (a b c) -> p a b c", a=shape[0], b=shape[1])
            elif len(shape) == 4:
                v = v.rearrange("p (a b c d) -> p a b c d", a=shape[0], b=shape[1], c=shape[2])
            return v

        ident, ones = cst[:, C_ID:C_ID + P], cst[:, C_ONE:C_ONE + P]
        flip, tri = cst[:, C_J:C_J + P], cst[:, C_MASK:C_MASK + P]
        iota, iota16 = cst[:, C_IOTA:C_IOTA + P], cst[:, C_I16:C_I16 + 16]

        mix, sq, yn = ar(0, DB, T), ar(2048, DB, T), ar(4096, DB, T)
        std, rstd = ar(6144, T), ar(6400, T)
        unused = ar(6656, 1)
        vT = ar(7168, 2, T)
        x_rows = ar(8192, NC_T, D)
        rc = ar(8192, NRET)
        qk, vt, sg = ar(12288, 16, T), ar(16384, NC_T, RH * RV), ar(20480, RVB, T)
        ry, rt = ar(24576, RVB, T), ar(28672, 2, 512)
        sd, rsq = ar(29696, 2, 384), ar(30720, 4, T)
        rstat = ar(10880, 2, 2, T)
        fg, fu, fm = ar(8192, 2, 512), ar(9216, 2, 512), ar(10240, 2, 512)
        aq, ak, av = ar(8192, 24, T), ar(14336, 24, T), ar(20480, NC_T, G3 * D)
        ac = ar(26624, NATT)
        bv = ar(27904, G3, 384)
        bs = ar(2112, 2, G3, T)
        pr = ar(29056, 2, 1152)
        pt_s = ar(31360, 1152)
        ao = ar(0, DB, T)
        ast = ar(2048, 2, 8)
        q2, k2, v2 = ar(8192, 4, T), ar(9216, 4, T), ar(10240, NC_T, 512)
        fz = ar(11264, 6, T)
        ca, cg = ar(12800, 2, T), ar(13312, 2, T)
        cpad, cy = ar(13824, 2, T + 32), ar(14400, 2, T)
        xrp, xc = ar(14912, 2, T + 4), ar(15440, 2, T)
        gg, rr, ri = ar(15952, 2, T), ar(16464, 2, T), ar(16976, 2, T)
        la, aa, th, mu, bt, hs = (ar(17488 + 512 * i, 2, T) for i in range(6))
        csq, cstd = ar(20560, 2, T), ar(21072, 2, T)
        spw = ar(21584, 8, 2)
        bd = ar(21632, 2, 2, P)
        p2, p2T, o2 = ar(22144, 2, 384), ar(22912, 384), ar(23296, DB, T)
        st2 = ar(25344, 2, 8)
        pq, pk = ar(8192, 16, T), ar(12288, 2, H2, P)
        sc = ar(28672, NC_T * H2, 2, P)
        def pick_part(off, *shape):
            n = int(np.prod(shape))
            names = " ".join("abcd"[:len(shape)])
            return picks[:, off:off + n].rearrange(f"p ({names}) -> p {names}",
                                                   **dict(zip("abcd", shape)))

        cur, best = pick_part(1152, 2, 2, P), pick_part(1664, 2, 2, P)
        cand, cand2 = pick_part(1152, 2, 16, 16), pick_part(1664, 2, 256)
        hot = mh[:, 0:2, :].rearrange("p h (a b) -> p h a b", a=16)
        hot_out, hot = hot, hot.bitcast(F32)
        ee, ge = pick_part(0, 2, NC_T * H2, 16), pick_part(512, NC_T * H2, 16)
        tv, tf, ti = pick_part(768, 2, 2, 16), pick_part(832, 2, 2, 16), pick_part(896, 2, 2, 16).bitcast(U32)
        sv, ci = pick_part(960, 2, 16), pick_part(992, 2, 16).bitcast(U32)
        cr, crf = pick_part(1024, 2, 2, 16).bitcast(U32), pick_part(1088, 2, 2, 16)
        gd = pick_part(2176, 2, NC_T * H2)
        e1T, e2T, gT = (pickT[:, m, :] for m in range(3))
        oh = [t[:, 4 * n:4 * n + 4, :].rearrange("p a (b n) -> p (a b) n", b=2) for t in (xh, xl) for n in range(2)]
        gated = [pick_part(512 * n, 4, P) for n in range(4)]
        hid = ar(0, NK, T)
        o_rows = ar(8192, NC_T, D)

        raw_ready = [sem(f"raw_ready{i}") for i in range(4)]
        w_hi, w_lo, mm_done, evac = sem("w_hi"), sem("w_lo"), sem("mm_done"), sem("evac")
        m_hi, m_lo = sem("m_hi"), sem("m_lo")
        const_in, x_in_s, retc_in, attc_in = sem("const_in"), sem("x_in"), sem("retc_in"), sem("attc_in")
        x_turned, x_copied, x_hi, x_lo = sem("x_turned"), sem("x_copied"), sem("x_hi"), sem("x_lo")
        v_turned, v_copied = sem("values_turned"), sem("values_copied")
        dve_step, act_step = sem("dve_step"), sem("act_step")
        n_res, n_mean, n_cen, n_sq, n_var, n_std, n_y, n_hi, n_lo = (
            sem(f"norm_{s}") for s in "residual mean centred squares variance std scaled hi lo".split())
        rope_mm, rope_done = sem("rope_mm"), sem("rope_done")
        r_s, r_sd, r_y, r_yc, r_mean, r_cen, r_sq, r_var, r_std, r_out = (
            sem(f"ret_{s}") for s in "scores decayed y y_copied mean centred squares var std out".split())
        f_mid = sem("ffn_mid")
        b_vec, b_vecc, b_store = sem("bias_vec"), sem("bias_vec_copied"), sem("bias_stored")
        b_in = [sem("bias_in0"), sem("bias_in1")]
        a_s, a_m, a_e, a_p, a_t, a_tc, a_o, a_oc, a_hi, a_lo = (
            sem(f"att_{s}") for s in "scores max exp probs turned turned_copied out out_copied hi lo".split())
        z_done, cum_done = sem("forget_z"), sem("forget_cum")
        z_abs, z_ln = sem("forget_abs"), sem("forget_ln")
        cv_y, cv_mean, cv_cen, cv_sq, cv_var, cv_std, cv_n, cv_o = (
            sem(f"conv_{s}") for s in "y mean centred squares var std normed out".split())
        bd_in, xc_done, rg_mm, rg_sig, rg_la, rg_exp, rg_m2, rg_mult, rg_o = (
            sem(s) for s in "bd_in rnn_x rnn_mm rnn_sigmoid rnn_log_a rnn_exp rnn_m2 rnn_mult rnn_out".split())
        sp_abs, sp_exp, sp_done = sem("rate_abs"), sem("rate_exp"), sem("rate_done")
        k_in, p_s, p_sc, pick_step, p_exp, p_e, p_t, p_tc = (
            sem(s) for s in "keys_in peer_scores peer_scores_copied peer_pick_step peer_exp "
            "peer_picked peer_turned peer_turned_copied".split())
        g_hot, g_gated = sem("peer_onehots"), sem("peer_gated_rows")
        g_mm, g_mul = sem("peer_gates"), sem("peer_weighted")
        o_turned, o_copied, o_stored = sem("out_turned"), sem("out_copied"), sem("out_stored")

        block = ctx.enter_context(nc.Block())

        NORMS = [("ln", "acc", V_LNG, V_LNB), ("ln", "acc", V_LNG + 8, V_LNB + 8),
                 ("ln", "mix", V_LNG + 16, V_LNB + 16), ("ln", "acc", V_LNG + 24, V_LNB + 24),
                 ("rms", None, V_N1, None), ("rms", "mix", V_N2, None),
                 ("rms", "acc", V_N1 + 8, None), ("rms", "mix", V_N2 + 8, None),
                 ("rms", "acc", V_FIN, None)]
        res_before = [4 * sum(s is not None for _, s, _, _ in NORMS[:k]) for k in range(10)]
        ln_before = [sum(m == "ln" for m, *_ in NORMS[:k]) for k in range(10)]

        def acc_tiles(k):
            return [START["ffn0"], START["att"], START["ffn1"], START["b0"], 0,
                    START["b0"] + 29, START["b1"], START["b1"] + 29, TILES][k]

        @block.sync
        def _(sp):
            def load(slot, g):
                sp.dma_start(raw[:, slot, :], stream[bass.ds(g, 1), :, :].rearrange("a p n -> p (a n)")) \
                    .then_inc(raw_ready[slot], 16)

            for g in range(4):
                load(g, g)
            with sp.Fori(1, TILES // 4) as i:
                for s in range(4):
                    sp.wait_ge(w_lo, i * 4 + (s - 3))
                    load(s, i * 4 + s)
            for g in range(TILES // 4 * 4, TILES):
                sp.wait_ge(w_lo, g - 3)
                load(g % 4, g)

        @block.gpsimd
        def _(pool):
            pool.dma_start(cst[:, :], consts).then_inc(const_in, 16)
            pool.dma_start(vec[:, :], vecs).then_inc(const_in, 16)
            pool.dma_start(x_rows, x_in.rearrange("(c p) d -> p c d", p=P)).then_inc(x_in_s, 16)
            pool.wait_ge(x_turned, 1)
            pool.dma_start(rc, ret_c).then_inc(retc_in, 16)
            pool.wait_ge(n_lo, 8)
            pool.dma_start(ac[0:33, :], att_c).then_inc(attc_in, 16)
            pool.wait_ge(b_vecc, G3)
            pool.dma_start(scratch.rearrange("g h x -> h g x"), bv[0:AH, :, :]).then_inc(b_store, 16)
            pool.wait_ge(b_store, 16)
            for h in range(AH):
                if h >= 2:
                    pool.wait_ge(a_s, h - 1)
                pool.dma_start(bs[:, h % 2, :, :], bass.AP(
                    scratch.tensor, h * 384, [[1, P], [AH * 384, G3], [1, T]])).then_inc(b_in[h % 2], 16)

            for k in range(2):
                pool.wait_ge(n_lo, 4 * (5 + 2 * k))
                pool.dma_start(bd, rg_w[k]).then_inc(bd_in, 16)
                pool.wait_ge(n_lo, 4 * (6 + 2 * k))
                pool.dma_start(pk, keys[k]).then_inc(k_in, 16)
            pool.wait_ge(o_copied, 4)
            pool.dma_start(out.rearrange("(c p) d -> p c d", p=P), o_rows).then_inc(o_stored, 16)
            pool.wait_ge(o_stored, 16)

        @block.scalar
        def _(act):
            A = nc.scalar.activation
            steps = [0]

            def link(ins):
                steps[0] = steps[0] + 1
                ins.then_inc(act_step, 1)
                act.wait_ge(act_step, steps[0])

            def hi(b, i=None, body=0):
                if i is None and b >= TILES:
                    return
                n = 0 if i is None else i
                act.wait_ge(raw_ready[b % 4], 16 * (b // 4 + 1) + n * (4 * body))
                if b >= 2:
                    act.wait_ge(mm_done, (b - 1) + n * body)
                A(wh[b % 2][:, :, :], raw[:, b % 4, :].rearrange("p (a b) -> p a b", a=DB), ACT.Copy) \
                    .then_inc(w_hi, 1)

            def evacuate(g, e, dst, func=ACT.Copy, i=None, body=0, ebody=0, scale=1.0, bias=None,
                         src=None, rows=P):
                n = 0 if i is None else i
                act.wait_ge(mm_done, g + 1 + n * body)
                src = ps_t[0:rows, e % 2, 0:T] if src is None else src
                kw = {} if bias is None else {"bias": bias}
                A(dst, src, func, scale=scale, **kw).then_inc(evac, 1)

            def run(g0, e0, count, dst, **kw):
                with act.Fori(0, count // 4) as i:
                    for j in range(4):
                        hi(g0 + j + 2, i, 4)
                        evacuate(g0 + j, e0 + j, dst(i * 4 + j), i=i, body=4, **kw)

            def values(g0, e0, count):
                with act.Fori(0, count // 4) as i:
                    for j in range(4):
                        hi(g0 + j + 2, i, 4)
                        evacuate(g0 + j, e0 + j, vT[:, j % 2, :], i=i, body=4)

            def one(ap, n):
                return ap[:, bass.ds(n, 1), :].rearrange("p a b -> p (a b)")

            def pair_hi(src, u, i=None, step=0, tile=0, body=0):
                n = 0 if i is None else i
                if tile:
                    act.wait_ge(mm_done, tile + n * body)
                s = 2 * (u % 2)
                A(mh[:, s:s + 2, :], src, ACT.Copy).then_inc(m_hi, 1)

            def norm(k):
                kind, _, gain, bias = NORMS[k]
                N = D
                for g in range(4):
                    if kind == "ln":
                        act.wait_ge(n_cen, 4 * ln_before[k] + g + 1)
                    elif NORMS[k][1] is not None:
                        act.wait_ge(n_res, res_before[k] + g + 1)
                    else:
                        act.wait_ge(n_lo, 4 * (k - 1) + g + 1)
                    A(sq[:, 2 * g:2 * g + 2, :], xT[:, 2 * g:2 * g + 2, :], ACT.Square).then_inc(n_sq, 1)
                A(unused, ones[:, 0:1], ACT.Sqrt)
                act.wait_ge(n_var, k + 1)
                eps = V_EPS1 if kind == "ln" else V_EPS2
                A(std, ps_x[:, 1, 0:T], ACT.Sqrt, bias=vec[:, eps:eps + 1], scale=1.0 / N).then_inc(n_std, 1)
                for g in range(4 if k < 8 else 0):
                    act.wait_ge(n_y, 4 * k + g + 1)
                    if kind == "ln":
                        for b in (2 * g, 2 * g + 1):
                            ins = A(xh[:, b, :], yn[:, b, :], ACT.Identity, bias=vec[:, bias + b:bias + b + 1])
                    else:
                        ins = A(xh[:, 2 * g:2 * g + 2, :], yn[:, 2 * g:2 * g + 2, :], ACT.Copy)
                    ins.then_inc(n_hi, 1)

            act.wait_ge(const_in, 32)
            hi(0)
            hi(1)
            act.wait_ge(x_turned, 1)
            for g in range(4):
                A(xT[:, 2 * g:2 * g + 2, :], acc[:, 2 * g:2 * g + 2, :], ACT.Copy).then_inc(x_copied, 1)
            act.wait_ge(x_copied, 4)
            A(xh[:, :, :], xT[:, :, :], ACT.Copy).then_inc(x_hi, 1)

            run(0, 0, 16, lambda n: one(qk, n))
            values(RET_V, RET_V, 16)
            run(RET_G, RET_G, 16, lambda n: one(sg, n), func=ACT.Silu)
            for h in range(RH):
                act.wait_ge(r_y, h + 1)
                yh = ry[:, 4 * h:4 * h + 4, :]
                b0 = 4 * (h % 2)
                A(yh, acc[:, b0:b0 + 4, :], ACT.Copy).then_inc(r_yc, 1)
                act.wait_ge(r_cen, h + 1)
                A(rsq, yh, ACT.Square).then_inc(r_sq, 1)
                act.wait_ge(r_var, h + 1)
                A(rstat[:, h % 2, 0, :], ps_t[:, 1, 0:T], ACT.Sqrt, bias=vec[:, V_EPS1:V_EPS1 + 1],
                  scale=1.0 / RV).then_inc(r_std, 1)
            act.wait_ge(r_out, RH)
            pair_hi(ry[:, 0:2, :], 0)
            pair_hi(ry[:, 2:4, :], 1)
            with act.Fori(0, 3) as i:
                for j in range(4):
                    hi(RET_O + j + 2, i, 4)
                    if j % 2:
                        u = j // 2 + 2
                        pair_hi(ry[:, bass.ds(i * 4 + 2 * u, 2), :], u, i, 2, RET_O + j + 1, 4)
            for j in range(12, 16):
                hi(RET_O + j + 2)
            norm(0)

            def ffn(k):
                name = f"ffn{k}"
                g0, e0, u0 = START[name], EV[name], PAIR[name]

                def a_tiles(g, e, u, i=None):
                    for j in range(4):
                        hi(g + j + 2, i, 12)
                        dst = (fg if j < 2 else fu)[:, u % 2, (j % 2) * T:(j % 2 + 1) * T]
                        evacuate(g + j, e + j, dst, ACT.Silu if j < 2 else ACT.Copy, i=i, body=12)

                def pair(u, tile, i=None):
                    n = 0 if i is None else i
                    act.wait_ge(f_mid, FU * k + u + 1 + n * 2)
                    pair_hi(fm[:, u % 2, :].rearrange("p (a t) -> p a t", a=2), u0 + u, i, 2, tile, 12)

                a_tiles(g0, e0, 0)
                pair(0, g0)
                with act.Fori(0, (FU - 1) // 2) as i:
                    for v in range(2):
                        b = g0 + 4 + 6 * v
                        a_tiles(b, e0 + 4 + 4 * v, v + 1, i)
                        hi(b + 4 + 2, i, 12)
                        pair(v + 1, b, i)
                        hi(b + 5 + 2, i, 12)
                b = g0 + FFN_TILES - 2
                hi(b + 2)
                hi(b + 3)

            ffn(0)
            norm(1)

            g0, e0 = START["att"], EV["att"]
            act.wait_ge(b_vec, 1)
            for g in range(G3):
                A(bv[0:AH, g, :], ps_a[0:AH, g, 0:384], ACT.Copy).then_inc(b_vecc, 1)
            run(g0, e0, 24, lambda n: one(aq, n), scale=HD ** -0.5)
            run(g0 + 24, e0 + 24, 24, lambda n: one(ak, n))
            values(g0 + 48, e0 + 48, 24)

            def exps(h):
                act.wait_ge(a_m, h + 1)
                s = h % 2
                if h >= 2:
                    act.wait_ge(a_t, h - 1)
                flat = ps[:, 3 * s:3 * s + 3, :].rearrange("p a b -> p (a b)")
                A(pr[:, s, 0:768], flat[:, 0:768], ACT.Exp, bias=ast[:, s, 2:3],
                  accum_out=ast[:, s, 4:5]).then_inc(act_step, 1)
                A(pr[:, s, 768:1152], flat[:, 1024:1408], ACT.Exp, bias=ast[:, s, 3:4],
                  accum_out=ast[:, s, 5:6]).then_inc(a_e, 1)
                steps[0] += 1

            def turned(h):
                s = h % 2
                act.wait_ge(a_t, h + 1)
                A(pt_s[:, 0:512], ps[:, 6, :], ACT.Copy).then_inc(a_tc, 1)
                A(pt_s[:, 512:1024], ps[:, 7, :], ACT.Copy).then_inc(a_tc, 1)
                A(pt_s[:, 1024:1152], ps[:, 3 * s, 0:P], ACT.Copy).then_inc(a_tc, 1)

            def outs(h):
                s, r = h % 2, 64 * (h % 2)
                act.wait_ge(a_o, h + 1)
                A(ao[r:r + HD, h // 2, :], ps[r:r + HD, 3 * s + 1, 0:T], ACT.Copy).then_inc(a_oc, 1)

            exps(0)
            for h in range(AH):
                turned(h)
                if h + 1 < AH:
                    exps(h + 1)
                outs(h)
            act.wait_ge(a_oc, AH)
            A(xh[:, :, :], ao, ACT.Copy).then_inc(a_hi, 1)
            run(g0 + 72, e0 + 72, 8, lambda n: one(mix, n))
            norm(2)
            ffn(1)
            norm(3)

            norm(4)
            for k in range(2):
                g0, e0 = START[f"b{k}"], EV[f"b{k}"]
                dsts = [(q2[:, j, :], ACT.Copy, {"scale": HD ** -0.5}) for j in range(4)]
                dsts += [(k2[:, j, :], ACT.Copy, {}) for j in range(4)]
                dsts += [(vT[:, j % 2, :], ACT.Copy, {}) for j in range(4)]
                dsts += [(fz[0:H2, 0, :], ACT.Identity, {"bias": vec[0:H2, V_BF + k:V_BF + k + 1], "rows": H2})]
                dsts += [(ca[:, j, :], ACT.Copy, {}) for j in range(2)]
                dsts += [(cg[:, j, :], ACT.Sigmoid, {}) for j in range(2)]
                dsts += [(xrp[:, j, 4:4 + T], ACT.Copy, {}) for j in range(2)]
                dsts += [(gg[:, j, :], ACT.Gelu_apprx_tanh, {}) for j in range(2)]
                for j, (dst, func, kw) in enumerate(dsts):
                    hi(g0 + j + 2)
                    evacuate(g0 + j, e0 + j, dst, func, **kw)
                act.wait_ge(z_abs, k + 1)
                link(A(fz[0:H2, 2, :], fz[0:H2, 1, :], ACT.Exp, scale=-1.0))
                A(fz[0:H2, 3, :], fz[0:H2, 2, :], ACT.Ln, bias=ones[0:H2, 0:1]).then_inc(z_ln, 1)
                act.wait_ge(sp_abs, k + 1)
                A(spw[:, 2, :], spw[:, 1, :], ACT.Exp, scale=-1.0).then_inc(sp_exp, 1)
                def exps2(h):
                    s = h % 2
                    act.wait_ge(a_m, AH + H2 * k + h + 1)
                    if h >= 2:
                        act.wait_ge(a_t, AH + H2 * k + h - 1)
                    A(p2[:, s, 0:256], ps[:, s, 0:256], ACT.Exp, bias=st2[:, s, 2:3],
                      accum_out=st2[:, s, 4:5]).then_inc(act_step, 1)
                    A(p2[:, s, 256:384], ps[:, s, 256:384], ACT.Exp, bias=st2[:, s, 3:4],
                      accum_out=st2[:, s, 5:6]).then_inc(a_e, 1)
                    steps[0] += 1

                exps2(0)
                exps2(1)
                for h in range(H2):
                    s, r = h % 2, 64 * (h % 2)
                    act.wait_ge(a_t, AH + H2 * k + h + 1)
                    A(p2T, ps_x[:, 0, 0:384], ACT.Copy).then_inc(a_tc, 1)
                    if h + 2 < H2:
                        exps2(h + 2)
                    act.wait_ge(a_o, AH + H2 * k + h + 1)
                    A(o2[r:r + HD, h // 2, :], ps_x[r:r + HD, 1, 0:T], ACT.Copy).then_inc(a_oc, 1)
                act.wait_ge(cv_cen, k + 1)
                A(csq, cy, ACT.Square).then_inc(cv_sq, 1)
                act.wait_ge(cv_var, k + 1)
                A(cstd[:, 0, :], ps_x[:, 1, 0:T], ACT.Sqrt, bias=vec[:, V_EPS2:V_EPS2 + 1],
                  scale=1.0 / 256).then_inc(cv_std, 1)
                act.wait_ge(cv_n, k + 1)
                for b in range(2):
                    c = 2 * k + b
                    A(o2[:, 4 + b, :], cy[:, b, :], ACT.Silu, scale=vec[:, V_CG + c:V_CG + c + 1],
                      bias=vec[:, V_CN + c:V_CN + c + 1]).then_inc(cv_o, 1)
                act.wait_ge(rg_mm, k + 1)
                for b in range(2):
                    c = 2 * k + b
                    A(rr[:, b, :], ps_a[:, 2, b * T:(b + 1) * T], ACT.Sigmoid,
                      bias=vec[:, V_BR + c:V_BR + c + 1]).then_inc(rg_sig, 1)
                    A(ri[:, b, :], ps_a[:, 3, b * T:(b + 1) * T], ACT.Sigmoid,
                      bias=vec[:, V_BI + c:V_BI + c + 1]).then_inc(rg_sig, 1)
                act.wait_ge(rg_la, k + 1)
                A(aa, la, ACT.Exp).then_inc(rg_exp, 1)
                A(th, la, ACT.Tanh, scale=-1.0).then_inc(rg_exp, 1)
                act.wait_ge(rg_m2, k + 1)
                A(mu, mu, ACT.Sqrt).then_inc(rg_mult, 1)
                act.wait_ge(rg_o, k + 1)
                act.wait_ge(cv_o, 2 * k + 2)
                act.wait_ge(a_oc, AH + H2 * (k + 1))
                A(xh[:, :, :], o2, ACT.Copy).then_inc(a_hi, 1)
                run(g0 + 21, e0 + 21, 8, lambda n: one(mix, n))
                norm(5 + 2 * k)

                run(g0 + 29, e0 + 29, 16, lambda n: one(pq, n))
                for c in range(NC_T):
                    for j in range(4):
                        act.wait_ge(p_s, 4 * (2 * k + c) + j + 1)
                        A(sc[:, 8 * c + 2 * j:8 * c + 2 * j + 2, :, :],
                          ps_a[:, j, :].rearrange("p (a b c) -> p a b c", a=2, b=2), ACT.Copy).then_inc(p_sc, 1)
                gu, eu = g0 + 45, e0 + 45
                run(gu, eu, 96, lambda n: one(hid, n), func=ACT.Gelu_apprx_tanh)
                hi(gu + 98)
                evacuate(gu + 96, eu + 96, hid[:, 96, :], ACT.Gelu_apprx_tanh)
                act.wait_ge(pick_step, 8 * PICK_STEPS * (k + 1))
                A(ge, ge, ACT.Exp).then_inc(p_exp, 1)
                for j in range(97, 100):
                    hi(gu + j + 2)
                    evacuate(gu + j, eu + j, hid[:, j, :], ACT.Gelu_apprx_tanh)
                act.wait_ge(p_t, k + 1)
                for c in range(NC_T):
                    A(pickT[:, 0:3, c * P:(c + 1) * P], ps_x[:, c, 0:384].rearrange("p (a b) -> p a b", a=3),
                      ACT.Copy).then_inc(p_tc, 1)
                run(gu + 100, eu + 100, 28, lambda n: one(hid, n + 100), func=ACT.Gelu_apprx_tanh)


                def gate_rows(t, s):
                    for j in range(4):
                        ins = A(gated[s][:, j, :], oh[s][:, j, :].bitcast(F32), ACT.Copy,
                                scale=gT[:, bass.ds(t + j, 1)])
                    ins.then_inc(g_gated, 1)

                act.wait_ge(p_tc, 2 * (k + 1))
                for n in range(4):
                    act.wait_ge(g_hot, 64 * k + n + 1)
                    gate_rows(n * 4, n)
                with act.Fori(0, 15) as i:
                    for s in range(4):
                        act.wait_ge(g_hot, i * 4 + 64 * k + 5 + s)
                        act.wait_ge(g_mm, i * 4 + 64 * k + 1 + s)
                        gate_rows(i * 16 + 16 + 4 * s, s)
                act.wait_ge(g_mul, 64 * (k + 1))
                gv, u0 = g0 + 173, PAIR[f"b{k}"]
                pair_hi(hid[:, 0:2, :], u0)
                pair_hi(hid[:, 2:4, :], u0 + 1)
                with act.Fori(0, 31) as i:
                    for j in range(4):
                        hi(gv + j + 2, i, 4)
                        if j % 2:
                            u = j // 2 + 2
                            pair_hi(hid[:, bass.ds(i * 4 + 2 * u, 2), :], u0 + u, i, 2, gv + j + 1, 4)
                for j in range(124, 128):
                    hi(gv + j + 2)
                norm(6 + 2 * k)
            for j in range(4):
                act.wait_ge(o_turned, j + 1)
                A(o_rows[:, j // 2, (j % 2) * 512:(j % 2 + 1) * 512], ps_a[:, j, :], ACT.Copy).then_inc(o_copied, 1)

        @block.vector
        def _(dve):
            V = nc.vector
            steps = [0]

            def link(ins, wait=True):
                steps[0] = steps[0] + 1
                ins.then_inc(dve_step, 1)
                if wait:
                    dve.wait_ge(dve_step, steps[0])

            def lo(b, i=None, body=0):
                if i is None and b >= TILES:
                    return
                n = 0 if i is None else i
                dve.wait_ge(w_hi, b + 1 + n * body)
                V.tensor_tensor(wl[b % 2][:, :, :], raw[:, b % 4, :].rearrange("p (a b) -> p a b", a=DB),
                                wh[b % 2][:, :, :].bitcast(F32), ALU.subtract).then_inc(w_lo, 1)

            def run(g0, count):
                with dve.Fori(0, count // 4) as i:
                    for j in range(4):
                        lo(g0 + j + 2, i, 4)

            def pair_lo(src, u, i=None, step=0):
                n = 0 if i is None else i
                dve.wait_ge(m_hi, u + 1 + n * step)
                s = 2 * (u % 2)
                V.tensor_tensor(ml[:, s:s + 2, :], src, mh[:, s:s + 2, :].bitcast(F32), ALU.subtract) \
                    .then_inc(m_lo, 1)

            def norm(k):
                kind, source, gain, bias = NORMS[k]
                if source == "acc":
                    dve.wait_ge(mm_done, acc_tiles(k))
                elif source == "mix":
                    dve.wait_ge(evac, {2: EV["att"] + 80, 5: EV["b0"] + 29, 7: EV["b1"] + 29}[k])
                if source is not None:
                    src = acc if source == "acc" else mix
                    for g in range(4):
                        b = slice(2 * g, 2 * g + 2)
                        V.scalar_tensor_tensor(out=xT[:, b, :], in0=xT[:, b, :],
                                               scalar=ALPHA if kind == "ln" else 1.0, in1=src[:, b, :],
                                               op0=ALU.mult, op1=ALU.add).then_inc(n_res, 1)
                if kind == "ln":
                    dve.wait_ge(n_mean, ln_before[k] + 1)
                    for g in range(4):
                        b = slice(2 * g, 2 * g + 2)
                        V.scalar_tensor_tensor(out=xT[:, b, :],
                                               in0=ps_x[:, 0, 0:T].unsqueeze(1).to_broadcast([P, 2, T]),
                                               scalar=-1.0 / D, in1=xT[:, b, :], op0=ALU.mult, op1=ALU.add) \
                            .then_inc(n_cen, 1)
                dve.wait_ge(n_std, k + 1)
                link(V.reciprocal(rstd, std))
                for g in range(4):
                    for b in (2 * g, 2 * g + 1):
                        ins = V.scalar_tensor_tensor(out=yn[:, b, :], in0=xT[:, b, :],
                                                     scalar=vec[:, gain + b:gain + b + 1], in1=rstd,
                                                     op0=ALU.mult, op1=ALU.mult)
                    ins.then_inc(n_y, 1)
                dve.wait_ge(n_y, 4 * (k + 1))
                y = xT if kind == "ln" else yn
                for g in range(4 if k < 8 else 0):
                    b = slice(2 * g, 2 * g + 2)
                    if kind == "ln":
                        for c in (2 * g, 2 * g + 1):
                            link(V.tensor_scalar(xT[:, c, :], yn[:, c, :], vec[:, bias + c:bias + c + 1], None,
                                                 ALU.add), wait=(c % 2 == 1))
                    dve.wait_ge(n_hi, 4 * k + g + 1)
                    V.tensor_tensor(xl[:, b, :], y[:, b, :], xh[:, b, :].bitcast(F32), ALU.subtract) \
                        .then_inc(n_lo, 1)

            lo(0)
            lo(1)
            dve.wait_ge(x_hi, 1)
            V.tensor_tensor(xl[:, :, :], xT[:, :, :], xh[:, :, :].bitcast(F32), ALU.subtract).then_inc(x_lo, 1)

            def values(g0, v0, count, dst):
                def copy(n, j, i=None):
                    dve.wait_ge(v_turned, n + 1 + (0 if i is None else i * 4))
                    m = j if i is None else i * 4 + j
                    V.tensor_copy(dst[:, :, bass.ds(m * P, P)],
                                  ps_x[:, n % 2, 0:T].rearrange("p (c n) -> p c n", c=2)).then_inc(v_copied, 1)

                for j in range(4):
                    lo(g0 + j + 2)
                    if j:
                        copy(v0 + j - 1, j - 1)
                if count > 4:
                    with dve.Fori(0, count // 4 - 1) as i:
                        for j in range(4):
                            lo(g0 + 4 + j + 2, i, 4)
                            copy(v0 + 3 + j, 3 + j, i)
                copy(v0 + count - 1, count - 1)

            run(0, 16)
            values(RET_V, 0, 16, vt)
            run(RET_G, 16)
            for b in range(8):
                dve.wait_ge(retc_in, 16)
                dve.wait_ge(evac, 16)
                dve.wait_ge(rope_mm, b + 1)
                pair = qk[:, 2 * b:2 * b + 2, :]
                cos, sin = (rc[:, c:c + 512].rearrange("p (a t) -> p a t", a=2) for c in (R_COS, R_SIN))
                t1 = rt[:, 0, :].rearrange("p (a t) -> p a t", a=2)
                t2 = rt[:, 1, :].rearrange("p (a t) -> p a t", a=2)
                link(V.tensor_tensor(t1, pair, cos, ALU.mult), wait=False)
                link(V.tensor_tensor(t2, ps_x[:, b % 2, :].rearrange("p (a t) -> p a t", a=2), sin, ALU.mult))
                V.tensor_tensor(pair, t1, t2, ALU.add).then_inc(rope_done, 1)
                dve.wait_ge(rope_done, b + 1)
            for h in range(RH):
                yh = ry[:, 4 * h:4 * h + 4, :]
                dve.wait_ge(r_s, h + 1)
                V.tensor_tensor(sd[:, h % 2, :], ps_x[:, h % 2, 0:384], rc[:, R_D + 384 * h:R_D + 384 * (h + 1)],
                                ALU.mult).then_inc(r_sd, 1)
                dve.wait_ge(r_mean, h + 1)
                V.scalar_tensor_tensor(out=yh, in0=ps_t[:, 0, 0:T].unsqueeze(1).to_broadcast([P, 4, T]),
                                       scalar=-1.0 / RV, in1=yh, op0=ALU.mult, op1=ALU.add).then_inc(r_cen, 1)
                dve.wait_ge(r_std, h + 1)
                link(V.reciprocal(rstat[:, h % 2, 1, :], rstat[:, h % 2, 0, :]))
                link(V.tensor_tensor(yh, yh, rstat[:, h % 2, 1, :].unsqueeze(1).to_broadcast([P, 4, T]), ALU.mult))
                V.tensor_tensor(yh, yh, sg[:, 4 * h:4 * h + 4, :], ALU.mult).then_inc(r_out, 1)
            pair_lo(ry[:, 0:2, :], 0)
            pair_lo(ry[:, 2:4, :], 1)
            with dve.Fori(0, 3) as i:
                for j in range(4):
                    lo(RET_O + j + 2, i, 4)
                    if j % 2:
                        u = j // 2 + 2
                        pair_lo(ry[:, bass.ds(i * 4 + 2 * u, 2), :], u, i, 2)
            for j in range(12, 16):
                lo(RET_O + j + 2)
            norm(0)

            def ffn(k):
                name = f"ffn{k}"
                g0, e0, u0 = START[name], EV[name], PAIR[name]

                def mid(u, e, i=None):
                    n = 0 if i is None else i
                    dve.wait_ge(evac, e + n * 8)
                    V.tensor_tensor(fm[:, u % 2, :], fg[:, u % 2, :], fu[:, u % 2, :], ALU.mult).then_inc(f_mid, 1)

                def rest(u, i=None):
                    pair_lo(fm[:, u % 2, :].rearrange("p (a t) -> p a t", a=2), u0 + u, i, 2)

                for j in range(4):
                    lo(g0 + j + 2)
                mid(0, e0 + 4)
                rest(0)
                with dve.Fori(0, (FU - 1) // 2) as i:
                    for v in range(2):
                        b = g0 + 4 + 6 * v
                        for j in range(5):
                            lo(b + j + 2, i, 12)
                        mid(v + 1, e0 + 8 + 4 * v, i)
                        rest(v + 1, i)
                        lo(b + 5 + 2, i, 12)
                lo(g0 + FFN_TILES)
                lo(g0 + FFN_TILES + 1)

            ffn(0)
            norm(1)

            g0, e0 = START["att"], EV["att"]
            run(g0, 48)
            values(g0 + 48, 16, 24, av)

            def softmax_max(n, s, st, views):
                dve.wait_ge(a_s, n + 1)
                for c, v in enumerate(views):
                    link(V.tensor_reduce(st[:, s, c:c + 1], v, AX, ALU.max), wait=(c == 1))
                V.tensor_scalar(st[:, s, 2:4], st[:, s, 0:2], -1.0, None, ALU.mult).then_inc(a_m, 1)

            def softmax_scale(n, s, st, probs):
                dve.wait_ge(a_e, n + 1)
                link(V.reciprocal(st[:, s, 6:8], st[:, s, 4:6]))
                link(V.tensor_scalar(probs[0], probs[0], st[:, s, 6:7], None, ALU.mult), wait=False)
                V.tensor_scalar(probs[1], probs[1], st[:, s, 7:8], None, ALU.mult).then_inc(a_p, 1)

            def att_max(h):
                s = h % 2
                flat = ps[:, 3 * s:3 * s + 3, :].rearrange("p a b -> p (a b)")
                softmax_max(h, s, ast, (flat[:, 0:768], flat[:, 1024:1408]))

            att_max(0)
            for h in range(AH):
                softmax_scale(h, h % 2, ast, (pr[:, h % 2, 0:768], pr[:, h % 2, 768:1152]))
                if h + 1 < AH:
                    att_max(h + 1)
            dve.wait_ge(a_hi, 1)
            V.tensor_tensor(xl[:, :, :], ao, xh[:, :, :].bitcast(F32), ALU.subtract).then_inc(a_lo, 1)
            run(g0 + 72, 8)
            norm(2)
            ffn(1)
            norm(3)

            norm(4)
            for k in range(2):
                g0, e0 = START[f"b{k}"], EV[f"b{k}"]
                link(V.memset(cpad[:, :, 0:32], 0.0), wait=False)
                link(V.memset(xrp[:, :, 0:4], 0.0), wait=False)
                for j in range(8):
                    lo(g0 + j + 2)
                values(g0 + 8, 40 + 4 * k, 4, v2)
                for j in range(12, 21):
                    lo(g0 + j + 2)
                dve.wait_ge(evac, e0 + 13)
                z = [fz[0:H2, j, :] for j in range(6)]
                link(V.tensor_scalar(z[4], z[0], -1.0, None, ALU.mult))
                V.tensor_tensor(z[1], z[0], z[4], ALU.max).then_inc(z_abs, 1)
                link(V.tensor_scalar(z[0], z[0], 0.0, None, ALU.min))
                dve.wait_ge(z_ln, k + 1)
                link(V.tensor_tensor(z[0], z[0], z[3], ALU.subtract))
                link(V.memset(z[2], 1.0))
                link(V.tensor_tensor_scan(z[4], z[2], z[0], 0.0, ALU.mult, ALU.add))
                V.tensor_scalar(z[5], z[4], -1.0, None, ALU.mult).then_inc(cum_done, 1)
                lam = vec[:, V_LAM + 2 * k:V_LAM + 2 * k + 2]
                link(V.tensor_scalar(spw[:, 0, :], lam, -1.0, None, ALU.mult))
                V.tensor_tensor(spw[:, 1, :], spw[:, 0, :], lam, ALU.max).then_inc(sp_abs, 1)
                dve.wait_ge(sp_exp, k + 1)
                link(V.tensor_scalar(spw[:, 3, :], spw[:, 2, :], 2.0, None, ALU.add))
                link(V.reciprocal(spw[:, 3, :], spw[:, 3, :]))
                link(V.tensor_tensor(spw[:, 3, :], spw[:, 3, :], spw[:, 2, :], ALU.mult))
                link(V.tensor_tensor(spw[:, 4, :], spw[:, 3, :], spw[:, 3, :], ALU.mult))
                link(V.memset(spw[:, 5, :], 1.0 / 19))
                for n in range(17, 0, -2):
                    link(V.tensor_tensor(spw[:, 5, :], spw[:, 5, :], spw[:, 4, :], ALU.mult))
                    link(V.tensor_scalar(spw[:, 5, :], spw[:, 5, :], 1.0 / n, None, ALU.add))
                link(V.tensor_tensor(spw[:, 5, :], spw[:, 5, :], spw[:, 3, :], ALU.mult))
                link(V.tensor_scalar(spw[:, 0, :], spw[:, 0, :], 0.0, -RG_C, ALU.max, ALU.mult))
                link(V.scalar_tensor_tensor(out=spw[:, 6, :], in0=spw[:, 5, :], scalar=-2.0 * RG_C,
                                            in1=spw[:, 0, :], op0=ALU.mult, op1=ALU.add))
                dve.wait_ge(evac, e0 + 21)
                for t in range(RK):
                    for b in range(2):
                        w = V_RW + (2 * k + b) * RK + t
                        src = xrp[:, b, t + 1:t + 1 + T]
                        if t == 0:
                            c = V_RB + 2 * k + b
                            ins = V.tensor_scalar(xc[:, b, :], src, vec[:, w:w + 1], vec[:, c:c + 1],
                                                  ALU.mult, ALU.add)
                        else:
                            ins = V.scalar_tensor_tensor(out=xc[:, b, :], in0=src, scalar=vec[:, w:w + 1],
                                                         in1=xc[:, b, :], op0=ALU.mult, op1=ALU.add)
                        if t == RK - 1 and b == 1:
                            ins.then_inc(xc_done, 1)
                        else:
                            link(ins, wait=(b == 1))
                def att2_max(h):
                    s = h % 2
                    softmax_max(AH + H2 * k + h, s, st2, (ps[:, s, 0:256], ps[:, s, 256:384]))

                att2_max(0)
                att2_max(1)
                for h in range(H2):
                    softmax_scale(AH + H2 * k + h, h % 2, st2, (p2[:, h % 2, 0:256], p2[:, h % 2, 256:384]))
                    if h + 2 < H2:
                        att2_max(h + 2)
                link(V.tensor_tensor(cpad[:, :, 32:32 + T], ca, cg, ALU.mult))
                for t in range(CK):
                    for b in range(2):
                        w = V_CW + (2 * k + b) * CK + t
                        src = cpad[:, b, t + 2:t + 2 + T]
                        if t == 0:
                            c = V_CB + 2 * k + b
                            ins = V.tensor_scalar(cy[:, b, :], src, vec[:, w:w + 1], vec[:, c:c + 1],
                                                  ALU.mult, ALU.add)
                        else:
                            ins = V.scalar_tensor_tensor(out=cy[:, b, :], in0=src, scalar=vec[:, w:w + 1],
                                                         in1=cy[:, b, :], op0=ALU.mult, op1=ALU.add)
                        if t == CK - 1 and b == 1:
                            ins.then_inc(cv_y, 1)
                        else:
                            link(ins, wait=(b == 1))
                dve.wait_ge(cv_mean, k + 1)
                V.scalar_tensor_tensor(out=cy, in0=ps_x[:, 0, 0:T].unsqueeze(1).to_broadcast([P, 2, T]),
                                       scalar=-1.0 / 256, in1=cy, op0=ALU.mult, op1=ALU.add).then_inc(cv_cen, 1)
                dve.wait_ge(cv_std, k + 1)
                link(V.reciprocal(cstd[:, 1, :], cstd[:, 0, :]))
                V.tensor_tensor(cy, cy, cstd[:, 1, :].unsqueeze(1).to_broadcast([P, 2, T]), ALU.mult) \
                    .then_inc(cv_n, 1)
                dve.wait_ge(rg_sig, 4 * (k + 1))
                link(V.tensor_tensor(la, rr, spw[:, 6, :].unsqueeze(2).to_broadcast([P, 2, T]), ALU.mult),
                     wait=False)
                V.tensor_tensor(bt, ri, xc, ALU.mult).then_inc(rg_la, 1)
                dve.wait_ge(rg_exp, 2 * (k + 1))
                link(V.tensor_scalar(mu, th, 1.0, None, ALU.add))
                link(V.reciprocal(mu, mu))
                V.scalar_tensor_tensor(out=mu, in0=th, scalar=2.0, in1=mu, op0=ALU.mult, op1=ALU.mult) \
                    .then_inc(rg_m2, 1)
                dve.wait_ge(rg_mult, k + 1)
                link(V.tensor_tensor(bt, bt, mu, ALU.mult))
                for b in range(2):
                    link(V.tensor_tensor_scan(hs[:, b, :], aa[:, b, :], bt[:, b, :], 0.0, ALU.mult, ALU.add),
                         wait=(b == 1))
                V.tensor_tensor(o2[:, 6:8, :], hs, gg, ALU.mult).then_inc(rg_o, 1)
                dve.wait_ge(a_hi, k + 2)
                V.tensor_tensor(xl[:, :, :], o2, xh[:, :, :].bitcast(F32), ALU.subtract).then_inc(a_lo, 1)
                run(g0 + 21, 8)
                norm(5 + 2 * k)

                run(g0 + 29, 16)
                gu = g0 + 45
                dve.wait_ge(p_sc, 8 * (k + 1))
                pick = [0]

                def count(ins):
                    pick[0] = pick[0] + 1
                    ins.then_inc(pick_step, 1)

                def so_far(i):
                    dve.wait_ge(pick_step, i * PICK_STEPS + (8 * PICK_STEPS * k + pick[0]))

                sides = [(a, s) for a in range(2) for s in range(2)]
                flat = cand.rearrange("p h a b -> p h (a b)")
                B4 = [P, 2, 16, 16]
                with dve.Fori(0, 8) as i:
                    def tile(j):
                        so_far(i)
                        lo(gu + j + 2, i, 12)

                    def rank_hot(s):
                        count(V.tensor_tensor(hot_out, crf[:, s, :, :].unsqueeze(3).to_broadcast(B4),
                                              iota16.unsqueeze(1).unsqueeze(1).to_broadcast(B4), ALU.is_equal))
                        so_far(i)

                    def onto_keys(s):
                        count(V.tensor_tensor(hot_out, hot, tf[:, :, s, :].unsqueeze(2).to_broadcast(B4), ALU.mult))
                        so_far(i)
                        count(V.tensor_reduce(ee[:, s, bass.ds(i * 2, 2), :], hot, AX, ALU.add))

                    count(V.tensor_copy(cur, sc[:, bass.ds(i * 2, 2), :, :]))
                    tile(0)
                    for a, s in sides:
                        count(V.max(tv[:, a, s, 0:8], cur[:, a, s, :]))
                    tile(1)
                    for a, s in sides:
                        count(V.max_index(ti[:, a, s, 0:8], tv[:, a, s, 0:8], cur[:, a, s, :]))
                    tile(2)
                    for a, s in sides:
                        count(V.match_replace(best[:, a, s, :], tv[:, a, s, 0:8], cur[:, a, s, :], LOWEST))
                    tile(3)
                    for a, s in sides:
                        count(V.max(tv[:, a, s, 8:16], best[:, a, s, :]))
                    tile(4)
                    count(V.tensor_tensor(cand, tv[:, :, 0, :].unsqueeze(3).to_broadcast(B4),
                                          tv[:, :, 1, :].unsqueeze(2).to_broadcast(B4), ALU.add))
                    for a, s in sides:
                        count(V.max_index(ti[:, a, s, 8:16], tv[:, a, s, 8:16], best[:, a, s, :]))
                    tile(5)
                    count(V.tensor_copy(tf, ti))
                    for a in range(2):
                        count(V.max(sv[:, a, 0:8], flat[:, a, :]))
                    tile(6)
                    for a in range(2):
                        count(V.max_index(ci[:, a, 0:8], sv[:, a, 0:8], flat[:, a, :]))
                        count(V.match_replace(cand2[:, a, :], sv[:, a, 0:8], flat[:, a, :], LOWEST))
                    tile(7)
                    for a in range(2):
                        count(V.max(sv[:, a, 8:16], cand2[:, a, :]))
                    tile(8)
                    for a in range(2):
                        count(V.max_index(ci[:, a, 8:16], sv[:, a, 8:16], cand2[:, a, :]))
                    count(V.tensor_tensor(ge[:, bass.ds(i * 2, 2), :], sv, sv[:, :, 0:1].to_broadcast([P, 2, 16]),
                                          ALU.subtract))
                    tile(9)
                    count(V.tensor_single_scalar(cr[:, 0, :, :], ci, 4, ALU.logical_shift_right))
                    count(V.tensor_single_scalar(cr[:, 1, :, :], ci, 15, ALU.bitwise_and))
                    so_far(i)
                    count(V.tensor_copy(crf, cr))
                    so_far(i)
                    rank_hot(0)
                    tile(10)
                    onto_keys(0)
                    tile(11)
                    rank_hot(1)
                    onto_keys(1)
                    so_far(i)
                    assert pick[0] == PICK_STEPS
                lo(gu + 98)
                lo(gu + 99)
                dve.wait_ge(p_exp, k + 1)
                link(V.tensor_reduce(gd[:, 0, :], ge, AX, ALU.add))
                link(V.reciprocal(gd[:, 1, :], gd[:, 0, :]))
                V.tensor_tensor(ge, ge, gd[:, 1, :].unsqueeze(2).to_broadcast([P, NC_T * H2, 16]), ALU.mult) \
                    .then_inc(p_e, 1)
                lo(gu + 100)
                lo(gu + 101)
                run(gu + 100, 28)
                dve.wait_ge(p_tc, 2 * (k + 1))
                dve.wait_ge(evac, e0 + 173)

                def onehots(t, s):
                    B = [P, 2, 4, P]
                    V.tensor_tensor(oh[s].rearrange("p (a b) n -> p a b n", a=2),
                                    iota.unsqueeze(1).unsqueeze(1).to_broadcast(B),
                                    pickT[:, 0:2, bass.ds(t, 4)].unsqueeze(3).to_broadcast(B),
                                    ALU.is_equal).then_inc(g_hot, 1)

                def weigh(t, s):
                    h = hid[:, :, bass.ds(t, 4)].rearrange("p m t -> p t m")
                    V.tensor_tensor(h, h, ps_a[:, s, :].rearrange("p (t m) -> p t m", t=4), ALU.mult) \
                        .then_inc(g_mul, 1)

                for n in range(4):
                    onehots(n * 4, n)
                with dve.Fori(0, 15) as i:
                    for s in range(4):
                        dve.wait_ge(g_mm, i * 4 + 64 * k + 1 + s)
                        weigh(i * 16 + 4 * s, s)
                        onehots(i * 16 + 16 + 4 * s, s)
                for s in range(4):
                    dve.wait_ge(g_mm, 64 * k + 61 + s)
                    weigh(240 + 4 * s, s)
                gv, u0 = g0 + 173, PAIR[f"b{k}"]
                pair_lo(hid[:, 0:2, :], u0)
                pair_lo(hid[:, 2:4, :], u0 + 1)
                with dve.Fori(0, 31) as i:
                    for j in range(4):
                        lo(gv + j + 2, i, 4)
                        if j % 2:
                            u = j // 2 + 2
                            pair_lo(hid[:, bass.ds(i * 4 + 2 * u, 2), :], u0 + u, i, 2)
                for j in range(124, 128):
                    lo(gv + j + 2)
                norm(6 + 2 * k)

        @block.tensor
        def _(pe):
            M = nc.tensor.matmul

            def passes(out_ap, parts_l, parts_r, first=True, last=True, skip=False):
                (lh, ll), (rh, rl) = parts_l, parts_r
                M(out_ap, lh, rh, start=first, stop=False, skip_group_check=skip)
                M(out_ap, lh, rl, start=False, stop=False, skip_group_check=skip)
                return M(out_ap, ll, rh, start=False, stop=last, skip_group_check=skip)

            def wait_tile(b, i, body):
                pe.wait_ge(w_lo, b + 1 + (0 if i is None else i * body))

            def wait_free(e, i, ebody):
                if e >= 2:
                    pe.wait_ge(evac, e - 1 + (0 if i is None else i * ebody))

            def tile_a(b, e, i=None, body=0, ebody=0):
                wait_tile(b, i, body)
                wait_free(e, i, ebody)
                for c in range(DB):
                    ins = passes(ps_t[:, e % 2, 0:T], (wh[b % 2][:, c, :], wl[b % 2][:, c, :]),
                                 (xh[:, c, :], xl[:, c, :]), c == 0, c == DB - 1)
                ins.then_inc(mm_done, 1)

            def tile_b(b, u, j, first=False, last=False, i=None, body=0, ustep=0):
                wait_tile(b, i, body)
                pe.wait_ge(m_lo, u + 1 + (0 if i is None else i * ustep))
                s = 2 * (u % 2) + j
                for c in range(DB):
                    ins = passes(acc[:, c, :], (wh[b % 2][:, c, :], wl[b % 2][:, c, :]),
                                 (mh[:, s, :], ml[:, s, :]), first and c % 2 == 0, last, skip=True)
                ins.then_inc(mm_done, 1)

            def run(tile, g0, e0, count):
                with pe.Fori(0, count // 4) as i:
                    for j in range(4):
                        tile(g0 + j, e0 + j, i, 4, 4)

            def values(g0, e0, v0, count):
                def turn(n, i=None):
                    e = e0 + n - v0
                    pe.wait_ge(evac, e + 1 + (0 if i is None else i * 4))
                    if n >= 2:
                        pe.wait_ge(v_copied, n - 1 + (0 if i is None else i * 4))
                    for c in range(NC_T):
                        ins = nc.tensor.transpose(ps_x[:, n % 2, c * P:(c + 1) * P],
                                                  vT[:, (n - v0) % 2, c * P:(c + 1) * P], ident)
                    ins.then_inc(v_turned, 1)

                for j in range(4):
                    tile_a(g0 + j, e0 + j)
                    if j:
                        turn(v0 + j - 1)
                if count > 4:
                    with pe.Fori(0, count // 4 - 1) as i:
                        for j in range(4):
                            tile_a(g0 + 4 + j, e0 + 4 + j, i, 4, 4)
                            turn(v0 + 3 + j, i)
                turn(v0 + count - 1)
                pe.wait_ge(v_copied, v0 + count)

            def norm(k):
                kind, source, gain, bias = NORMS[k]
                if kind == "ln":
                    for b in range(DB):
                        pe.wait_ge(n_res, res_before[k] + b // 2 + 1)
                        ins = M(ps_x[:, 0, 0:T], ones, xT[:, b, :], start=(b == 0), stop=(b == DB - 1))
                    ins.then_inc(n_mean, 1)
                for b in range(DB):
                    pe.wait_ge(n_sq, 4 * k + b // 2 + 1)
                    ins = M(ps_x[:, 1, 0:T], ones, sq[:, b, :], start=(b == 0), stop=(b == DB - 1))
                ins.then_inc(n_var, 1)
                if k < 8:
                    pe.wait_ge(n_lo, 4 * (k + 1))

            pe.wait_ge(const_in, 32)
            pe.wait_ge(x_in_s, 16)
            for c in range(NC_T):
                for b in range(DB):
                    ins = nc.tensor.transpose(acc[:, b, c * P:(c + 1) * P], x_rows[:, c, b * P:(b + 1) * P], ident)
            ins.then_inc(x_turned, 1)
            pe.wait_ge(x_lo, 1)

            for j in range(4):
                tile_a(j, j)
            run(tile_a, 4, 4, 12)
            values(RET_V, RET_V, 0, 16)
            run(tile_a, RET_G, RET_G, 16)
            pe.wait_ge(retc_in, 16)
            for b in range(8):
                if b >= 2:
                    pe.wait_ge(rope_done, b - 1)
                for j in range(2):
                    ins = M(ps_x[:, b % 2, j * T:(j + 1) * T], rc[:, R_ROT:R_ROT + P], qk[:, 2 * b + j, :],
                            start=True, stop=True)
                ins.then_inc(rope_mm, 1)
            pe.wait_ge(rope_done, 8)

            def ret_scores(h):
                if h >= 2:
                    pe.wait_ge(r_sd, h - 1)
                for j in range(2):
                    dst = ps_x[:, h % 2, 0:T] if j == 0 else ps_x[:, h % 2, T:T + P]
                    for b in range(2):
                        ins = M(dst, qk[:, 8 + 2 * h + b, j * P:(j + 1) * P], qk[:, 2 * h + b, j * P:T],
                                start=(b == 0), stop=(b == 1))
                ins.then_inc(r_s, 1)

            ret_scores(0)
            for h in range(RH):
                if h + 1 < RH:
                    ret_scores(h + 1)
                pe.wait_ge(r_sd, h + 1)
                if h >= 2:
                    pe.wait_ge(r_yc, h - 1)
                for b in range(4):
                    c0 = h * RV + b * P
                    dst = acc[:, 4 * (h % 2) + b, :]
                    M(dst, vt[:, 0, c0:c0 + P], sd[:, h % 2, 0:T], start=True, stop=False)
                    ins = M(dst[:, P:T], vt[:, 1, c0:c0 + P], sd[:, h % 2, T:T + P], start=False, stop=True)
                ins.then_inc(r_y, 1)
                pe.wait_ge(r_yc, h + 1)
                if h == 0:
                    pe.wait_ge(evac, EV["ffn0"])
                for b in range(4):
                    ins = M(ps_t[:, 0, 0:T], ones, ry[:, 4 * h + b, :], start=(b == 0), stop=(b == 3))
                ins.then_inc(r_mean, 1)
                pe.wait_ge(r_sq, h + 1)
                for b in range(4):
                    ins = M(ps_t[:, 1, 0:T], ones, rsq[:, b, :], start=(b == 0), stop=(b == 3))
                ins.then_inc(r_var, 1)
            tile_b(RET_O, 0, 0, first=True)
            tile_b(RET_O + 1, 0, 1)
            tile_b(RET_O + 2, 1, 0)
            tile_b(RET_O + 3, 1, 1)
            with pe.Fori(0, 3) as i:
                for j in range(4):
                    tile_b(RET_O + 4 + j, 2 + j // 2, j % 2, i=i, body=4, ustep=2)
            norm(0)

            def ffn(k):
                name = f"ffn{k}"
                g0, e0, u0 = START[name], EV[name], PAIR[name]
                for j in range(4):
                    tile_a(g0 + j, e0 + j)
                for v in range(2):
                    b = g0 + 4 + 6 * v
                    for j in range(4):
                        tile_a(b + j, e0 + 4 + 4 * v + j)
                    for j in range(2):
                        tile_b(b + 4 + j, u0 + v, j, first=(v == 0 and j == 0))
                with pe.Fori(0, (FU - 1) // 2 - 1) as i:
                    for v in range(2):
                        b = g0 + 16 + 6 * v
                        for j in range(4):
                            tile_a(b + j, e0 + 12 + 4 * v + j, i, 12, 8)
                        for j in range(2):
                            tile_b(b + 4 + j, u0 + 2 + v, j, i=i, body=12, ustep=2)
                for j in range(2):
                    tile_b(g0 + FFN_TILES - 2 + j, u0 + FU - 1, j)

            ffn(0)
            norm(1)

            g0, e0 = START["att"], EV["att"]
            pe.wait_ge(attc_in, 16)
            for g in range(G3):
                ins = M(ps_a[0:AH, g, 0:384], ac[0:33, G3 * 384 + g * AH:G3 * 384 + (g + 1) * AH],
                        ac[0:33, g * 384:(g + 1) * 384], start=True, stop=True)
            ins.then_inc(b_vec, 1)
            run(tile_a, g0, e0, 48)
            values(g0 + 48, e0 + 48, 16, 24)
            pe.wait_ge(evac, e0 + 72)
            pe.wait_ge(b_vecc, G3)

            def att_scores(h):
                s, r, hp = h % 2, 64 * (h % 2), h // 2
                pe.wait_ge(b_in[s], 16 * (h // 2 + 1))
                if h >= 2:
                    pe.wait_ge(a_oc, h - 1)
                flat = ps[:, 3 * s:3 * s + 3, :].rearrange("p a b -> p (a b)")
                for g in range(G3):
                    m = 8 * g + hp
                    for c in (1, 0):
                        w = T if c else P
                        o = g * T if c else 1024 + g * P
                        M(flat[:, o:o + w], aq[r:r + HD, m, c * P:(c + 1) * P], ak[r:r + HD, m, 0:w],
                          start=True, stop=False)
                        ins = M(flat[:, o:o + w], flip, bs[:, s, g, T - w:T], start=False, stop=True)
                ins.then_inc(a_s, 1)

            att_scores(0)
            for h in range(AH):
                s, r = h % 2, 64 * (h % 2)
                if h + 1 < AH:
                    att_scores(h + 1)
                pe.wait_ge(a_p, h + 1)
                if h:
                    pe.wait_ge(a_tc, 3 * h)
                for g in range(G3):
                    dst = ps[:, 6 + g // 2, (g % 2) * T:(g % 2) * T + T]
                    nc.tensor.transpose(dst[:, 0:P], pr[:, s, 768 + g * P:768 + (g + 1) * P], ident)
                    nc.tensor.transpose(dst[:, P:T], pr[:, s, g * T:g * T + P], ident)
                for g in range(G3):
                    dst = ps[:, 7, T + g * P:T + (g + 1) * P] if g < 2 else ps[:, 3 * s, 0:P]
                    ins = nc.tensor.transpose(dst, pr[:, s, g * T + P:(g + 1) * T], ident)
                ins.then_inc(a_t, 1)
                dst = ps[r:r + HD, 3 * s + 1, 0:T]
                for g in range(G3):
                    pe.wait_ge(a_tc, 3 * h + 1 + g // 2)
                    c0 = g * D + h * HD
                    M(dst, av[:, 0, c0:c0 + HD], pt_s[:, g * T:(g + 1) * T], start=(g == 0), stop=False)
                for g in range(G3):
                    pe.wait_ge(a_tc, 3 * h + 2 + g // 2)
                    c0, o = g * D + h * HD, 768 + g * P
                    ins = M(dst[:, P:T], av[:, 1, c0:c0 + HD], pt_s[:, o:o + P], start=False, stop=(g == 2))
                ins.then_inc(a_o, 1)
            pe.wait_ge(a_lo, 1)
            run(tile_a, g0 + 72, e0 + 72, 8)
            norm(2)
            ffn(1)
            norm(3)

            norm(4)
            for k in range(2):
                g0, e0 = START[f"b{k}"], EV[f"b{k}"]
                for j in range(8):
                    tile_a(g0 + j, e0 + j)
                values(g0 + 8, e0 + 8, 40 + 4 * k, 4)
                for j in range(12, 21):
                    tile_a(g0 + j, e0 + j)
                pe.wait_ge(xc_done, k + 1)
                pe.wait_ge(bd_in, 16 * (k + 1))
                pe.wait_ge(evac, e0 + 21)
                for m in range(2):
                    for b in range(2):
                        ins = M(ps_a[:, 2 + m, b * T:(b + 1) * T], bd[:, m, b, :], xc[:, b, :], start=True, stop=True)
                ins.then_inc(rg_mm, 1)
                pe.wait_ge(cum_done, k + 1)

                def att2_scores(h):
                    s, r, hp = h % 2, 64 * (h % 2), h // 2
                    if h >= 2:
                        pe.wait_ge(a_e, AH + H2 * k + h - 1)
                    one_h = ident[0:H2, h:h + 1]
                    for c in (1, 0):
                        w = T if c else P
                        o = 0 if c else T
                        dst = ps[:, s, o:o + w]
                        M(dst, q2[r:r + HD, hp, c * P:(c + 1) * P], k2[r:r + HD, hp, 0:w], start=True, stop=False)
                        M(dst, fz[0:H2, 4, c * P:(c + 1) * P], one_h.to_broadcast([H2, w]), start=False, stop=False)
                        M(dst, one_h.to_broadcast([H2, P]), fz[0:H2, 5, 0:w], start=False, stop=False)
                        ins = M(dst[:, w - P:w], ident, tri, start=False, stop=True)
                    ins.then_inc(a_s, 1)

                att2_scores(0)
                att2_scores(1)
                for h in range(H2):
                    s, r = h % 2, 64 * (h % 2)
                    n = AH + H2 * k + h
                    pe.wait_ge(a_p, n + 1)
                    if h:
                        pe.wait_ge(a_tc, 3 * AH + H2 * k + h)
                    nc.tensor.transpose(ps_x[:, 0, 0:P], p2[:, s, T:T + P], ident)
                    nc.tensor.transpose(ps_x[:, 0, P:T], p2[:, s, 0:P], ident)
                    nc.tensor.transpose(ps_x[:, 0, T:T + P], p2[:, s, P:T], ident).then_inc(a_t, 1)
                    if h + 2 < H2:
                        att2_scores(h + 2)
                    pe.wait_ge(a_tc, 3 * AH + H2 * k + h + 1)
                    if h:
                        pe.wait_ge(a_oc, n)
                    dst = ps_x[r:r + HD, 1, 0:T]
                    M(dst, v2[:, 0, h * HD:(h + 1) * HD], p2T[:, 0:T], start=True, stop=False)
                    M(dst[:, P:T], v2[:, 1, h * HD:(h + 1) * HD], p2T[:, T:T + P], start=False, stop=True) \
                        .then_inc(a_o, 1)
                pe.wait_ge(cv_y, k + 1)
                pe.wait_ge(a_oc, AH + H2 * (k + 1))
                for b in range(2):
                    ins = M(ps_x[:, 0, 0:T], ones, cy[:, b, :], start=(b == 0), stop=(b == 1))
                ins.then_inc(cv_mean, 1)
                pe.wait_ge(cv_sq, k + 1)
                for b in range(2):
                    ins = M(ps_x[:, 1, 0:T], ones, csq[:, b, :], start=(b == 0), stop=(b == 1))
                ins.then_inc(cv_var, 1)
                pe.wait_ge(a_lo, k + 2)
                run(tile_a, g0 + 21, e0 + 21, 8)
                norm(5 + 2 * k)

                run(tile_a, g0 + 29, e0 + 29, 16)
                pe.wait_ge(evac, e0 + 45)
                pe.wait_ge(k_in, 16 * (k + 1))
                for c in range(NC_T):
                    n = 2 * k + c
                    for j in range(4):
                        if c:
                            pe.wait_ge(p_sc, 4 * n + j - 3)
                        for h in (2 * j, 2 * j + 1):
                            for s in range(2):
                                o = (h % 2) * 256 + s * P
                                ins = M(ps_a[:, j, o:o + P], pq[:, 2 * h + s, c * P:(c + 1) * P],
                                        pk[:, s, h, :], start=True, stop=True)
                        ins.then_inc(p_s, 1)
                run(tile_a, g0 + 45, e0 + 45, 96)
                for j in range(96, 100):
                    tile_a(g0 + 45 + j, e0 + 45 + j)
                pe.wait_ge(p_e, k + 1)
                for c in range(NC_T):
                    for m, src in enumerate((ee[:, 0, :, :], ee[:, 1, :, :], ge)):
                        ins = nc.tensor.transpose(ps_x[:, c, m * P:(m + 1) * P],
                                                  src[:, 8 * c:8 * c + 8, :].rearrange("p h j -> p (h j)"), ident)
                ins.then_inc(p_t, 1)
                run(tile_a, g0 + 145, e0 + 145, 28)

                def gates(s):
                    for j in range(4):
                        ins = M(ps_a[:, s, j * P:(j + 1) * P], gated[s][:, j, :], oh[s][:, 4 + j, :].bitcast(F32),
                                start=True, stop=True)
                    ins.then_inc(g_mm, 1)

                pe.wait_ge(p_tc, 2 * (k + 1))
                for s in range(4):
                    pe.wait_ge(g_gated, 64 * k + s + 1)
                    gates(s)
                with pe.Fori(0, 15) as i:
                    for s in range(4):
                        pe.wait_ge(g_gated, i * 4 + 64 * k + 5 + s)
                        pe.wait_ge(g_mul, i * 4 + 64 * k + 1 + s)
                        gates(s)
                pe.wait_ge(g_mul, 64 * (k + 1))
                gv, u0 = g0 + 173, PAIR[f"b{k}"]
                for j in range(4):
                    tile_b(gv + j, u0 + j // 2, j % 2, first=(j == 0))
                with pe.Fori(0, 31) as i:
                    for j in range(4):
                        tile_b(gv + 4 + j, u0 + 2 + j // 2, j % 2, i=i, body=4, ustep=2)
                norm(6 + 2 * k)
            for c in range(NC_T):
                for b in range(DB):
                    pe.wait_ge(n_y, 32 + b // 2 + 1)
                    ins = nc.tensor.transpose(ps_a[:, 2 * c + b // 4, (b % 4) * P:(b % 4 + 1) * P],
                                              yn[:, b, c * P:(c + 1) * P], ident)
                    if b % 4 == 3:
                        ins.then_inc(o_turned, 1)


def constants():
    c = np.zeros((P, NCONST), np.float32)
    p = np.arange(P)
    c[:, C_ID:C_ID + P] = np.eye(P)
    c[:, C_ONE:C_ONE + P] = 1.0
    c[:, C_J:C_J + P] = np.eye(P)[::-1]
    c[:, C_MASK:C_MASK + P] = np.where(p[None, :] > p[:, None], MASKED, 0.0)
    c[:, C_IOTA:C_IOTA + P] = p
    c[:, C_I16:C_I16 + 16] = np.arange(16)
    return c


def retention_constants():
    c = np.zeros((P, NRET), np.float32)
    e, p, t = np.arange(0, P, 2), np.arange(P), np.arange(T)
    c[e + 1, R_ROT + e] = -1.0
    c[e, R_ROT + e + 1] = 1.0
    inv = np.float32(1.0) / (np.float32(10000.0) ** np.linspace(0.0, 1.0, RQ // 2, dtype=np.float32))
    ang = (t.astype(np.float32)[None, :] * inv[:, None]).astype(np.float32).astype(np.float64)
    pair = ((np.arange(2)[None, :] * P + p[:, None]) // 2)
    c[:, R_COS:R_COS + 512] = np.cos(ang)[pair].reshape(P, 512)
    c[:, R_SIN:R_SIN + 512] = np.sin(ang)[pair].reshape(P, 512)
    diff = np.concatenate([t, np.arange(P)])[None, :] - p[:, None]
    for h in range(RH):
        g = np.log1p(-(2.0 ** (-5.0 - h)))
        d = np.where(diff >= 0, np.exp(np.maximum(diff, 0) * g), 0.0) * RQ ** -0.5
        c[:, R_D + 384 * h:R_D + 384 * (h + 1)] = d
    return c


def bias_one_hots():
    c = np.zeros((33, G3, 384), np.float32)
    x = np.arange(384)
    delta = 255 - x
    half = BUCKETS // 2
    d = np.maximum(delta, 1).astype(np.float32)
    large = half + (np.log(d / half) / np.float32(np.log(MAXD / half)) * half).astype(np.int32)
    bucket = np.where(delta < half, delta, np.minimum(large, BUCKETS - 1))
    for g, (window, dil) in enumerate(PAIRS):
        ok = (delta >= 0) & (delta % dil == 0) & (delta // dil <= window // dil)
        c[bucket[ok], g, x[ok]] = 1.0
        c[32, g, ~ok] = MASKED
    return c.reshape(33, G3 * 384)


def kernel(**inputs):
    import concourse.bacc as bacc
    from concourse.bass_utils import run_bass_kernel_spmd

    a = {k: np.asarray(v) for k, v in inputs.items()}

    def cols(w):
        return w.reshape(DB, P, -1, P).transpose(2, 1, 0, 3).reshape(-1, P, TILE)

    stream = np.empty((TILES, P, TILE), np.float32)
    at = [0]

    def put(tiles):
        stream[at[0]:at[0] + len(tiles)] = tiles
        at[0] += len(tiles)

    def put_ffn(k):
        up = cols(a["ffn_w_up"][k])
        down = a["ffn_w_down"][k].reshape(-1, P, TILE)
        for u in range(FU + 1):
            if u < FU:
                put(up[2 * u:2 * u + 2])
                put(up[FF // P + 2 * u:FF // P + 2 * u + 2])
            if u:
                put(down[2 * u - 2:2 * u])

    w = a["ret_w_in"][0]
    put(cols(w))
    put(a["ret_w_out"][0].reshape(-1, P, TILE))
    put_ffn(0)
    put(cols(a["attn_w_in"][0]))
    put(cols(a["attn_w_out"][0]))
    put_ffn(1)
    for k in range(2):
        w = a["w_in_2"][k]
        put(cols(w[:, 0:1536]))
        forget = np.zeros((D, P), np.float32)
        forget[:, 0:H2] = w[:, 1536:1536 + H2]
        put(cols(forget))
        put(cols(w[:, 1536 + H2:]))
        put(cols(a["w_out_2"][k]))
        put(cols(a["peer_wq_2"][k]))
        put(a["peer_u_2"][k].reshape(NK, NK, DB, P).transpose(1, 3, 2, 0).reshape(NK, P, TILE))
        put(a["peer_v_2"][k].reshape(NK, NK, TILE).transpose(1, 0, 2))
    assert at[0] == TILES

    def blocks(v):
        return v.reshape(-1, P).T

    vecs = np.zeros((P, NVEC), np.float32)
    for c, v in ((V_LNG, a["ln_gain"]), (V_LNB, a["ln_bias"]), (V_N1, a["norm1_g_2"]), (V_N2, a["norm2_g_2"]),
                 (V_FIN, a["final_g_2"]), (V_CB, a["conv_dw_b_2"]), (V_CG, a["conv_ln_g_2"]),
                 (V_CN, a["conv_ln_b_2"]), (V_RB, a["rg_conv_b_2"]), (V_BR, a["rg_b_r_2"]),
                 (V_BI, a["rg_b_i_2"]), (V_LAM, a["rg_lambda_2"])):
        m = blocks(v)
        vecs[:, c:c + m.shape[1]] = m
    for c, v in ((V_CW, a["conv_dw_w_2"]), (V_RW, a["rg_conv_w_2"])):
        taps = v.shape[1]
        vecs[:, c:c + 4 * taps] = v.reshape(2, taps, 2, P).transpose(3, 0, 2, 1).reshape(P, 4 * taps)
    vecs[0:H2, V_BF:V_BF + 2] = a["b_forget_2"].T
    vecs[:, V_EPS1], vecs[:, V_EPS2] = LN_EPS, EPS2

    rg_w = np.zeros((2, P, 2, 2, P), np.float32)
    for m, name in enumerate(("rg_w_r_2", "rg_w_i_2")):
        for h in range(4):
            r = slice(64 * (h % 2), 64 * (h % 2) + 64)
            rg_w[:, r, m, h // 2, r] = a[name][:, h]
    keys = np.stack([a["peer_k1_2"], a["peer_k2_2"]], 1).transpose(0, 4, 1, 2, 3)
    att_c = np.zeros((33, NATT), np.float32)
    att_c[:, 0:G3 * 384] = bias_one_hots()
    att_c[0:32, G3 * 384:] = a["rel_bias"].T
    att_c[32, G3 * 384:] = 1.0

    arrays = {"stream": stream, "x": a["x"].reshape(T, D), "consts": constants(), "ret_c": retention_constants(),
              "att_c": att_c, "vecs": vecs, "rg_w": rg_w, "keys": keys}
    arrays = {k: np.ascontiguousarray(v, np.float32) for k, v in arrays.items()}
    nc = bacc.Bacc("TRN2", target_bir_lowering=False, num_devices=1)
    args = {k: nc.dram_tensor(k + "_dram", v.shape, F32, kind="ExternalInput").ap() for k, v in arrays.items()}
    scratch = nc.dram_tensor("bias_scratch", (G3, AH, 384), F32, kind="Internal").ap()
    out = nc.dram_tensor("out_dram", (T, D), F32, kind="ExternalOutput").ap()
    build(nc, args["stream"], args["x"], args["consts"], args["ret_c"], args["att_c"], args["vecs"],
          args["rg_w"], args["keys"], scratch, out)
    r = run_bass_kernel_spmd(nc, [{k + "_dram": v for k, v in arrays.items()}], core_ids=[0])
    return r.results[0]["out_dram"].reshape(1, T, D)
```

```python
from contextlib import ExitStack

import numpy as np

import concourse.bass as bass
from concourse import mybir

F32 = mybir.dt.float32
F32R = mybir.dt.float32r
U32 = mybir.dt.uint32
ACT = mybir.ActivationFunctionType
ALU = mybir.AluOpType
AX = mybir.AxisListType.X

P = 128
T = 256
D = 1024
DB = D // P
TILE = 1024
NC_T = T // P

RH, RQ, RV = 4, 256, 512
RVB = RH * RV // P
FF = 2816
FU = FF // P // 2
G3, AH, HD = 3, 16, 64
PAIRS = ((128, 1), (512, 4), (2048, 16))
BUCKETS, MAXD = 32, 2048
ALPHA = 4 ** 0.25
LN_EPS = 1e-5
H2 = 8
CK, RK = 31, 4
NK, TOPK = 128, 16
EPS2 = 1e-6
RG_C = 8.0
PICK_STEPS = 43
MASKED = -1e30
LOWEST = -3.0e38

RET0 = 0
RET_V, RET_G, RET_O = 16, 32, 48
FFN_TILES = 6 * FU
ATT_TILES = 80
B2_TILES = 21 + 8 + 16 + 128 + 128
START = {"ret": 0, "ffn0": 64, "att": 64 + FFN_TILES, "ffn1": 64 + FFN_TILES + ATT_TILES}
START["b0"] = START["ffn1"] + FFN_TILES
START["b1"] = START["b0"] + B2_TILES
TILES = START["b1"] + B2_TILES
EV = {"ret": 0, "ffn0": 48, "att": 48 + 4 * FU, "ffn1": 48 + 4 * FU + 80}
EV["b0"] = EV["ffn1"] + 4 * FU
EV["b1"] = EV["b0"] + 173
PAIR = {"ret": 0, "ffn0": 8, "ffn1": 8 + FU, "b0": 8 + 2 * FU, "b1": 8 + 2 * FU + 64}

C_ID, C_ONE, C_J, C_MASK, C_IOTA, C_I16 = 0, 128, 256, 384, 512, 640
NCONST = 656
R_ROT, R_COS, R_SIN, R_D = 0, 128, 640, 1152
NRET = 1152 + RH * 384
NATT = G3 * 384 + G3 * AH

V_LNG, V_LNB, V_N1, V_N2, V_FIN = 0, 32, 64, 80, 96
V_CW, V_CB, V_CG, V_CN, V_RW, V_RB, V_BR, V_BI, V_LAM, V_BF, V_EPS1, V_EPS2 = \
    104, 228, 232, 236, 240, 256, 260, 264, 268, 272, 274, 275
NVEC = 276


def build(nc, stream, x_in, consts, ret_c, att_c, vecs, rg_w, keys, scratch, out):
    with ExitStack() as ctx:
        def sb(name, cols, dt=F32):
            return ctx.enter_context(nc.sbuf_tensor(name, [P, *cols], dt))

        def sem(name):
            return ctx.enter_context(nc.semaphore(name))

        arena = sb("arena", [32768])
        xT = sb("xT", [DB, T])
        xh, xl = sb("xh", [DB, T], F32R), sb("xl", [DB, T], F32R)
        raw = sb("raw", [4, TILE])
        wh = [sb(f"wh{i}", [DB, P], F32R) for i in range(2)]
        wl = [sb(f"wl{i}", [DB, P], F32R) for i in range(2)]
        mh, ml = sb("mh", [4, T], F32R), sb("ml", [4, T], F32R)
        cst = sb("cst", [NCONST])
        vec = sb("vec", [NVEC])
        pickT = sb("pickT", [3, T])
        picks = sb("picks", [2240])
        unused = picks[:, 2239:2240]
        ps = ctx.enter_context(nc.psum_tensor("ps", [P, 8, 512], F32))
        ps_a, ps_t, ps_x = ps[:, 0:4, :], ps[:, 4:6, :], ps[:, 6:8, :]
        acc = ps_a.rearrange("p a (b t) -> p (a b) t", b=2)

        def ar(off, *shape):
            n = int(np.prod(shape))
            v = arena[:, off:off + n]
            if len(shape) == 2:
                v = v.rearrange("p (a b) -> p a b", a=shape[0])
            elif len(shape) == 3:
                v = v.rearrange("p (a b c) -> p a b c", a=shape[0], b=shape[1])
            elif len(shape) == 4:
                v = v.rearrange("p (a b c d) -> p a b c d", a=shape[0], b=shape[1], c=shape[2])
            return v

        ident, ones = cst[:, C_ID:C_ID + P], cst[:, C_ONE:C_ONE + P]
        flip, tri = cst[:, C_J:C_J + P], cst[:, C_MASK:C_MASK + P]
        iota, iota16 = cst[:, C_IOTA:C_IOTA + P], cst[:, C_I16:C_I16 + 16]

        mix, sq, yn = ar(0, DB, T), ar(2048, DB, T), ar(4096, DB, T)
        pair_x, pair_sq = ar(4096, 4, T), ar(5120, 4, T)
        std, rstd = ar(6144, T), ar(6400, T)
        vT = ar(7168, 2, T)
        x_rows = ar(8192, NC_T, D)
        rc = ar(8192, NRET)
        qk, vt, sg = ar(12288, 16, T), ar(16384, NC_T, RH * RV), ar(20480, RVB, T)
        ry, rt = ar(24576, RVB, T), ar(28672, 2, 512)
        sd, rsq = ar(29696, 2, 384), ar(30720, 4, T)
        rstat = ar(10880, 2, 2, T)
        fg, fu, fm = ar(8192, 2, 512), ar(9216, 2, 512), ar(10240, 2, 512)
        aq, ak, av = ar(8192, 24, T), ar(14336, 24, T), ar(20480, NC_T, G3 * D)
        ac = ar(26624, NATT)
        bv = ar(27904, G3, 384)
        bs = ar(2112, 2, G3, T)
        pr = ar(29056, 2, 1152)
        pt_s = ar(31360, 1152)
        ao = ar(0, DB, T)
        ast = ar(2048, 2, 8)
        q2, k2, v2 = ar(8192, 4, T), ar(9216, 4, T), ar(10240, NC_T, 512)
        fz = ar(11264, 6, T)
        ca, cg = ar(12800, 2, T), ar(13312, 2, T)
        cpad, cy = ar(13824, 2, T + 32), ar(14400, 2, T)
        xrp, xc = ar(14912, 2, T + 4), ar(15440, 2, T)
        gg, rr, ri = ar(15952, 2, T), ar(16464, 2, T), ar(16976, 2, T)
        la, aa, th, mu, bt, hs = (ar(17488 + 512 * i, 2, T) for i in range(6))
        csq, cstd = ar(20560, 2, T), ar(21072, 2, T)
        spw = ar(21584, 8, 2)
        bd = ar(21632, 2, 2, P)
        p2, p2T, o2 = ar(22144, 2, 384), ar(22912, 384), ar(23296, DB, T)
        st2 = ar(25344, 2, 8)
        pq, pk = ar(8192, 16, T), ar(12288, 2, H2, P)
        sc = ar(28672, NC_T * H2, 2, P)
        def pick_part(off, *shape):
            n = int(np.prod(shape))
            names = " ".join("abcd"[:len(shape)])
            return picks[:, off:off + n].rearrange(f"p ({names}) -> p {names}",
                                                   **dict(zip("abcd", shape)))

        cur, best = pick_part(1152, 2, 2, P), pick_part(1664, 2, 2, P)
        cand, cand2 = pick_part(1152, 2, 16, 16), pick_part(1664, 2, 256)
        hot = mh[:, 0:2, :].rearrange("p h (a b) -> p h a b", a=16)
        hot_out, hot = hot, hot.bitcast(F32)
        ee, ge = pick_part(0, 2, NC_T * H2, 16), pick_part(512, NC_T * H2, 16)
        tv, tf, ti = pick_part(768, 2, 2, 16), pick_part(832, 2, 2, 16), pick_part(896, 2, 2, 16).bitcast(U32)
        sv, ci = pick_part(960, 2, 16), pick_part(992, 2, 16).bitcast(U32)
        cr, crf = pick_part(1024, 2, 2, 16).bitcast(U32), pick_part(1088, 2, 2, 16)
        gd = pick_part(2176, 2, NC_T * H2)
        e1T, e2T, gT = (pickT[:, m, :] for m in range(3))
        oh = [t[:, 4 * n:4 * n + 4, :].rearrange("p a (b n) -> p (a b) n", b=2) for t in (xh, xl) for n in range(2)]
        gated = [pick_part(512 * n, 4, P) for n in range(4)]
        hid = ar(0, NK, T)
        o_rows = ar(8192, NC_T, D)

        raw_ready = [sem(f"raw_ready{i}") for i in range(4)]
        w_hi, w_lo, mm_done, evac = sem("w_hi"), sem("w_lo"), sem("mm_done"), sem("evac")
        m_hi, m_lo = sem("m_hi"), sem("m_lo")
        const_in, x_in_s, retc_in, attc_in = sem("const_in"), sem("x_in"), sem("retc_in"), sem("attc_in")
        x_turned, x_copied, x_hi, x_lo = sem("x_turned"), sem("x_copied"), sem("x_hi"), sem("x_lo")
        v_turned, v_copied = sem("values_turned"), sem("values_copied")
        dve_step, act_step = sem("dve_step"), sem("act_step")
        n_res, n_px, n_mean, n_cen, n_sq, n_psq, n_var, n_std, n_y, n_hi, n_lo = (
            sem(f"norm_{s}") for s in "residual pairs mean centred squares square_pairs variance std scaled "
            "hi lo".split())
        rope_mm, rope_done = sem("rope_mm"), sem("rope_done")
        r_s, r_sd, r_y, r_yc, r_mean, r_cen, r_sq, r_var, r_std, r_out = (
            sem(f"ret_{s}") for s in "scores decayed y y_copied mean centred squares var std out".split())
        f_mid = sem("ffn_mid")
        b_vec, b_vecc, b_store = sem("bias_vec"), sem("bias_vec_copied"), sem("bias_stored")
        b_in = [sem("bias_in0"), sem("bias_in1")]
        a_s1, a_s, a_b, a_m1, a_m, a_e, a_p, a_t, a_tc, a_o, a_oc, a_hi, a_lo = (
            sem(f"att_{s}") for s in "scores1 scores biased max1 max exp probs turned turned_copied out out_copied hi lo".split())
        z_done, cum_done = sem("forget_z"), sem("forget_cum")
        z_abs, z_ln = sem("forget_abs"), sem("forget_ln")
        cv_y, cv_mean, cv_cen, cv_sq, cv_var, cv_std, cv_n, cv_o = (
            sem(f"conv_{s}") for s in "y mean centred squares var std normed out".split())
        bd_in, xc_done, rg_mm, rg_sig, rg_la, rg_exp, rg_m2, rg_mult, rg_o = (
            sem(s) for s in "bd_in rnn_x rnn_mm rnn_sigmoid rnn_log_a rnn_exp rnn_m2 rnn_mult rnn_out".split())
        sp_abs, sp_exp, sp_done = sem("rate_abs"), sem("rate_exp"), sem("rate_done")
        k_in, p_s, p_sc, pick_step, p_exp, p_e, p_t, p_tc = (
            sem(s) for s in "keys_in peer_scores peer_scores_copied peer_pick_step peer_exp "
            "peer_picked peer_turned peer_turned_copied".split())
        g_hot, g_gated = sem("peer_onehots"), sem("peer_gated_rows")
        g_mm, g_mul = sem("peer_gates"), sem("peer_weighted")
        o_turned, o_copied, o_stored = sem("out_turned"), sem("out_copied"), sem("out_stored")

        block = ctx.enter_context(nc.Block())

        NORMS = [("ln", "acc", V_LNG, V_LNB), ("ln", "acc", V_LNG + 8, V_LNB + 8),
                 ("ln", "mix", V_LNG + 16, V_LNB + 16), ("ln", "acc", V_LNG + 24, V_LNB + 24),
                 ("rms", None, V_N1, None), ("rms", "mix", V_N2, None),
                 ("rms", "acc", V_N1 + 8, None), ("rms", "mix", V_N2 + 8, None),
                 ("rms", "acc", V_FIN, None)]
        res_before = [4 * sum(s is not None for _, s, _, _ in NORMS[:k]) for k in range(10)]
        split_before = [4 * sum(j not in (3, 8) for j in range(k)) for k in range(10)]
        ln_before = [sum(m == "ln" for m, *_ in NORMS[:k]) for k in range(10)]

        def acc_tiles(k):
            return [START["ffn0"], START["att"], START["ffn1"], START["b0"], 0,
                    START["b0"] + 29, START["b1"], START["b1"] + 29, TILES][k]

        @block.sync
        def _(sp):
            def load(slot, g):
                sp.dma_start(raw[:, slot, :], stream[bass.ds(g, 1), :, :].rearrange("a p n -> p (a n)")) \
                    .then_inc(raw_ready[slot], 16)

            for g in range(4):
                load(g, g)
            with sp.Fori(1, TILES // 4) as i:
                for s in range(4):
                    sp.wait_ge(w_lo, i * 4 + (s - 3))
                    load(s, i * 4 + s)
            for g in range(TILES // 4 * 4, TILES):
                sp.wait_ge(w_lo, g - 3)
                load(g % 4, g)

        @block.gpsimd
        def _(pool):
            pool.dma_start(cst[:, :], consts).then_inc(const_in, 16)
            pool.dma_start(vec[:, :], vecs).then_inc(const_in, 16)
            pool.dma_start(x_rows, x_in.rearrange("(c p) d -> p c d", p=P)).then_inc(x_in_s, 16)
            pool.wait_ge(x_turned, 1)
            pool.dma_start(rc, ret_c).then_inc(retc_in, 16)
            pool.wait_ge(n_lo, split_before[2])
            pool.dma_start(ac[0:33, :], att_c).then_inc(attc_in, 16)
            pool.wait_ge(b_vecc, G3)
            pool.dma_start(scratch.rearrange("g h x -> h g x"), bv[0:AH, :, :]).then_inc(b_store, 16)
            pool.wait_ge(b_store, 16)
            for h in range(AH):
                if h >= 2:
                    pool.wait_ge(a_b, h - 1)
                pool.dma_start(bs[:, h % 2, :, :], bass.AP(
                    scratch.tensor, h * 384, [[1, P], [AH * 384, G3], [1, T]])).then_inc(b_in[h % 2], 16)

            for k in range(2):
                pool.wait_ge(n_lo, split_before[5 + 2 * k])
                pool.dma_start(bd, rg_w[k]).then_inc(bd_in, 16)
                pool.wait_ge(n_lo, split_before[6 + 2 * k])
                pool.dma_start(pk, keys[k]).then_inc(k_in, 16)
            pool.wait_ge(o_copied, 4)
            pool.dma_start(out.rearrange("(c p) d -> p c d", p=P), o_rows).then_inc(o_stored, 16)
            pool.wait_ge(o_stored, 16)

        @block.scalar
        def _(act):
            A = nc.scalar.activation
            steps = [0]

            def link(ins):
                steps[0] = steps[0] + 1
                ins.then_inc(act_step, 1)
                act.wait_ge(act_step, steps[0])

            def hi(b, i=None, body=0):
                if i is None and b >= TILES:
                    return
                n = 0 if i is None else i
                act.wait_ge(raw_ready[b % 4], 16 * (b // 4 + 1) + n * (4 * body))
                if b >= 2:
                    act.wait_ge(mm_done, (b - 1) + n * body)
                A(wh[b % 2][:, :, :], raw[:, b % 4, :].rearrange("p (a b) -> p a b", a=DB), ACT.Copy) \
                    .then_inc(w_hi, 1)

            def evacuate(g, e, dst, func=ACT.Copy, i=None, body=0, ebody=0, scale=1.0, bias=None,
                         src=None, rows=P, back=False):
                n = 0 if i is None else i
                act.wait_ge(mm_done, g + 1 + n * body)
                src = ps_t[0:rows, e % 2, 0:T] if src is None else src
                if back:
                    src = src.rearrange("p (c t) -> p c t", c=NC_T)[:, :, ::-1]
                    dst = dst.rearrange("p (c t) -> p c t", c=NC_T)
                kw = {} if bias is None else {"bias": bias}
                A(dst, src, func, scale=scale, **kw).then_inc(evac, 1)

            def run(g0, e0, count, dst, **kw):
                func = kw.get("func", ACT.Copy)
                with act.Fori(0, count // 4) as i:
                    if func != ACT.Copy:
                        A(unused, ones[:, 0:1], func)
                    for j in range(4):
                        hi(g0 + j + 2, i, 4)
                        evacuate(g0 + j, e0 + j, dst(i * 4 + j), i=i, body=4, **kw)

            def values(g0, e0, count):
                with act.Fori(0, count // 4) as i:
                    for j in range(4):
                        hi(g0 + j + 2, i, 4)
                        evacuate(g0 + j, e0 + j, vT[:, j % 2, :], i=i, body=4)

            def one(ap, n):
                return ap[:, bass.ds(n, 1), :].rearrange("p a b -> p (a b)")

            def pair_hi(src, u, i=None, step=0, tile=0, body=0):
                n = 0 if i is None else i
                if tile:
                    act.wait_ge(mm_done, tile + n * body)
                s = 2 * (u % 2)
                A(mh[:, s:s + 2, :], src, ACT.Copy).then_inc(m_hi, 1)

            def norm(k):
                kind, _, gain, bias = NORMS[k]
                N = D
                for g in range(4):
                    if kind == "ln":
                        act.wait_ge(n_cen, 4 * ln_before[k] + g + 1)
                    elif NORMS[k][1] is not None:
                        act.wait_ge(n_res, res_before[k] + g + 1)
                    else:
                        act.wait_ge(n_y, 4 * k)
                    A(sq[:, 2 * g:2 * g + 2, :], xT[:, 2 * g:2 * g + 2, :], ACT.Square).then_inc(n_sq, 1)
                A(unused, ones[:, 0:1], ACT.Sqrt)
                act.wait_ge(n_var, k + 1)
                eps = V_EPS1 if kind == "ln" else V_EPS2
                A(std, ps_x[:, 1, 0:T], ACT.Sqrt, bias=vec[:, eps:eps + 1], scale=1.0 / N).then_inc(n_std, 1)
                for g in range(4 if k not in (3, 8) else 0):
                    act.wait_ge(n_y, 4 * k + g + 1)
                    if kind == "ln":
                        for b in (2 * g, 2 * g + 1):
                            ins = A(xh[:, b, :], yn[:, b, :], ACT.Identity, bias=vec[:, bias + b:bias + b + 1])
                    else:
                        ins = A(xh[:, 2 * g:2 * g + 2, :], yn[:, 2 * g:2 * g + 2, :], ACT.Copy)
                    ins.then_inc(n_hi, 1)

            act.wait_ge(const_in, 32)
            hi(0)
            hi(1)
            act.wait_ge(x_turned, 1)
            for g in range(4):
                A(xT[:, 2 * g:2 * g + 2, :], acc[:, 2 * g:2 * g + 2, :], ACT.Copy).then_inc(x_copied, 1)
            act.wait_ge(x_copied, 4)
            A(xh[:, :, :], xT[:, :, :], ACT.Copy).then_inc(x_hi, 1)

            run(0, 0, 16, lambda n: one(qk, n))
            values(RET_V, RET_V, 16)
            run(RET_G, RET_G, 16, lambda n: one(sg, n), func=ACT.Silu)
            def ret_copy(h):
                act.wait_ge(r_y, h + 1)
                b0 = 4 * (h % 2)
                A(ry[:, 4 * h:4 * h + 4, :], acc[:, b0:b0 + 4, :], ACT.Copy).then_inc(r_yc, 1)

            ret_copy(0)
            ret_copy(1)
            for h in range(RH):
                act.wait_ge(r_cen, h + 1)
                A(rsq, ry[:, 4 * h:4 * h + 4, :], ACT.Square).then_inc(r_sq, 1)
                if h + 2 < RH:
                    ret_copy(h + 2)
                act.wait_ge(r_var, h + 1)
                A(rstat[:, h % 2, 0, :], ps_t[:, 1, 0:T], ACT.Sqrt, bias=vec[:, V_EPS1:V_EPS1 + 1],
                  scale=1.0 / RV).then_inc(r_std, 1)
            act.wait_ge(r_out, 1)
            pair_hi(ry[:, 0:2, :], 0)
            pair_hi(ry[:, 2:4, :], 1)
            act.wait_ge(r_out, RH)
            with act.Fori(0, 3) as i:
                for j in range(4):
                    hi(RET_O + j + 2, i, 4)
                    if j % 2:
                        u = j // 2 + 2
                        pair_hi(ry[:, bass.ds(i * 4 + 2 * u, 2), :], u, i, 2, RET_O + j + 1, 4)
            for j in range(12, 16):
                hi(RET_O + j + 2)
            norm(0)

            def ffn(k):
                name = f"ffn{k}"
                g0, e0, u0 = START[name], EV[name], PAIR[name]

                def a_tiles(g, e, u, i=None):
                    for j in range(4):
                        hi(g + j + 2, i, 12)
                        dst = (fg if j < 2 else fu)[:, u % 2, (j % 2) * T:(j % 2 + 1) * T]
                        evacuate(g + j, e + j, dst, ACT.Silu if j < 2 else ACT.Copy, i=i, body=12)

                def pair(u, tile, i=None):
                    n = 0 if i is None else i
                    act.wait_ge(f_mid, FU * k + u + 1 + n * 2)
                    pair_hi(fm[:, u % 2, :].rearrange("p (a t) -> p a t", a=2), u0 + u, i, 2, tile, 12)

                a_tiles(g0, e0, 0)
                pair(0, g0)
                with act.Fori(0, (FU - 1) // 2) as i:
                    A(unused, ones[:, 0:1], ACT.Silu)
                    for v in range(2):
                        b = g0 + 4 + 6 * v
                        a_tiles(b, e0 + 4 + 4 * v, v + 1, i)
                        hi(b + 4 + 2, i, 12)
                        pair(v + 1, b, i)
                        hi(b + 5 + 2, i, 12)
                b = g0 + FFN_TILES - 2
                hi(b + 2)
                hi(b + 3)

            ffn(0)
            norm(1)

            g0, e0 = START["att"], EV["att"]
            act.wait_ge(b_vec, 1)
            for g in range(G3):
                A(bv[0:AH, g, :], ps_a[0:AH, g, 0:384], ACT.Copy).then_inc(b_vecc, 1)
            run(g0, e0, 24, lambda n: one(aq, n), scale=HD ** -0.5, back=True)
            run(g0 + 24, e0 + 24, 24, lambda n: one(ak, n))
            values(g0 + 48, e0 + 48, 24)

            def exps1(h):
                s = h % 2
                act.wait_ge(a_m1, h + 1)
                A(pr[:, s, 0:768], pr[:, s, 0:768], ACT.Exp, bias=ast[:, s, 2:3],
                  accum_out=ast[:, s, 4:5]).then_inc(act_step, 1)
                steps[0] += 1

            def exps0(h):
                s = h % 2
                act.wait_ge(a_m, h + 1)
                A(pr[:, s, 768:1152], pr[:, s, 768:1152], ACT.Exp, bias=ast[:, s, 3:4],
                  accum_out=ast[:, s, 5:6]).then_inc(a_e, 1)

            def turned(h):
                s = h % 2
                act.wait_ge(a_t, h + 1)
                A(pt_s[:, 1024:1152], ps[:, 3 * s + 2, P:T], ACT.Copy).then_inc(a_tc, 1)
                A(pt_s[:, 0:512], ps[:, 6, :], ACT.Copy).then_inc(a_tc, 1)
                A(pt_s[:, 512:1024], ps[:, 7, :], ACT.Copy).then_inc(a_tc, 1)

            def outs(h):
                s, r = h % 2, 64 * (h % 2)
                act.wait_ge(a_o, h + 1)
                A(ao[r:r + HD, h // 2, :].rearrange("p (c t) -> p c t", c=NC_T),
                  ps[r:r + HD, 3 * s + 2, T:2 * T].rearrange("p (c t) -> p c t", c=NC_T)[:, :, ::-1],
                  ACT.Copy).then_inc(a_oc, 1)
                if s:
                    act.wait_ge(a_oc, h + 1)
                    A(xh[:, h // 2, :], ao[:, h // 2, :], ACT.Copy).then_inc(a_hi, 1)

            exps1(0)
            exps0(0)
            for h in range(AH):
                turned(h)
                if h + 1 < AH:
                    exps1(h + 1)
                    exps0(h + 1)
                outs(h)
            run(g0 + 72, e0 + 72, 8, lambda n: one(mix, n))
            norm(2)
            ffn(1)
            norm(3)

            norm(4)
            for k in range(2):
                g0, e0 = START[f"b{k}"], EV[f"b{k}"]
                dsts = [(fz[0:H2, 0, :], ACT.Identity, {"bias": vec[0:H2, V_BF + k:V_BF + k + 1], "rows": H2})]
                dsts += [(ca[:, j, :], ACT.Copy, {}) for j in range(2)]
                dsts += [(cg[:, j, :], ACT.Sigmoid, {}) for j in range(2)]
                dsts += [(xrp[:, j, 4:4 + T], ACT.Copy, {}) for j in range(2)]
                dsts += [(gg[:, j, :], ACT.Gelu_apprx_tanh, {}) for j in range(2)]
                dsts += [(q2[:, j, :], ACT.Copy, {"scale": HD ** -0.5}) for j in range(4)]
                dsts += [(k2[:, j, :], ACT.Copy, {}) for j in range(4)]
                dsts += [(vT[:, j % 2, :], ACT.Copy, {}) for j in range(4)]
                for j, (dst, func, kw) in enumerate(dsts):
                    hi(g0 + j + 2)
                    evacuate(g0 + j, e0 + j, dst, func, **kw)
                    if j == 9:
                        act.wait_ge(z_abs, k + 1)
                        link(A(fz[0:H2, 2, :], fz[0:H2, 1, :], ACT.Exp, scale=-1.0))
                        A(fz[0:H2, 3, :], fz[0:H2, 2, :], ACT.Ln, bias=ones[0:H2, 0:1]).then_inc(z_ln, 1)
                        act.wait_ge(sp_abs, k + 1)
                        A(spw[:, 2, :], spw[:, 1, :], ACT.Exp, scale=-1.0).then_inc(sp_exp, 1)
                    if j == 15:
                        act.wait_ge(rg_mm, k + 1)
                        for b in range(2):
                            c = 2 * k + b
                            A(rr[:, b, :], ps_a[:, 2, b * T:(b + 1) * T], ACT.Sigmoid,
                              bias=vec[:, V_BR + c:V_BR + c + 1]).then_inc(rg_sig, 1)
                            A(ri[:, b, :], ps_a[:, 3, b * T:(b + 1) * T], ACT.Sigmoid,
                              bias=vec[:, V_BI + c:V_BI + c + 1]).then_inc(rg_sig, 1)
                def exps2(h):
                    s = h % 2
                    act.wait_ge(a_m, AH + H2 * k + h + 1)
                    if h >= 2:
                        act.wait_ge(a_t, AH + H2 * k + h - 1)
                    A(p2[:, s, 0:256], ps[:, s, 0:256], ACT.Exp, bias=st2[:, s, 2:3],
                      accum_out=st2[:, s, 4:5]).then_inc(act_step, 1)
                    A(p2[:, s, 256:384], ps[:, s, 256:384], ACT.Exp, bias=st2[:, s, 3:4],
                      accum_out=st2[:, s, 5:6]).then_inc(a_e, 1)
                    steps[0] += 1

                exps2(0)
                for h in range(H2):
                    s, r = h % 2, 64 * (h % 2)
                    act.wait_ge(a_t, AH + H2 * k + h + 1)
                    A(p2T, ps_x[:, 0, 0:384], ACT.Copy).then_inc(a_tc, 1)
                    if h + 1 < H2:
                        exps2(h + 1)
                    if h == 3:
                        act.wait_ge(rg_la, k + 1)
                        A(aa, la, ACT.Exp).then_inc(rg_exp, 1)
                        A(th, la, ACT.Tanh, scale=-1.0).then_inc(rg_exp, 1)
                    elif h == 5:
                        act.wait_ge(cv_cen, k + 1)
                        A(csq, cy, ACT.Square).then_inc(cv_sq, 1)
                    elif h == 6:
                        act.wait_ge(cv_var, k + 1)
                        A(cstd[:, 0, :], ps_t[:, 1, 0:T], ACT.Sqrt, bias=vec[:, V_EPS2:V_EPS2 + 1],
                          scale=1.0 / 256).then_inc(cv_std, 1)
                        act.wait_ge(rg_m2, k + 1)
                        A(mu, mu, ACT.Sqrt).then_inc(rg_mult, 1)
                    act.wait_ge(a_o, AH + H2 * k + h + 1)
                    A(o2[r:r + HD, h // 2, :], ps_x[r:r + HD, 1, 0:T], ACT.Copy).then_inc(a_oc, 1)
                    if s:
                        act.wait_ge(a_oc, AH + H2 * k + h + 1)
                        A(xh[:, h // 2, :], o2[:, h // 2, :], ACT.Copy).then_inc(a_hi, 1)
                act.wait_ge(cv_n, k + 1)
                for b in range(2):
                    c = 2 * k + b
                    A(o2[:, 4 + b, :], cy[:, b, :], ACT.Silu, scale=vec[:, V_CG + c:V_CG + c + 1],
                      bias=vec[:, V_CN + c:V_CN + c + 1]).then_inc(cv_o, 1)
                act.wait_ge(cv_o, 2 * k + 2)
                A(xh[:, 4:6, :], o2[:, 4:6, :], ACT.Copy).then_inc(a_hi, 1)
                act.wait_ge(rg_o, k + 1)
                A(xh[:, 6:8, :], o2[:, 6:8, :], ACT.Copy).then_inc(a_hi, 1)
                run(g0 + 21, e0 + 21, 8, lambda n: one(mix, n))
                norm(5 + 2 * k)

                run(g0 + 29, e0 + 29, 16, lambda n: one(pq, n))
                for c in range(NC_T):
                    for j in range(4):
                        act.wait_ge(p_s, 4 * (2 * k + c) + j + 1)
                        A(sc[:, 8 * c + 2 * j:8 * c + 2 * j + 2, :, :],
                          ps_a[:, j, :].rearrange("p (a b c) -> p a b c", a=2, b=2), ACT.Copy).then_inc(p_sc, 1)
                gu, eu = g0 + 45, e0 + 45
                run(gu, eu, 96, lambda n: one(hid, n), func=ACT.Gelu_apprx_tanh)
                hi(gu + 98)
                evacuate(gu + 96, eu + 96, hid[:, 96, :], ACT.Gelu_apprx_tanh)
                act.wait_ge(pick_step, 8 * PICK_STEPS * (k + 1))
                A(ge, ge, ACT.Exp).then_inc(p_exp, 1)
                for j in range(97, 100):
                    hi(gu + j + 2)
                    evacuate(gu + j, eu + j, hid[:, j, :], ACT.Gelu_apprx_tanh)
                act.wait_ge(p_t, k + 1)
                for c in range(NC_T):
                    A(pickT[:, 0:3, c * P:(c + 1) * P], ps_x[:, c, 0:384].rearrange("p (a b) -> p a b", a=3),
                      ACT.Copy).then_inc(p_tc, 1)
                run(gu + 100, eu + 100, 28, lambda n: one(hid, n + 100), func=ACT.Gelu_apprx_tanh)


                def gate_rows(t, s):
                    for j in range(4):
                        ins = A(gated[s][:, j, :], oh[s][:, j, :].bitcast(F32), ACT.Copy,
                                scale=gT[:, bass.ds(t + j, 1)])
                    ins.then_inc(g_gated, 1)

                act.wait_ge(p_tc, 2 * (k + 1))
                for n in range(4):
                    act.wait_ge(g_hot, 64 * k + n + 1)
                    gate_rows(n * 4, n)
                with act.Fori(0, 15) as i:
                    for s in range(4):
                        act.wait_ge(g_hot, i * 4 + 64 * k + 5 + s)
                        act.wait_ge(g_mm, i * 4 + 64 * k + 1 + s)
                        gate_rows(i * 16 + 16 + 4 * s, s)
                act.wait_ge(g_mul, 64 * (k + 1))
                gv, u0 = g0 + 173, PAIR[f"b{k}"]
                pair_hi(hid[:, 0:2, :], u0)
                pair_hi(hid[:, 2:4, :], u0 + 1)
                with act.Fori(0, 31) as i:
                    for j in range(4):
                        hi(gv + j + 2, i, 4)
                        if j % 2:
                            u = j // 2 + 2
                            pair_hi(hid[:, bass.ds(i * 4 + 2 * u, 2), :], u0 + u, i, 2, gv + j + 1, 4)
                for j in range(124, 128):
                    hi(gv + j + 2)
                norm(6 + 2 * k)
            for j in range(4):
                act.wait_ge(o_turned, j + 1)
                A(o_rows[:, j // 2, (j % 2) * 512:(j % 2 + 1) * 512], ps_a[:, j, :], ACT.Copy).then_inc(o_copied, 1)

        @block.vector
        def _(dve):
            V = nc.vector
            steps = [0]

            def link(ins, wait=True):
                steps[0] = steps[0] + 1
                ins.then_inc(dve_step, 1)
                if wait:
                    dve.wait_ge(dve_step, steps[0])

            def lo(b, i=None, body=0):
                if i is None and b >= TILES:
                    return
                n = 0 if i is None else i
                dve.wait_ge(w_hi, b + 1 + n * body)
                V.tensor_tensor(wl[b % 2][:, :, :], raw[:, b % 4, :].rearrange("p (a b) -> p a b", a=DB),
                                wh[b % 2][:, :, :].bitcast(F32), ALU.subtract).then_inc(w_lo, 1)

            def run(g0, count):
                with dve.Fori(0, count // 4) as i:
                    for j in range(4):
                        lo(g0 + j + 2, i, 4)

            def pair_lo(src, u, i=None, step=0):
                n = 0 if i is None else i
                dve.wait_ge(m_hi, u + 1 + n * step)
                s = 2 * (u % 2)
                V.tensor_tensor(ml[:, s:s + 2, :], src, mh[:, s:s + 2, :].bitcast(F32), ALU.subtract) \
                    .then_inc(m_lo, 1)

            def norm(k):
                kind, source, gain, bias = NORMS[k]
                if source == "acc":
                    dve.wait_ge(mm_done, acc_tiles(k))
                elif source == "mix":
                    dve.wait_ge(evac, {2: EV["att"] + 80, 5: EV["b0"] + 29, 7: EV["b1"] + 29}[k])
                def pair_sum(g, dst, src, done):
                    V.tensor_tensor(dst[:, g, :], src[:, 2 * g, :], src[:, 2 * g + 1, :], ALU.add).then_inc(done, 1)

                def square_pair(g):
                    dve.wait_ge(n_sq, 4 * k + g + 1)
                    pair_sum(g, pair_sq, sq, n_psq)

                src = acc if source == "acc" else mix
                for g in range(4):
                    b = slice(2 * g, 2 * g + 2)
                    if source is not None:
                        V.scalar_tensor_tensor(out=xT[:, b, :], in0=xT[:, b, :],
                                               scalar=ALPHA if kind == "ln" else 1.0, in1=src[:, b, :],
                                               op0=ALU.mult, op1=ALU.add).then_inc(n_res, 1)
                    if kind == "ln":
                        dve.wait_ge(n_res, res_before[k] + g + 1)
                        pair_sum(g, pair_x, xT, n_px)
                    elif g:
                        square_pair(g - 1)
                if kind == "ln":
                    dve.wait_ge(n_mean, ln_before[k] + 1)
                    for g in range(4):
                        b = slice(2 * g, 2 * g + 2)
                        V.scalar_tensor_tensor(out=xT[:, b, :],
                                               in0=ps_x[:, 0, 0:T].unsqueeze(1).to_broadcast([P, 2, T]),
                                               scalar=-1.0 / D, in1=xT[:, b, :], op0=ALU.mult, op1=ALU.add) \
                            .then_inc(n_cen, 1)
                        if g:
                            square_pair(g - 1)
                square_pair(3)
                dve.wait_ge(n_std, k + 1)
                link(V.reciprocal(rstd, std))

                def rest(g):
                    dve.wait_ge(n_hi, split_before[k] + g + 1)
                    b = slice(2 * g, 2 * g + 2)
                    if kind == "ln":
                        for c in (2 * g, 2 * g + 1):
                            ins = V.scalar_tensor_tensor(out=xl[:, c, :], in0=yn[:, c, :],
                                                         scalar=vec[:, bias + c:bias + c + 1],
                                                         in1=xh[:, c, :].bitcast(F32),
                                                         op0=ALU.add, op1=ALU.subtract)
                    else:
                        ins = V.tensor_tensor(xl[:, b, :], yn[:, b, :], xh[:, b, :].bitcast(F32), ALU.subtract)
                    ins.then_inc(n_lo, 1)

                split = k not in (3, 8)
                for g in range(4):
                    for b in (2 * g, 2 * g + 1):
                        ins = V.scalar_tensor_tensor(out=yn[:, b, :], in0=xT[:, b, :],
                                                     scalar=vec[:, gain + b:gain + b + 1], in1=rstd,
                                                     op0=ALU.mult, op1=ALU.mult)
                        if k == 3:
                            link(ins)
                            ins = V.tensor_scalar(xT[:, b, :], yn[:, b, :], vec[:, bias + b:bias + b + 1], None,
                                                  ALU.add)
                    ins.then_inc(n_y, 1)
                    if split and g:
                        rest(g - 1)
                if split:
                    rest(3)
                dve.wait_ge(n_y, 4 * (k + 1))
                if kind == "ln" and split:
                    for b in range(DB):
                        link(V.tensor_scalar(xT[:, b, :], yn[:, b, :], vec[:, bias + b:bias + b + 1], None,
                                             ALU.add), wait=(b == DB - 1))

            lo(0)
            lo(1)
            dve.wait_ge(x_hi, 1)
            V.tensor_tensor(xl[:, :, :], xT[:, :, :], xh[:, :, :].bitcast(F32), ALU.subtract).then_inc(x_lo, 1)

            def values(g0, v0, count, dst):
                def copy(n, j, i=None):
                    dve.wait_ge(v_turned, n + 1 + (0 if i is None else i * 4))
                    m = j if i is None else i * 4 + j
                    V.tensor_copy(dst[:, :, bass.ds(m * P, P)],
                                  ps_x[:, n % 2, 0:T].rearrange("p (c n) -> p c n", c=2)).then_inc(v_copied, 1)

                for j in range(4):
                    lo(g0 + j + 2)
                    if j:
                        copy(v0 + j - 1, j - 1)
                if count > 4:
                    with dve.Fori(0, count // 4 - 1) as i:
                        for j in range(4):
                            lo(g0 + 4 + j + 2, i, 4)
                            copy(v0 + 3 + j, 3 + j, i)
                copy(v0 + count - 1, count - 1)

            run(0, 16)
            values(RET_V, 0, 16, vt)
            dve.wait_ge(retc_in, 16)
            dve.wait_ge(evac, 16)
            cos, sin, t1, t2 = (v.rearrange("p (a t) -> p a t", a=2) for v in (
                rc[:, R_COS:R_COS + 512], rc[:, R_SIN:R_SIN + 512], rt[:, 0, :], rt[:, 1, :]))
            for j in range(16):
                b = j // 2
                pair = qk[:, 2 * b:2 * b + 2, :]
                lo(RET_G + j + 2)
                if j % 2 == 0:
                    dve.wait_ge(rope_mm, b + 1)
                    link(V.tensor_tensor(t1, pair, cos, ALU.mult), wait=False)
                    link(V.tensor_tensor(t2, ps_x[:, b % 2, :].rearrange("p (a t) -> p a t", a=2), sin, ALU.mult))
                else:
                    V.tensor_tensor(pair, t1, t2, ALU.add).then_inc(rope_done, 1)
                    dve.wait_ge(rope_done, b + 1)

            def ret_decay(h):
                dve.wait_ge(r_s, h + 1)
                if h >= 2:
                    dve.wait_ge(r_y, h - 1)
                V.tensor_tensor(sd[:, h % 2, :], ps_x[:, h % 2, 0:384], rc[:, R_D + 384 * h:R_D + 384 * (h + 1)],
                                ALU.mult).then_inc(r_sd, 1)

            def ret_centre(h):
                yh = ry[:, 4 * h:4 * h + 4, :]
                dve.wait_ge(r_mean, h + 1)
                V.scalar_tensor_tensor(out=yh, in0=ps_t[:, 0, 0:T].unsqueeze(1).to_broadcast([P, 4, T]),
                                       scalar=-1.0 / RV, in1=yh, op0=ALU.mult, op1=ALU.add).then_inc(r_cen, 1)

            for h in range(3):
                ret_decay(h)
            ret_centre(0)
            ret_decay(3)
            for h in range(RH):
                if h + 1 < RH:
                    ret_centre(h + 1)
                yh = ry[:, 4 * h:4 * h + 4, :]
                dve.wait_ge(r_std, h + 1)
                link(V.reciprocal(rstat[:, h % 2, 1, :], rstat[:, h % 2, 0, :]))
                link(V.tensor_tensor(yh, yh, rstat[:, h % 2, 1, :].unsqueeze(1).to_broadcast([P, 4, T]), ALU.mult))
                V.tensor_tensor(yh, yh, sg[:, 4 * h:4 * h + 4, :], ALU.mult).then_inc(r_out, 1)
            dve.wait_ge(r_out, RH)
            pair_lo(ry[:, 0:2, :], 0)
            pair_lo(ry[:, 2:4, :], 1)
            with dve.Fori(0, 3) as i:
                for j in range(4):
                    lo(RET_O + j + 2, i, 4)
                    if j % 2:
                        u = j // 2 + 2
                        pair_lo(ry[:, bass.ds(i * 4 + 2 * u, 2), :], u, i, 2)
            for j in range(12, 16):
                lo(RET_O + j + 2)
            norm(0)

            def ffn(k):
                name = f"ffn{k}"
                g0, e0, u0 = START[name], EV[name], PAIR[name]

                def mid(u, e, i=None):
                    n = 0 if i is None else i
                    dve.wait_ge(evac, e + n * 8)
                    V.tensor_tensor(fm[:, u % 2, :], fg[:, u % 2, :], fu[:, u % 2, :], ALU.mult).then_inc(f_mid, 1)

                def rest(u, i=None):
                    pair_lo(fm[:, u % 2, :].rearrange("p (a t) -> p a t", a=2), u0 + u, i, 2)

                for j in range(4):
                    lo(g0 + j + 2)
                mid(0, e0 + 4)
                rest(0)
                with dve.Fori(0, (FU - 1) // 2) as i:
                    for v in range(2):
                        b = g0 + 4 + 6 * v
                        for j in range(4):
                            lo(b + j + 2, i, 12)
                        mid(v + 1, e0 + 8 + 4 * v, i)
                        lo(b + 4 + 2, i, 12)
                        rest(v + 1, i)
                        lo(b + 5 + 2, i, 12)
                lo(g0 + FFN_TILES)
                lo(g0 + FFN_TILES + 1)

            ffn(0)
            norm(1)

            g0, e0 = START["att"], EV["att"]
            run(g0, 48)
            values(g0 + 48, 16, 24, av)

            def softmax_max(n, s, st, views):
                dve.wait_ge(a_s, n + 1)
                for c, v in enumerate(views):
                    link(V.tensor_reduce(st[:, s, c:c + 1], v, AX, ALU.max), wait=(c == 1))
                V.tensor_scalar(st[:, s, 2:4], st[:, s, 0:2], -1.0, None, ALU.mult).then_inc(a_m, 1)

            def softmax_scale(n, s, st, probs):
                dve.wait_ge(a_e, n + 1)
                link(V.reciprocal(st[:, s, 6:8], st[:, s, 4:6]))
                link(V.tensor_scalar(probs[0], probs[0], st[:, s, 6:7], None, ALU.mult), wait=False)
                V.tensor_scalar(probs[1], probs[1], st[:, s, 7:8], None, ALU.mult).then_inc(a_p, 1)

            def att_max(h, c):
                s = h % 2
                flat = ps[:, 3 * s:3 * s + 3, :].rearrange("p a b -> p (a b)")
                dve.wait_ge(a_s1 if c else a_s, h + 1)
                if c:
                    dve.wait_ge(b_in[s], 16 * (h // 2 + 1))
                    if h >= 2:
                        dve.wait_ge(a_t, h - 1)
                first, end, w = (0, 768, T) if c else (768, 1152, P)
                part = pr[:, s, first:end]
                ins = V.tensor_tensor(part.rearrange("p (g j) -> p g j", g=G3),
                                      flat[:, first:end].rearrange("p (g j) -> p g j", g=G3),
                                      bs[:, s, :, T - w:T], ALU.add)
                if c:
                    link(ins)
                else:
                    ins.then_inc(a_b, 1)
                    dve.wait_ge(a_b, h + 1)
                link(V.tensor_reduce(ast[:, s, 1 - c:2 - c], part, AX, ALU.max))
                V.tensor_scalar(ast[:, s, 3 - c:4 - c], ast[:, s, 1 - c:2 - c], -1.0, None, ALU.mult) \
                    .then_inc(a_m1 if c else a_m, 1)

            def att_scale(h):
                softmax_scale(h, h % 2, ast, (pr[:, h % 2, 0:768], pr[:, h % 2, 768:1152]))

            def mixed_rest(src, count, first, end):
                dve.wait_ge(a_hi, count)
                V.tensor_tensor(xl[:, first:end, :], src[:, first:end, :], xh[:, first:end, :].bitcast(F32),
                                ALU.subtract).then_inc(a_lo, 1)

            att_max(0, 1)
            att_max(0, 0)
            att_max(1, 1)
            att_scale(0)
            for h in range(AH):
                if h + 1 < AH:
                    att_max(h + 1, 0)
                    att_scale(h + 1)
                if h + 2 < AH:
                    att_max(h + 2, 1)
                if h % 2 == 0 and h:
                    mixed_rest(ao, h // 2, h // 2 - 1, h // 2)
            mixed_rest(ao, DB, DB - 1, DB)
            run(g0 + 72, 8)
            norm(2)
            ffn(1)
            norm(3)

            norm(4)
            for k in range(2):
                g0, e0 = START[f"b{k}"], EV[f"b{k}"]
                link(V.memset(cpad[:, :, 0:32], 0.0), wait=False)
                link(V.memset(xrp[:, :, 0:4], 0.0), wait=False)
                for j in range(2):
                    lo(g0 + j + 2)
                dve.wait_ge(evac, e0 + 1)
                z = [fz[0:H2, j, :] for j in range(6)]
                link(V.tensor_scalar(z[4], z[0], -1.0, None, ALU.mult))
                V.tensor_tensor(z[1], z[0], z[4], ALU.max).then_inc(z_abs, 1)
                lo(g0 + 4)
                link(V.tensor_scalar(z[0], z[0], 0.0, None, ALU.min))
                lam = vec[:, V_LAM + 2 * k:V_LAM + 2 * k + 2]
                link(V.tensor_scalar(spw[:, 0, :], lam, -1.0, None, ALU.mult))
                V.tensor_tensor(spw[:, 1, :], spw[:, 0, :], lam, ALU.max).then_inc(sp_abs, 1)
                for j in range(3, 7):
                    lo(g0 + j + 2)

                def short_taps(t):
                    for b in range(2):
                        w = V_RW + (2 * k + b) * RK + t
                        src = xrp[:, b, t + 1:t + 1 + T]
                        if t == 0:
                            c = V_RB + 2 * k + b
                            ins = V.tensor_scalar(xc[:, b, :], src, vec[:, w:w + 1], vec[:, c:c + 1],
                                                  ALU.mult, ALU.add)
                        else:
                            ins = V.scalar_tensor_tensor(out=xc[:, b, :], in0=src, scalar=vec[:, w:w + 1],
                                                         in1=xc[:, b, :], op0=ALU.mult, op1=ALU.add)
                        if t == RK - 1 and b == 1:
                            ins.then_inc(xc_done, 1)
                        else:
                            link(ins, wait=(b == 1))

                def taps(first, end):
                    for t in range(first, end):
                        for b in range(2):
                            w = V_CW + (2 * k + b) * CK + t
                            src = cpad[:, b, t + 2:t + 2 + T]
                            if t == 0:
                                c = V_CB + 2 * k + b
                                ins = V.tensor_scalar(cy[:, b, :], src, vec[:, w:w + 1], vec[:, c:c + 1],
                                                      ALU.mult, ALU.add)
                            else:
                                ins = V.scalar_tensor_tensor(out=cy[:, b, :], in0=src, scalar=vec[:, w:w + 1],
                                                             in1=cy[:, b, :], op0=ALU.mult, op1=ALU.add)
                            if t == CK - 1 and b == 1:
                                ins.then_inc(cv_y, 1)
                            else:
                                link(ins, wait=(b == 1))

                dve.wait_ge(evac, e0 + 7)
                short_taps(0)
                short_taps(1)
                lo(g0 + 9)
                short_taps(2)
                short_taps(3)
                lo(g0 + 10)
                link(V.tensor_tensor(cpad[:, :, 32:32 + T], ca, cg, ALU.mult))
                taps(0, 1)
                lo(g0 + 11)
                taps(1, 3)
                lo(g0 + 12)
                taps(3, 4)
                dve.wait_ge(z_ln, k + 1)
                link(V.tensor_tensor(z[0], z[0], z[3], ALU.subtract))
                link(V.memset(z[2], 1.0))
                lo(g0 + 13)
                link(V.tensor_tensor_scan(z[4], z[2], z[0], 0.0, ALU.mult, ALU.add))
                V.tensor_scalar(z[5], z[4], -1.0, None, ALU.mult).then_inc(cum_done, 1)
                dve.wait_ge(sp_exp, k + 1)
                link(V.tensor_scalar(spw[:, 3, :], spw[:, 2, :], 2.0, None, ALU.add))
                link(V.reciprocal(spw[:, 3, :], spw[:, 3, :]))
                link(V.tensor_tensor(spw[:, 3, :], spw[:, 3, :], spw[:, 2, :], ALU.mult))
                link(V.tensor_tensor(spw[:, 4, :], spw[:, 3, :], spw[:, 3, :], ALU.mult))
                lo(g0 + 14)
                link(V.memset(spw[:, 5, :], 1.0 / 19))
                for n in range(17, 0, -2):
                    link(V.tensor_tensor(spw[:, 5, :], spw[:, 5, :], spw[:, 4, :], ALU.mult))
                    link(V.tensor_scalar(spw[:, 5, :], spw[:, 5, :], 1.0 / n, None, ALU.add))
                lo(g0 + 15)
                link(V.tensor_tensor(spw[:, 5, :], spw[:, 5, :], spw[:, 3, :], ALU.mult))
                link(V.tensor_scalar(spw[:, 0, :], spw[:, 0, :], 0.0, -RG_C, ALU.max, ALU.mult))
                link(V.scalar_tensor_tensor(out=spw[:, 6, :], in0=spw[:, 5, :], scalar=-2.0 * RG_C,
                                            in1=spw[:, 0, :], op0=ALU.mult, op1=ALU.add))
                taps(4, 5)
                lo(g0 + 16)
                taps(5, 7)
                lo(g0 + 17)
                taps(7, 9)
                lo(g0 + 18)
                taps(9, 11)
                values(g0 + 17, 40 + 4 * k, 4, v2)
                def att2_max(h):
                    s = h % 2
                    softmax_max(AH + H2 * k + h, s, st2, (ps[:, s, 0:256], ps[:, s, 256:384]))

                def att2_scale(h):
                    softmax_scale(AH + H2 * k + h, h % 2, st2, (p2[:, h % 2, 0:256], p2[:, h % 2, 256:384]))

                att2_max(0)
                att2_max(1)
                att2_scale(0)
                for h in range(H2):
                    if h < 4:
                        taps(11 + 5 * h, 16 + 5 * h)
                    if h == 2:
                        dve.wait_ge(rg_sig, 4 * (k + 1))
                        link(V.tensor_tensor(la, rr, spw[:, 6, :].unsqueeze(2).to_broadcast([P, 2, T]), ALU.mult),
                             wait=False)
                        V.tensor_tensor(bt, ri, xc, ALU.mult).then_inc(rg_la, 1)
                    elif h == 4:
                        dve.wait_ge(cv_mean, k + 1)
                        V.scalar_tensor_tensor(out=cy, in0=ps_t[:, 0, 0:T].unsqueeze(1).to_broadcast([P, 2, T]),
                                               scalar=-1.0 / 256, in1=cy, op0=ALU.mult, op1=ALU.add) \
                            .then_inc(cv_cen, 1)
                        dve.wait_ge(rg_exp, 2 * (k + 1))
                        link(V.tensor_scalar(mu, th, 1.0, None, ALU.add))
                        link(V.reciprocal(mu[:, 0, :], mu[:, 0, :]))
                    elif h == 5:
                        link(V.reciprocal(mu[:, 1, :], mu[:, 1, :]))
                        V.scalar_tensor_tensor(out=mu, in0=th, scalar=2.0, in1=mu, op0=ALU.mult, op1=ALU.mult) \
                            .then_inc(rg_m2, 1)
                    if h + 1 < H2:
                        att2_scale(h + 1)
                    if h + 2 < H2:
                        att2_max(h + 2)
                    if h % 2 == 0 and h:
                        mixed_rest(o2, DB + 6 * k + h // 2, h // 2 - 1, h // 2)
                dve.wait_ge(cv_std, k + 1)
                link(V.reciprocal(cstd[:, 1, :], cstd[:, 0, :]))
                V.tensor_tensor(cy, cy, cstd[:, 1, :].unsqueeze(1).to_broadcast([P, 2, T]), ALU.mult) \
                    .then_inc(cv_n, 1)
                dve.wait_ge(rg_mult, k + 1)
                link(V.tensor_tensor(bt, bt, mu, ALU.mult))
                for b in range(2):
                    link(V.tensor_tensor_scan(hs[:, b, :], aa[:, b, :], bt[:, b, :], 0.0, ALU.mult, ALU.add),
                         wait=(b == 1))
                V.tensor_tensor(o2[:, 6:8, :], hs, gg, ALU.mult).then_inc(rg_o, 1)
                mixed_rest(o2, DB + 6 * k + 4, 3, 4)
                mixed_rest(o2, DB + 6 * k + 5, 4, 6)
                mixed_rest(o2, DB + 6 * k + 6, 6, 8)
                run(g0 + 21, 8)
                norm(5 + 2 * k)

                run(g0 + 29, 16)
                gu = g0 + 45
                dve.wait_ge(p_sc, 8 * (k + 1))
                pick = [0]

                def count(ins):
                    pick[0] = pick[0] + 1
                    ins.then_inc(pick_step, 1)

                def so_far(i):
                    dve.wait_ge(pick_step, i * PICK_STEPS + (8 * PICK_STEPS * k + pick[0]))

                sides = [(a, s) for a in range(2) for s in range(2)]
                flat = cand.rearrange("p h a b -> p h (a b)")
                B4 = [P, 2, 16, 16]
                with dve.Fori(0, 8) as i:
                    def tile(j):
                        so_far(i)
                        lo(gu + j + 2, i, 12)

                    def rank_hot(s):
                        count(V.tensor_tensor(hot_out, crf[:, s, :, :].unsqueeze(3).to_broadcast(B4),
                                              iota16.unsqueeze(1).unsqueeze(1).to_broadcast(B4), ALU.is_equal))
                        so_far(i)

                    def onto_keys(s):
                        count(V.tensor_tensor(hot_out, hot, tf[:, :, s, :].unsqueeze(2).to_broadcast(B4), ALU.mult))
                        so_far(i)
                        count(V.tensor_reduce(ee[:, s, bass.ds(i * 2, 2), :], hot, AX, ALU.add))

                    count(V.tensor_copy(cur, sc[:, bass.ds(i * 2, 2), :, :]))
                    tile(0)
                    for a, s in sides:
                        count(V.max(tv[:, a, s, 0:8], cur[:, a, s, :]))
                    tile(1)
                    for a, s in sides:
                        count(V.max_index(ti[:, a, s, 0:8], tv[:, a, s, 0:8], cur[:, a, s, :]))
                    tile(2)
                    for a, s in sides:
                        count(V.match_replace(best[:, a, s, :], tv[:, a, s, 0:8], cur[:, a, s, :], LOWEST))
                    tile(3)
                    for a, s in sides:
                        count(V.max(tv[:, a, s, 8:16], best[:, a, s, :]))
                    tile(4)
                    count(V.tensor_tensor(cand, tv[:, :, 0, :].unsqueeze(3).to_broadcast(B4),
                                          tv[:, :, 1, :].unsqueeze(2).to_broadcast(B4), ALU.add))
                    for a, s in sides:
                        count(V.max_index(ti[:, a, s, 8:16], tv[:, a, s, 8:16], best[:, a, s, :]))
                    tile(5)
                    count(V.tensor_copy(tf, ti))
                    for a in range(2):
                        count(V.max(sv[:, a, 0:8], flat[:, a, :]))
                    tile(6)
                    for a in range(2):
                        count(V.max_index(ci[:, a, 0:8], sv[:, a, 0:8], flat[:, a, :]))
                        count(V.match_replace(cand2[:, a, :], sv[:, a, 0:8], flat[:, a, :], LOWEST))
                    tile(7)
                    for a in range(2):
                        count(V.max(sv[:, a, 8:16], cand2[:, a, :]))
                    tile(8)
                    for a in range(2):
                        count(V.max_index(ci[:, a, 8:16], sv[:, a, 8:16], cand2[:, a, :]))
                    count(V.tensor_tensor(ge[:, bass.ds(i * 2, 2), :], sv, sv[:, :, 0:1].to_broadcast([P, 2, 16]),
                                          ALU.subtract))
                    tile(9)
                    count(V.tensor_single_scalar(cr[:, 0, :, :], ci, 4, ALU.logical_shift_right))
                    count(V.tensor_single_scalar(cr[:, 1, :, :], ci, 15, ALU.bitwise_and))
                    so_far(i)
                    count(V.tensor_copy(crf, cr))
                    so_far(i)
                    rank_hot(0)
                    tile(10)
                    onto_keys(0)
                    tile(11)
                    rank_hot(1)
                    onto_keys(1)
                    so_far(i)
                    assert pick[0] == PICK_STEPS
                lo(gu + 98)
                lo(gu + 99)
                dve.wait_ge(p_exp, k + 1)
                link(V.tensor_reduce(gd[:, 0, :], ge, AX, ALU.add))
                link(V.reciprocal(gd[:, 1, :], gd[:, 0, :]))
                V.tensor_tensor(ge, ge, gd[:, 1, :].unsqueeze(2).to_broadcast([P, NC_T * H2, 16]), ALU.mult) \
                    .then_inc(p_e, 1)
                lo(gu + 100)
                lo(gu + 101)
                run(gu + 100, 28)
                dve.wait_ge(p_tc, 2 * (k + 1))
                dve.wait_ge(evac, e0 + 173)

                def onehots(t, s):
                    B = [P, 2, 4, P]
                    V.tensor_tensor(oh[s].rearrange("p (a b) n -> p a b n", a=2),
                                    iota.unsqueeze(1).unsqueeze(1).to_broadcast(B),
                                    pickT[:, 0:2, bass.ds(t, 4)].unsqueeze(3).to_broadcast(B),
                                    ALU.is_equal).then_inc(g_hot, 1)

                def weigh(t, s):
                    h = hid[:, :, bass.ds(t, 4)].rearrange("p m t -> p t m")
                    V.tensor_tensor(h, h, ps_a[:, s, :].rearrange("p (t m) -> p t m", t=4), ALU.mult) \
                        .then_inc(g_mul, 1)

                for n in range(4):
                    onehots(n * 4, n)
                with dve.Fori(0, 15) as i:
                    for s in range(4):
                        dve.wait_ge(g_mm, i * 4 + 64 * k + 1 + s)
                        weigh(i * 16 + 4 * s, s)
                        onehots(i * 16 + 16 + 4 * s, s)
                for s in range(4):
                    dve.wait_ge(g_mm, 64 * k + 61 + s)
                    weigh(240 + 4 * s, s)
                gv, u0 = g0 + 173, PAIR[f"b{k}"]
                pair_lo(hid[:, 0:2, :], u0)
                pair_lo(hid[:, 2:4, :], u0 + 1)
                with dve.Fori(0, 31) as i:
                    for j in range(4):
                        lo(gv + j + 2, i, 4)
                        if j % 2:
                            u = j // 2 + 2
                            pair_lo(hid[:, bass.ds(i * 4 + 2 * u, 2), :], u0 + u, i, 2)
                for j in range(124, 128):
                    lo(gv + j + 2)
                norm(6 + 2 * k)

        @block.tensor
        def _(pe):
            M = nc.tensor.matmul

            def passes(out_ap, parts_l, parts_r, first=True, last=True, skip=False):
                (lh, ll), (rh, rl) = parts_l, parts_r
                M(out_ap, lh, rh, start=first, stop=False, skip_group_check=skip)
                M(out_ap, lh, rl, start=False, stop=False, skip_group_check=skip)
                return M(out_ap, ll, rh, start=False, stop=last, skip_group_check=skip)

            def wait_tile(b, i, body):
                pe.wait_ge(w_lo, b + 1 + (0 if i is None else i * body))

            def wait_free(e, i, ebody):
                if e >= 2:
                    pe.wait_ge(evac, e - 1 + (0 if i is None else i * ebody))

            def tile_a(b, e, i=None, body=0, ebody=0, norm=None):
                wait_tile(b, i, body)
                wait_free(e, i, ebody)
                for c in range(DB):
                    if norm is not None and c % 2 == 0:
                        pe.wait_ge(n_lo, split_before[norm] + c // 2 + 1)
                    ins = passes(ps_t[:, e % 2, 0:T], (wh[b % 2][:, c, :], wl[b % 2][:, c, :]),
                                 (xh[:, c, :], xl[:, c, :]), c == 0, c == DB - 1)
                ins.then_inc(mm_done, 1)

            def tile_b(b, u, j, first=False, last=False, i=None, body=0, ustep=0):
                wait_tile(b, i, body)
                pe.wait_ge(m_lo, u + 1 + (0 if i is None else i * ustep))
                s = 2 * (u % 2) + j
                for c in range(DB):
                    ins = passes(acc[:, c, :], (wh[b % 2][:, c, :], wl[b % 2][:, c, :]),
                                 (mh[:, s, :], ml[:, s, :]), first and c % 2 == 0, last, skip=True)
                ins.then_inc(mm_done, 1)

            def run(tile, g0, e0, count):
                with pe.Fori(0, count // 4) as i:
                    for j in range(4):
                        tile(g0 + j, e0 + j, i, 4, 4)

            def values(g0, e0, v0, count):
                def turn(n, i=None):
                    e = e0 + n - v0
                    pe.wait_ge(evac, e + 1 + (0 if i is None else i * 4))
                    if n >= 2:
                        pe.wait_ge(v_copied, n - 1 + (0 if i is None else i * 4))
                    for c in range(NC_T):
                        ins = nc.tensor.transpose(ps_x[:, n % 2, c * P:(c + 1) * P],
                                                  vT[:, (n - v0) % 2, c * P:(c + 1) * P], ident)
                    ins.then_inc(v_turned, 1)

                for j in range(4):
                    tile_a(g0 + j, e0 + j)
                    if j:
                        turn(v0 + j - 1)
                if count > 4:
                    with pe.Fori(0, count // 4 - 1) as i:
                        for j in range(4):
                            tile_a(g0 + 4 + j, e0 + 4 + j, i, 4, 4)
                            turn(v0 + 3 + j, i)
                turn(v0 + count - 1)
                pe.wait_ge(v_copied, v0 + count)

            def norm(k):
                kind, source, gain, bias = NORMS[k]
                if kind == "ln":
                    for g in range(4):
                        pe.wait_ge(n_px, 4 * ln_before[k] + g + 1)
                        ins = M(ps_x[:, 0, 0:T], ones, pair_x[:, g, :], start=(g == 0), stop=(g == 3))
                    ins.then_inc(n_mean, 1)
                for g in range(4):
                    pe.wait_ge(n_psq, 4 * k + g + 1)
                    ins = M(ps_x[:, 1, 0:T], ones, pair_sq[:, g, :], start=(g == 0), stop=(g == 3))
                ins.then_inc(n_var, 1)

            pe.wait_ge(const_in, 32)
            pe.wait_ge(x_in_s, 16)
            for c in range(NC_T):
                for b in range(DB):
                    ins = nc.tensor.transpose(acc[:, b, c * P:(c + 1) * P], x_rows[:, c, b * P:(b + 1) * P], ident)
            ins.then_inc(x_turned, 1)
            pe.wait_ge(x_lo, 1)

            for j in range(4):
                tile_a(j, j)
            run(tile_a, 4, 4, 12)
            values(RET_V, RET_V, 0, 16)
            pe.wait_ge(retc_in, 16)
            for n in range(16):
                tile_a(RET_G + n, RET_G + n)
                if n % 2 == 0:
                    b = n // 2
                    if b >= 2:
                        pe.wait_ge(rope_done, b - 1)
                    for j in range(2):
                        ins = M(ps_x[:, b % 2, j * T:(j + 1) * T], rc[:, R_ROT:R_ROT + P], qk[:, 2 * b + j, :],
                                start=True, stop=True)
                    ins.then_inc(rope_mm, 1)
            pe.wait_ge(rope_done, 8)

            def ret_scores(h):
                if h >= 2:
                    pe.wait_ge(r_sd, h - 1)
                for j in range(2):
                    dst = ps_x[:, h % 2, 0:T] if j == 0 else ps_x[:, h % 2, T:T + P]
                    for b in range(2):
                        ins = M(dst, qk[:, 8 + 2 * h + b, j * P:(j + 1) * P], qk[:, 2 * h + b, j * P:T],
                                start=(b == 0), stop=(b == 1))
                ins.then_inc(r_s, 1)

            def ret_values(h):
                pe.wait_ge(r_sd, h + 1)
                if h >= 2:
                    pe.wait_ge(r_yc, h - 1)
                for b in range(4):
                    c0 = h * RV + b * P
                    dst = acc[:, 4 * (h % 2) + b, :]
                    M(dst, vt[:, 0, c0:c0 + P], sd[:, h % 2, 0:T], start=True, stop=False)
                    ins = M(dst[:, P:T], vt[:, 1, c0:c0 + P], sd[:, h % 2, T:T + P], start=False, stop=True)
                ins.then_inc(r_y, 1)

            def ret_mean(h):
                pe.wait_ge(r_yc, h + 1)
                if h:
                    pe.wait_ge(r_cen, h)
                for b in range(4):
                    ins = M(ps_t[:, 0, 0:T], ones, ry[:, 4 * h + b, :], start=(b == 0), stop=(b == 3))
                ins.then_inc(r_mean, 1)

            ret_scores(0)
            ret_scores(1)
            ret_values(0)
            ret_scores(2)
            ret_values(1)
            pe.wait_ge(evac, EV["ffn0"])
            ret_mean(0)
            ret_scores(3)
            for h in range(RH):
                if h + 2 < RH:
                    ret_values(h + 2)
                if h + 1 < RH:
                    ret_mean(h + 1)
                pe.wait_ge(r_sq, h + 1)
                if h:
                    pe.wait_ge(r_std, h)
                for b in range(4):
                    ins = M(ps_t[:, 1, 0:T], ones, rsq[:, b, :], start=(b == 0), stop=(b == 3))
                ins.then_inc(r_var, 1)
            tile_b(RET_O, 0, 0, first=True)
            tile_b(RET_O + 1, 0, 1)
            tile_b(RET_O + 2, 1, 0)
            tile_b(RET_O + 3, 1, 1)
            with pe.Fori(0, 3) as i:
                for j in range(4):
                    tile_b(RET_O + 4 + j, 2 + j // 2, j % 2, i=i, body=4, ustep=2)
            norm(0)

            def ffn(k):
                name = f"ffn{k}"
                g0, e0, u0 = START[name], EV[name], PAIR[name]
                for j in range(4):
                    tile_a(g0 + j, e0 + j, norm=2 * k if j == 0 else None)
                for v in range(2):
                    b = g0 + 4 + 6 * v
                    for j in range(4):
                        tile_a(b + j, e0 + 4 + 4 * v + j)
                    for j in range(2):
                        tile_b(b + 4 + j, u0 + v, j, first=(v == 0 and j == 0))
                with pe.Fori(0, (FU - 1) // 2 - 1) as i:
                    for v in range(2):
                        b = g0 + 16 + 6 * v
                        for j in range(4):
                            tile_a(b + j, e0 + 12 + 4 * v + j, i, 12, 8)
                        for j in range(2):
                            tile_b(b + 4 + j, u0 + 2 + v, j, i=i, body=12, ustep=2)
                for j in range(2):
                    tile_b(g0 + FFN_TILES - 2 + j, u0 + FU - 1, j)

            ffn(0)
            norm(1)

            g0, e0 = START["att"], EV["att"]
            pe.wait_ge(attc_in, 16)
            for g in range(G3):
                ins = M(ps_a[0:AH, g, 0:384], ac[0:33, G3 * 384 + g * AH:G3 * 384 + (g + 1) * AH],
                        ac[0:33, g * 384:(g + 1) * 384], start=True, stop=True)
            ins.then_inc(b_vec, 1)
            for j in range(4):
                tile_a(g0 + j, e0 + j, norm=1 if j == 0 else None)
            run(tile_a, g0 + 4, e0 + 4, 44)
            values(g0 + 48, e0 + 48, 16, 24)
            pe.wait_ge(evac, e0 + 72)
            pe.wait_ge(b_vecc, G3)

            def att_scores(h, groups):
                s, r, hp = h % 2, 64 * (h % 2), h // 2
                flat = ps[:, 3 * s:3 * s + 3, :].rearrange("p a b -> p (a b)")
                for g, c in groups:
                    w = T if c else P
                    o = g * T if c else 768 + g * P
                    m = 8 * g + hp
                    ins = M(flat[:, o:o + w], aq[r:r + HD, m, c * P:(c + 1) * P], ak[r:r + HD, m, 0:w],
                            start=True, stop=True)
                return ins

            EARLY, LATE = [(0, 1), (1, 1), (2, 1), (0, 0), (1, 0)], [(2, 0)]
            att_scores(0, EARLY).then_inc(a_s1, 1)
            att_scores(0, LATE).then_inc(a_s, 1)
            att_scores(1, EARLY).then_inc(a_s1, 1)
            for h in range(AH):
                s, r = h % 2, 64 * (h % 2)
                pe.wait_ge(a_p, h + 1)
                if h:
                    pe.wait_ge(a_tc, 3 * h)
                for g in range(G3):
                    dst = ps[:, 6 + g // 2, (g % 2) * T:(g % 2) * T + T]
                    nc.tensor.transpose(dst[:, 0:P], pr[:, s, 768 + g * P:768 + (g + 1) * P], ident)
                    nc.tensor.transpose(dst[:, P:T], pr[:, s, g * T:g * T + P], ident)
                for g in range(G3):
                    dst = ps[:, 7, T + g * P:T + (g + 1) * P] if g < 2 else ps[:, 3 * s + 2, P:T]
                    ins = nc.tensor.transpose(dst, pr[:, s, g * T + P:(g + 1) * T], ident)
                ins.then_inc(a_t, 1)
                if h + 1 < AH:
                    if h:
                        pe.wait_ge(a_oc, h)
                    att_scores(h + 1, LATE).then_inc(a_s, 1)
                if h + 2 < AH:
                    att_scores(h + 2, EARLY).then_inc(a_s1, 1)
                pe.wait_ge(a_tc, 3 * h + 3)
                dst = ps[r:r + HD, 3 * s + 2, T:2 * T]
                for g in range(G3):
                    c0 = g * D + h * HD
                    M(dst, av[:, 0, c0:c0 + HD], pt_s[:, g * T:(g + 1) * T], start=(g == 0), stop=False)
                for g in range(G3):
                    c0, o = g * D + h * HD, 768 + g * P
                    ins = M(dst[:, P:T], av[:, 1, c0:c0 + HD], pt_s[:, o:o + P], start=False, stop=(g == 2))
                ins.then_inc(a_o, 1)
            pe.wait_ge(a_lo, DB)
            run(tile_a, g0 + 72, e0 + 72, 8)
            norm(2)
            ffn(1)
            norm(3)

            norm(4)
            for k in range(2):
                g0, e0 = START[f"b{k}"], EV[f"b{k}"]
                for j in range(15):
                    tile_a(g0 + j, e0 + j, norm=4 + 2 * k if j == 0 else None)
                pe.wait_ge(xc_done, k + 1)
                pe.wait_ge(bd_in, 16 * (k + 1))
                for m in range(2):
                    for b in range(2):
                        ins = M(ps_a[:, 2 + m, b * T:(b + 1) * T], bd[:, m, b, :], xc[:, b, :], start=True, stop=True)
                ins.then_inc(rg_mm, 1)
                for j in range(15, 17):
                    tile_a(g0 + j, e0 + j)
                values(g0 + 17, e0 + 17, 40 + 4 * k, 4)
                pe.wait_ge(cum_done, k + 1)

                def att2_scores(h):
                    s, r, hp = h % 2, 64 * (h % 2), h // 2
                    if h >= 2:
                        pe.wait_ge(a_e, AH + H2 * k + h - 1)
                    one_h = ident[0:H2, h:h + 1]
                    for c in (1, 0):
                        w = T if c else P
                        o = 0 if c else T
                        dst = ps[:, s, o:o + w]
                        M(dst, q2[r:r + HD, hp, c * P:(c + 1) * P], k2[r:r + HD, hp, 0:w], start=True, stop=False)
                        M(dst, fz[0:H2, 4, c * P:(c + 1) * P], one_h.to_broadcast([H2, w]), start=False, stop=False)
                        M(dst, one_h.to_broadcast([H2, P]), fz[0:H2, 5, 0:w], start=False, stop=False)
                        ins = M(dst[:, w - P:w], ident, tri, start=False, stop=True)
                    ins.then_inc(a_s, 1)

                att2_scores(0)
                att2_scores(1)
                for h in range(H2):
                    s, r = h % 2, 64 * (h % 2)
                    n = AH + H2 * k + h
                    pe.wait_ge(a_p, n + 1)
                    if h:
                        pe.wait_ge(a_tc, 3 * AH + H2 * k + h)
                    nc.tensor.transpose(ps_x[:, 0, 0:P], p2[:, s, T:T + P], ident)
                    nc.tensor.transpose(ps_x[:, 0, P:T], p2[:, s, 0:P], ident)
                    nc.tensor.transpose(ps_x[:, 0, T:T + P], p2[:, s, P:T], ident).then_inc(a_t, 1)
                    if h + 2 < H2:
                        att2_scores(h + 2)
                    if h == 3:
                        pe.wait_ge(cv_y, k + 1)
                        for b in range(2):
                            ins = M(ps_t[:, 0, 0:T], ones, cy[:, b, :], start=(b == 0), stop=(b == 1))
                        ins.then_inc(cv_mean, 1)
                    elif h == 5:
                        pe.wait_ge(cv_sq, k + 1)
                        for b in range(2):
                            ins = M(ps_t[:, 1, 0:T], ones, csq[:, b, :], start=(b == 0), stop=(b == 1))
                        ins.then_inc(cv_var, 1)
                    pe.wait_ge(a_tc, 3 * AH + H2 * k + h + 1)
                    if h:
                        pe.wait_ge(a_oc, n)
                    dst = ps_x[r:r + HD, 1, 0:T]
                    M(dst, v2[:, 0, h * HD:(h + 1) * HD], p2T[:, 0:T], start=True, stop=False)
                    M(dst[:, P:T], v2[:, 1, h * HD:(h + 1) * HD], p2T[:, T:T + P], start=False, stop=True) \
                        .then_inc(a_o, 1)
                pe.wait_ge(a_lo, DB + 6 * (k + 1))
                run(tile_a, g0 + 21, e0 + 21, 8)
                norm(5 + 2 * k)

                for j in range(29, 33):
                    tile_a(g0 + j, e0 + j, norm=5 + 2 * k if j == 29 else None)
                run(tile_a, g0 + 33, e0 + 33, 12)
                pe.wait_ge(evac, e0 + 45)
                pe.wait_ge(k_in, 16 * (k + 1))
                for c in range(NC_T):
                    n = 2 * k + c
                    for j in range(4):
                        if c:
                            pe.wait_ge(p_sc, 4 * n + j - 3)
                        for h in (2 * j, 2 * j + 1):
                            for s in range(2):
                                o = (h % 2) * 256 + s * P
                                ins = M(ps_a[:, j, o:o + P], pq[:, 2 * h + s, c * P:(c + 1) * P],
                                        pk[:, s, h, :], start=True, stop=True)
                        ins.then_inc(p_s, 1)
                run(tile_a, g0 + 45, e0 + 45, 96)
                for j in range(96, 100):
                    tile_a(g0 + 45 + j, e0 + 45 + j)
                pe.wait_ge(p_e, k + 1)
                for c in range(NC_T):
                    for m, src in enumerate((ee[:, 0, :, :], ee[:, 1, :, :], ge)):
                        ins = nc.tensor.transpose(ps_x[:, c, m * P:(m + 1) * P],
                                                  src[:, 8 * c:8 * c + 8, :].rearrange("p h j -> p (h j)"), ident)
                ins.then_inc(p_t, 1)
                run(tile_a, g0 + 145, e0 + 145, 28)

                def gates(s):
                    for j in range(4):
                        ins = M(ps_a[:, s, j * P:(j + 1) * P], gated[s][:, j, :], oh[s][:, 4 + j, :].bitcast(F32),
                                start=True, stop=True)
                    ins.then_inc(g_mm, 1)

                pe.wait_ge(p_tc, 2 * (k + 1))
                for s in range(4):
                    pe.wait_ge(g_gated, 64 * k + s + 1)
                    gates(s)
                with pe.Fori(0, 15) as i:
                    for s in range(4):
                        pe.wait_ge(g_gated, i * 4 + 64 * k + 5 + s)
                        pe.wait_ge(g_mul, i * 4 + 64 * k + 1 + s)
                        gates(s)
                pe.wait_ge(g_mul, 64 * (k + 1))
                gv, u0 = g0 + 173, PAIR[f"b{k}"]
                for j in range(4):
                    tile_b(gv + j, u0 + j // 2, j % 2, first=(j == 0))
                with pe.Fori(0, 31) as i:
                    for j in range(4):
                        tile_b(gv + 4 + j, u0 + 2 + j // 2, j % 2, i=i, body=4, ustep=2)
                norm(6 + 2 * k)
            for c in range(NC_T):
                for b in range(DB):
                    pe.wait_ge(n_y, 32 + b // 2 + 1)
                    ins = nc.tensor.transpose(ps_a[:, 2 * c + b // 4, (b % 4) * P:(b % 4 + 1) * P],
                                              yn[:, b, c * P:(c + 1) * P], ident)
                    if b % 4 == 3:
                        ins.then_inc(o_turned, 1)


def constants():
    c = np.zeros((P, NCONST), np.float32)
    p = np.arange(P)
    c[:, C_ID:C_ID + P] = np.eye(P)
    c[:, C_ONE:C_ONE + P] = 1.0
    c[:, C_J:C_J + P] = np.eye(P)[::-1]
    c[:, C_MASK:C_MASK + P] = np.where(p[None, :] > p[:, None], MASKED, 0.0)
    c[:, C_IOTA:C_IOTA + P] = p
    c[:, C_I16:C_I16 + 16] = np.arange(16)
    return c


def retention_constants():
    c = np.zeros((P, NRET), np.float32)
    e, p, t = np.arange(0, P, 2), np.arange(P), np.arange(T)
    c[e + 1, R_ROT + e] = -1.0
    c[e, R_ROT + e + 1] = 1.0
    inv = np.float32(1.0) / (np.float32(10000.0) ** np.linspace(0.0, 1.0, RQ // 2, dtype=np.float32))
    ang = (t.astype(np.float32)[None, :] * inv[:, None]).astype(np.float32).astype(np.float64)
    pair = ((np.arange(2)[None, :] * P + p[:, None]) // 2)
    c[:, R_COS:R_COS + 512] = np.cos(ang)[pair].reshape(P, 512)
    c[:, R_SIN:R_SIN + 512] = np.sin(ang)[pair].reshape(P, 512)
    diff = np.concatenate([t, np.arange(P)])[None, :] - p[:, None]
    for h in range(RH):
        g = np.log1p(-(2.0 ** (-5.0 - h)))
        d = np.where(diff >= 0, np.exp(np.maximum(diff, 0) * g), 0.0) * RQ ** -0.5
        c[:, R_D + 384 * h:R_D + 384 * (h + 1)] = d
    return c


def bias_one_hots():
    c = np.zeros((33, G3, 384), np.float32)
    x = np.arange(384)
    delta = 255 - x
    half = BUCKETS // 2
    d = np.maximum(delta, 1).astype(np.float32)
    large = half + (np.log(d / half) / np.float32(np.log(MAXD / half)) * half).astype(np.int32)
    bucket = np.where(delta < half, delta, np.minimum(large, BUCKETS - 1))
    for g, (window, dil) in enumerate(PAIRS):
        ok = (delta >= 0) & (delta % dil == 0) & (delta // dil <= window // dil)
        c[bucket[ok], g, x[ok]] = 1.0
        c[32, g, ~ok] = MASKED
    return c.reshape(33, G3 * 384)


def kernel(**inputs):
    import concourse.bacc as bacc
    from concourse.bass_utils import run_bass_kernel_spmd

    a = {k: np.asarray(v) for k, v in inputs.items()}

    def cols(w):
        return w.reshape(DB, P, -1, P).transpose(2, 1, 0, 3).reshape(-1, P, TILE)

    stream = np.empty((TILES, P, TILE), np.float32)
    at = [0]

    def put(tiles):
        stream[at[0]:at[0] + len(tiles)] = tiles
        at[0] += len(tiles)

    def put_ffn(k):
        up = cols(a["ffn_w_up"][k])
        down = a["ffn_w_down"][k].reshape(-1, P, TILE)
        for u in range(FU + 1):
            if u < FU:
                put(up[2 * u:2 * u + 2])
                put(up[FF // P + 2 * u:FF // P + 2 * u + 2])
            if u:
                put(down[2 * u - 2:2 * u])

    w = a["ret_w_in"][0]
    put(cols(w))
    put(a["ret_w_out"][0].reshape(-1, P, TILE))
    put_ffn(0)
    put(cols(a["attn_w_in"][0]))
    put(cols(a["attn_w_out"][0]))
    put_ffn(1)
    for k in range(2):
        w = a["w_in_2"][k]
        forget = np.zeros((D, P), np.float32)
        forget[:, 0:H2] = w[:, 1536:1536 + H2]
        put(cols(forget))
        put(cols(w[:, 1536 + H2:]))
        put(cols(w[:, 0:1536]))
        put(cols(a["w_out_2"][k]))
        put(cols(a["peer_wq_2"][k]))
        put(a["peer_u_2"][k].reshape(NK, NK, DB, P).transpose(1, 3, 2, 0).reshape(NK, P, TILE))
        put(a["peer_v_2"][k].reshape(NK, NK, TILE).transpose(1, 0, 2))
    assert at[0] == TILES

    def blocks(v):
        return v.reshape(-1, P).T

    vecs = np.zeros((P, NVEC), np.float32)
    for c, v in ((V_LNG, a["ln_gain"]), (V_LNB, a["ln_bias"]), (V_N1, a["norm1_g_2"]), (V_N2, a["norm2_g_2"]),
                 (V_FIN, a["final_g_2"]), (V_CB, a["conv_dw_b_2"]), (V_CG, a["conv_ln_g_2"]),
                 (V_CN, a["conv_ln_b_2"]), (V_RB, a["rg_conv_b_2"]), (V_BR, a["rg_b_r_2"]),
                 (V_BI, a["rg_b_i_2"]), (V_LAM, a["rg_lambda_2"])):
        m = blocks(v)
        vecs[:, c:c + m.shape[1]] = m
    for c, v in ((V_CW, a["conv_dw_w_2"]), (V_RW, a["rg_conv_w_2"])):
        taps = v.shape[1]
        vecs[:, c:c + 4 * taps] = v.reshape(2, taps, 2, P).transpose(3, 0, 2, 1).reshape(P, 4 * taps)
    vecs[0:H2, V_BF:V_BF + 2] = a["b_forget_2"].T
    vecs[:, V_EPS1], vecs[:, V_EPS2] = LN_EPS, EPS2

    rg_w = np.zeros((2, P, 2, 2, P), np.float32)
    for m, name in enumerate(("rg_w_r_2", "rg_w_i_2")):
        for h in range(4):
            r = slice(64 * (h % 2), 64 * (h % 2) + 64)
            rg_w[:, r, m, h // 2, r] = a[name][:, h]
    keys = np.stack([a["peer_k1_2"], a["peer_k2_2"]], 1).transpose(0, 4, 1, 2, 3)
    att_c = np.zeros((33, NATT), np.float32)
    att_c[:, 0:G3 * 384] = bias_one_hots()
    att_c[0:32, G3 * 384:] = a["rel_bias"].T
    att_c[32, G3 * 384:] = 1.0

    arrays = {"stream": stream, "x": a["x"].reshape(T, D), "consts": constants(), "ret_c": retention_constants(),
              "att_c": att_c, "vecs": vecs, "rg_w": rg_w, "keys": keys}
    arrays = {k: np.ascontiguousarray(v, np.float32) for k, v in arrays.items()}
    nc = bacc.Bacc("TRN2", target_bir_lowering=False, num_devices=1)
    args = {k: nc.dram_tensor(k + "_dram", v.shape, F32, kind="ExternalInput").ap() for k, v in arrays.items()}
    scratch = nc.dram_tensor("bias_scratch", (G3, AH, 384), F32, kind="Internal").ap()
    out = nc.dram_tensor("out_dram", (T, D), F32, kind="ExternalOutput").ap()
    build(nc, args["stream"], args["x"], args["consts"], args["ret_c"], args["att_c"], args["vecs"],
          args["rg_w"], args["keys"], scratch, out)
    r = run_bass_kernel_spmd(nc, [{k + "_dram": v for k, v in arrays.items()}], core_ids=[0])
    return r.results[0]["out_dram"].reshape(1, T, D)
```
